# Optimizing a Trainium2 kernel written in Bass

```python
import math
import jax
import jax.numpy as jnp
from jax import lax
import numpy as np

D_MODEL = 1024
BATCH = 1
SEQ = 1024
DEPTH = 2

GRID_W = 64
CTX_LEN = 256
HEAD_DIM = 64

HY_CH = 256
HY_SHORT = 3
HY_BANDS = 16
HY_EMB = 1 + 2 * HY_BANDS
HY_FFN = 64
HY_DECAY_MIN = -math.log(1e-2) / 1.5
HY_DECAY_MAX = -math.log(1e-2) / 0.3
HY_FILTER_SCALE = 0.05

WA_HEADS = 4
WA_KV_HEADS = 2
WINDOW = 128
WA_BLOCK = 128

NA_HEADS = 4
NA_KR = 8
NA_KC = 16

GDN_HEADS = 4
GDN_CONV = 4
GDN_CHUNK = 64

HY_IN = 3 * HY_CH
WA_IN = (WA_HEADS + 2 * WA_KV_HEADS) * HEAD_DIM
NA_IN = 3 * NA_HEADS * HEAD_DIM
GDN_W = GDN_HEADS * HEAD_DIM
GDN_IN = 4 * GDN_W + 4 * GDN_HEADS
D_IN = HY_IN + WA_IN + NA_IN + GDN_IN
D_MIX = HY_CH + (WA_HEADS + NA_HEADS) * HEAD_DIM + GDN_W

N_EXPERTS = 32
TOP_K = 4
D_EXPERT = 256
D_SHARED = 256
ROUTED_SCALE = 2.5
MOE_BLOCK = 128

ROPE_BASE = 10000.0
EPS = 1e-6
NEG = -1e30

kernel_name = 'hymba_hybrid_dit_moe_block'

def rmsnorm(x, g):
    xf = x.astype(jnp.float32)
    y = xf * lax.rsqrt(jnp.mean(xf * xf, axis=-1, keepdims=True) + EPS)
    return (y * g.astype(jnp.float32)).astype(x.dtype)

def depthwise_conv(x, w, left):
    k = w.shape[0]
    length = x.shape[1]
    xp = jnp.pad(x, ((0, 0), (left, k - 1 - left), (0, 0)))
    out = xp[:, 0:length] * w[0]
    for i in range(1, k):
        out = out + xp[:, i:i + length] * w[i]
    return out

def axial_rope(x, row, col):
    quarter = HEAD_DIM // 4
    half = HEAD_DIM // 2
    inv_freq = ROPE_BASE ** (-jnp.arange(quarter, dtype=jnp.float32) / quarter)

    def rotate(xa, pos):
        ang = pos.astype(jnp.float32)[:, None] * inv_freq[None, :]
        cos = jnp.cos(ang)[None, :, None, :]
        sin = jnp.sin(ang)[None, :, None, :]
        x1, x2 = xa[..., :quarter], xa[..., quarter:]
        return jnp.concatenate([x1 * cos - x2 * sin, x1 * sin + x2 * cos], axis=-1)

    xf = x.astype(jnp.float32)
    return jnp.concatenate([rotate(xf[..., :half], row), rotate(xf[..., half:], col)], axis=-1).astype(x.dtype)

def hyena_filters(length, w1, b1, w2, b2, w3, freq):
    t = jnp.arange(length, dtype=jnp.float32)
    t_norm = t / max(length - 1, 1)
    bands = jnp.linspace(1e-4, HY_BANDS - 1, HY_BANDS, dtype=jnp.float32)
    ang = (2.0 * math.pi / length) * t[:, None] * bands[None, :]
    z = jnp.concatenate([t_norm[:, None], jnp.cos(ang), -jnp.sin(ang)], axis=-1)
    fr = freq.astype(jnp.float32)
    h = jnp.sin(fr * (z @ w1.astype(jnp.float32) + b1.astype(jnp.float32)))
    h = jnp.sin(fr * (h @ w2.astype(jnp.float32) + b2.astype(jnp.float32)))
    h = h @ w3.astype(jnp.float32)
    decay = jnp.tile(jnp.linspace(HY_DECAY_MIN, HY_DECAY_MAX, HY_CH, dtype=jnp.float32), 2)
    h = h * jnp.exp(-t_norm[:, None] * decay[None, :])
    return h[:, :HY_CH], h[:, HY_CH:]

def bidirectional_long_conv(u, h_fwd, h_bwd, bias):
    length = u.shape[1]
    n = 2 * length
    kbuf = jnp.concatenate([h_fwd, jnp.zeros((1, HY_CH), jnp.float32), h_bwd[1:][::-1]], axis=0)
    uf = jnp.fft.rfft(u, n=n, axis=1)
    kf = jnp.fft.rfft(kbuf, n=n, axis=0)
    y = jnp.fft.irfft(uf * kf[None], n=n, axis=1)[:, :length]
    return y + u * bias

def hyena_mixer(p, conv_w, w1, b1, w2, b2, w3, freq, bias):
    length = p.shape[1]
    u = depthwise_conv(p, conv_w, (HY_SHORT - 1) // 2).astype(jnp.float32)
    x0, x1, v = u[..., :HY_CH], u[..., HY_CH:2 * HY_CH], u[..., 2 * HY_CH:]
    h_fwd, h_bwd = hyena_filters(length, w1, b1, w2, b2, w3, freq)
    z = bidirectional_long_conv(x1 * v, h_fwd, h_bwd, bias.astype(jnp.float32))
    return (x0 * z).astype(p.dtype)

def window_attention(p, pc, sink, row, col, need_ctx):
    b, s, _ = p.shape
    lc = pc.shape[1]
    grp = WA_HEADS // WA_KV_HEADS
    qd, kvd = WA_HEADS * HEAD_DIM, WA_KV_HEADS * HEAD_DIM
    scale = HEAD_DIM ** -0.5

    def split(t):
        n = t.shape[1]
        return (t[..., :qd].reshape(b, n, WA_KV_HEADS, grp, HEAD_DIM),
                t[..., qd:qd + kvd].reshape(b, n, WA_KV_HEADS, HEAD_DIM),
                t[..., qd + kvd:].reshape(b, n, WA_KV_HEADS, HEAD_DIM))

    q, k, v = split(p)
    qc, kc, vc = split(pc)
    q = axial_rope(q.reshape(b, s, WA_HEADS, HEAD_DIM), row, col).reshape(b, s, WA_KV_HEADS, grp, HEAD_DIM)
    k = axial_rope(k, row, col)
    sink_hg = sink.astype(jnp.float32).reshape(WA_KV_HEADS, grp)

    nb = s // WA_BLOCK
    span = WA_BLOCK + 2 * WINDOW
    pad = ((0, 0), (WINDOW, WINDOW), (0, 0), (0, 0))
    idx = jnp.arange(nb)[:, None] * WA_BLOCK + jnp.arange(span)[None, :]
    kb = jnp.pad(k, pad)[:, idx]
    vb = jnp.pad(v, pad)[:, idx]
    qb = q.reshape(b, nb, WA_BLOCK, WA_KV_HEADS, grp, HEAD_DIM)
    qpos = jnp.arange(nb)[:, None] * WA_BLOCK + jnp.arange(WA_BLOCK)[None, :]
    kpos = idx - WINDOW
    valid = ((jnp.abs(qpos[:, :, None] - kpos[:, None, :]) <= WINDOW)
             & (kpos[:, None, :] >= 0) & (kpos[:, None, :] < s))
    s_loc = jnp.einsum('bnqhgd,bnkhd->bnhgqk', qb, kb, preferred_element_type=jnp.float32) * scale
    s_loc = jnp.where(valid[None, :, None, None], s_loc, NEG)
    s_ctx = jnp.einsum('bnqhgd,bkhd->bnhgqk', qb, kc, preferred_element_type=jnp.float32) * scale
    sink_col = jnp.broadcast_to(sink_hg[None, None, :, :, None, None], s_ctx.shape[:-1] + (1,))
    prob = jax.nn.softmax(jnp.concatenate([sink_col, s_ctx, s_loc], axis=-1), axis=-1)
    o = (jnp.einsum('bnhgqk,bkhd->bnqhgd', prob[..., 1:1 + lc], vc.astype(jnp.float32))
         + jnp.einsum('bnhgqk,bnkhd->bnqhgd', prob[..., 1 + lc:], vb.astype(jnp.float32)))
    y = o.reshape(b, s, qd).astype(p.dtype)

    yc = None
    if need_ctx:
        sc = jnp.einsum('bqhgd,bkhd->bhgqk', qc, kc, preferred_element_type=jnp.float32) * scale
        sink_c = jnp.broadcast_to(sink_hg[None, :, :, None, None], sc.shape[:-1] + (1,))
        pcx = jax.nn.softmax(jnp.concatenate([sink_c, sc], axis=-1), axis=-1)
        yc = jnp.einsum('bhgqk,bkhd->bqhgd', pcx[..., 1:], vc.astype(jnp.float32)).reshape(b, lc, qd).astype(p.dtype)
    return y, yc

def neighborhood_attention(p, pc, rpb, need_ctx):
    b, s, _ = p.shape
    lc = pc.shape[1]
    hd = NA_HEADS * HEAD_DIM
    scale = HEAD_DIM ** -0.5
    rows = s // GRID_W
    kr = min(NA_KR, rows)
    q = p[..., :hd].reshape(b, rows, GRID_W, NA_HEADS, HEAD_DIM)
    k = p[..., hd:2 * hd].reshape(b, rows, GRID_W, NA_HEADS, HEAD_DIM)
    v = p[..., 2 * hd:].reshape(b, rows, GRID_W, NA_HEADS, HEAD_DIM)
    qc = pc[..., :hd].reshape(b, lc, NA_HEADS, HEAD_DIM)
    kc = pc[..., hd:2 * hd].reshape(b, lc, NA_HEADS, HEAD_DIM)
    vc = pc[..., 2 * hd:].reshape(b, lc, NA_HEADS, HEAD_DIM)

    r = jnp.arange(rows)
    key_rows = jnp.clip(r - kr // 2, 0, rows - kr)[:, None] + jnp.arange(kr)[None, :]
    kg = k[:, key_rows].reshape(b, rows, kr * GRID_W, NA_HEADS, HEAD_DIM)
    vg = v[:, key_rows].reshape(b, rows, kr * GRID_W, NA_HEADS, HEAD_DIM)
    cq = jnp.arange(GRID_W)
    c_start = jnp.clip(cq - NA_KC // 2, 0, GRID_W - NA_KC)
    col_ok = (cq[None, :] >= c_start[:, None]) & (cq[None, :] < c_start[:, None] + NA_KC)
    mask = jnp.broadcast_to(col_ok[:, None, :], (GRID_W, kr, GRID_W)).reshape(GRID_W, kr * GRID_W)
    dr = key_rows - r[:, None]
    dc = cq[None, :] - cq[:, None]
    ri = jnp.clip(dr + NA_KR - 1, 0, 2 * NA_KR - 2)[:, None, :, None]
    ci = jnp.clip(dc + NA_KC - 1, 0, 2 * NA_KC - 2)[None, :, None, :]
    bias = rpb.astype(jnp.float32)[:, ri, ci]
    bias = bias.reshape(NA_HEADS, rows, GRID_W, kr * GRID_W).transpose(1, 0, 2, 3)

    s_loc = jnp.einsum('brqhd,brkhd->brhqk', q, kg, preferred_element_type=jnp.float32) * scale + bias[None]
    s_loc = jnp.where(mask[None, None, None], s_loc, NEG)
    s_ctx = jnp.einsum('brqhd,bkhd->brhqk', q, kc, preferred_element_type=jnp.float32) * scale
    prob = jax.nn.softmax(jnp.concatenate([s_ctx, s_loc], axis=-1), axis=-1)
    o = (jnp.einsum('brhqk,bkhd->brqhd', prob[..., :lc], vc.astype(jnp.float32))
         + jnp.einsum('brhqk,brkhd->brqhd', prob[..., lc:], vg.astype(jnp.float32)))
    y = o.reshape(b, s, hd).astype(p.dtype)

    yc = None
    if need_ctx:
        sc = jnp.einsum('bqhd,bkhd->bhqk', qc, kc, preferred_element_type=jnp.float32) * scale
        pcx = jax.nn.softmax(sc, axis=-1)
        yc = jnp.einsum('bhqk,bkhd->bqhd', pcx, vc.astype(jnp.float32)).reshape(b, lc, hd).astype(p.dtype)
    return y, yc

def l2norm(x):
    return x * lax.rsqrt(jnp.sum(x * x, axis=-1, keepdims=True) + EPS)

def gdn_inputs(p, conv_w, a_log, dt_bias):
    b, n, _ = p.shape
    qkv = jax.nn.silu(depthwise_conv(p[..., :3 * GDN_W], conv_w, GDN_CONV // 2).astype(jnp.float32))
    q = l2norm(qkv[..., :GDN_W].reshape(b, n, GDN_HEADS, HEAD_DIM)) * HEAD_DIM ** -0.5
    k = l2norm(qkv[..., GDN_W:2 * GDN_W].reshape(b, n, GDN_HEADS, HEAD_DIM))
    v = qkv[..., 2 * GDN_W:].reshape(b, n, GDN_HEADS, HEAD_DIM)
    gate = p[..., 3 * GDN_W:4 * GDN_W].astype(jnp.float32)
    a = p[..., 4 * GDN_W:4 * GDN_W + 2 * GDN_HEADS].astype(jnp.float32).reshape(b, n, 2, GDN_HEADS)
    bb = p[..., 4 * GDN_W + 2 * GDN_HEADS:].astype(jnp.float32).reshape(b, n, 2, GDN_HEADS)
    g = -jnp.exp(a_log.astype(jnp.float32)) * jax.nn.softplus(a + dt_bias.astype(jnp.float32))
    beta = jax.nn.sigmoid(bb)
    return q, k, v, gate, g, beta

def gdn_chunked(q, k, v, g, beta, s0, emit):
    b, n, h, d = q.shape
    nc = n // GDN_CHUNK

    def to_chunks(x):
        x = x.reshape((b, nc, GDN_CHUNK, h) + x.shape[3:])
        return jnp.moveaxis(x, (1, 3), (0, 2))

    qc, kc, vc = to_chunks(q), to_chunks(k), to_chunks(v)
    gc, bc = to_chunks(g), to_chunks(beta)
    gcum = jnp.cumsum(gc, axis=-1)
    tri = jnp.tril(jnp.ones((GDN_CHUNK, GDN_CHUNK), bool))
    strict = jnp.tril(jnp.ones((GDN_CHUNK, GDN_CHUNK), bool), -1)
    decay = jnp.exp(jnp.where(tri, gcum[..., :, None] - gcum[..., None, :], NEG))
    kb = kc * bc[..., None]
    lmat = jnp.where(strict, jnp.einsum('nbhid,nbhjd->nbhij', kb, kc) * decay, 0.0)
    eye = jnp.eye(GDN_CHUNK, dtype=jnp.float32)
    tmat = lax.linalg.triangular_solve(eye + lmat, jnp.broadcast_to(eye, lmat.shape), left_side=True, lower=True)
    u = tmat @ (vc * bc[..., None])
    w = tmat @ (kb * jnp.exp(gcum)[..., None])
    k_dec = kc * jnp.exp(gcum[..., -1:] - gcum)[..., None]
    g_last = jnp.exp(gcum[..., -1])
    xs = (u, w, k_dec, g_last)
    if emit:
        attn = jnp.einsum('nbhid,nbhjd->nbhij', qc, kc) * decay
        q_dec = qc * jnp.exp(gcum)[..., None]
        xs = xs + (attn, q_dec)

    def step(state, xs_c):
        u_c, w_c, kd_c, gl = xs_c[:4]
        u_new = u_c - jnp.einsum('bhcd,bhde->bhce', w_c, state)
        s_new = state * gl[..., None, None] + jnp.einsum('bhcd,bhce->bhde', kd_c, u_new)
        if emit:
            a_c, qd_c = xs_c[4:]
            o = jnp.einsum('bhcd,bhde->bhce', qd_c, state) + jnp.einsum('bhij,bhje->bhie', a_c, u_new)
            return s_new, o
        return s_new, None

    s_final, o = lax.scan(step, s0, xs)
    if emit:
        o = jnp.moveaxis(o, (0, 2), (1, 3)).reshape(b, n, h, d)
    return o, s_final

def gdn_mixer(p, pc, conv_w, a_log, dt_bias, norm_g, need_ctx):
    q, k, v, gate, g, beta = gdn_inputs(p, conv_w, a_log, dt_bias)
    qc, kc, vc, gatec, gc, betac = gdn_inputs(pc, conv_w, a_log, dt_bias)
    b = p.shape[0]
    outs, outs_c = [], []
    for direction in range(2):
        flip = (lambda t: t[:, ::-1]) if direction == 1 else (lambda t: t)
        s0 = jnp.zeros((b, GDN_HEADS, HEAD_DIM, HEAD_DIM), jnp.float32)
        oc, s_ctx = gdn_chunked(flip(qc), flip(kc), flip(vc), flip(gc[:, :, direction]),
                                flip(betac[:, :, direction]), s0, need_ctx)
        o, _ = gdn_chunked(flip(q), flip(k), flip(v), flip(g[:, :, direction]),
                           flip(beta[:, :, direction]), s_ctx, True)
        outs.append(flip(o))
        if need_ctx:
            outs_c.append(flip(oc))

    def finish(o, gt):
        bb, n = o.shape[:2]
        return (rmsnorm(o, norm_g).reshape(bb, n, GDN_W) * jax.nn.silu(gt)).astype(p.dtype)

    y = finish(outs[0] + outs[1], gate)
    yc = finish(outs_c[0] + outs_c[1], gatec) if need_ctx else None
    return y, yc

def moe_ffn(t, w_router, e_bias, w_gate, w_up, w_down, ws_gate, ws_up, ws_down):
    n_tok, d = t.shape
    scores = jax.nn.sigmoid(jnp.dot(t, w_router, preferred_element_type=jnp.float32))
    _, top_idx = lax.top_k(scores + e_bias.astype(jnp.float32), TOP_K)
    top_s = jnp.take_along_axis(scores, top_idx, axis=-1)
    top_w = top_s / jnp.sum(top_s, axis=-1, keepdims=True) * ROUTED_SCALE
    n_asg = n_tok * TOP_K
    flat_e = top_idx.reshape(n_asg)
    flat_w = top_w.reshape(n_asg)
    counts = jnp.bincount(flat_e, length=N_EXPERTS)
    padded = (counts + MOE_BLOCK - 1) // MOE_BLOCK * MOE_BLOCK
    pad_end = jnp.cumsum(padded)
    pad_start = pad_end - padded
    raw_start = jnp.cumsum(counts) - counts
    order = jnp.argsort(flat_e)
    sorted_e = flat_e[order]
    dest = pad_start[sorted_e] + jnp.arange(n_asg) - raw_start[sorted_e]
    n_blocks = -(-n_asg // MOE_BLOCK) + N_EXPERTS
    n_rows = n_blocks * MOE_BLOCK
    row_tok = jnp.full((n_rows,), n_tok, jnp.int32).at[dest].set((order // TOP_K).astype(jnp.int32))
    row_w = jnp.zeros((n_rows,), jnp.float32).at[dest].set(flat_w[order])
    blk_e = jnp.minimum(jnp.searchsorted(pad_end, jnp.arange(n_blocks) * MOE_BLOCK, side='right'), N_EXPERTS - 1)
    t_pad = jnp.concatenate([t, jnp.zeros((1, d), t.dtype)], axis=0)
    xb = t_pad[row_tok].reshape(n_blocks, MOE_BLOCK, d)

    def expert_block(args):
        xblk, e = args
        hid = jax.nn.silu(xblk @ w_gate[e]) * (xblk @ w_up[e])
        return hid @ w_down[e]

    yb = lax.map(expert_block, (xb, blk_e)).reshape(n_rows, d)
    routed = jax.ops.segment_sum(yb * row_w[:, None].astype(yb.dtype), row_tok, num_segments=n_tok + 1)[:n_tok]
    shared = (jax.nn.silu(t @ ws_gate) * (t @ ws_up)) @ ws_down
    return routed + shared

def setup_inputs(seed: int = 0) -> dict:
    key = jax.random.key(seed)
    ks = iter(jax.random.split(key, 40))
    f32 = jnp.float32

    def nrm(shape, scale):
        return scale * jax.random.normal(next(ks), shape, f32)

    nl, d = DEPTH, D_MODEL
    a_init = jax.random.uniform(next(ks), (nl, 2, GDN_HEADS), f32, 1.0, 16.0)
    dt = jnp.exp(jax.random.uniform(next(ks), (nl, 2, GDN_HEADS), f32, math.log(1e-3), math.log(1e-1)))
    return {
        'x': nrm((BATCH, SEQ, d), 1.0),
        'c': nrm((BATCH, d), 1.0),
        'ctx': nrm((BATCH, CTX_LEN, d), 1.0),
        'c_ctx': nrm((d,), 1.0),
        'w_ada': nrm((nl, d, 6 * d), 0.5 * d ** -0.5),
        'b_ada': nrm((nl, 6 * d), 0.02),
        'norm1': 1.0 + nrm((nl, d), 0.02),
        'norm2': 1.0 + nrm((nl, d), 0.02),
        'norm_f': 1.0 + nrm((d,), 0.02),
        'w_in': nrm((nl, d, D_IN), d ** -0.5),
        'w_out': nrm((nl, D_MIX, d), D_MIX ** -0.5),
        'hy_conv': nrm((nl, HY_SHORT, HY_IN), HY_SHORT ** -0.5),
        'hy_w1': nrm((nl, HY_EMB, HY_FFN), HY_EMB ** -0.5),
        'hy_b1': nrm((nl, HY_FFN), 0.1),
        'hy_w2': nrm((nl, HY_FFN, HY_FFN), HY_FFN ** -0.5),
        'hy_b2': nrm((nl, HY_FFN), 0.1),
        'hy_w3': nrm((nl, HY_FFN, 2 * HY_CH), HY_FILTER_SCALE * HY_FFN ** -0.5),
        'hy_freq': 1.0 + nrm((nl, HY_FFN), 0.1),
        'hy_bias': nrm((nl, HY_CH), 0.5),
        'wa_sink': nrm((nl, WA_HEADS), 0.5),
        'na_rpb': nrm((nl, NA_HEADS, 2 * NA_KR - 1, 2 * NA_KC - 1), 0.02),
        'gdn_conv': nrm((nl, GDN_CONV, 3 * GDN_W), GDN_CONV ** -0.5),
        'gdn_a_log': jnp.log(a_init),
        'gdn_dt_bias': dt + jnp.log(-jnp.expm1(-dt)),
        'gdn_norm': 1.0 + nrm((nl, HEAD_DIM), 0.02),
        'moe_router': nrm((nl, d, N_EXPERTS), d ** -0.5),
        'moe_bias': nrm((nl, N_EXPERTS), 0.01),
        'moe_gate': nrm((nl, N_EXPERTS, d, D_EXPERT), d ** -0.5),
        'moe_up': nrm((nl, N_EXPERTS, d, D_EXPERT), d ** -0.5),
        'moe_down': nrm((nl, N_EXPERTS, D_EXPERT, d), D_EXPERT ** -0.5),
        'sh_gate': nrm((nl, d, D_SHARED), d ** -0.5),
        'sh_up': nrm((nl, d, D_SHARED), d ** -0.5),
        'sh_down': nrm((nl, D_SHARED, d), D_SHARED ** -0.5),
    }

def reference(x, c, ctx, c_ctx, w_ada, b_ada, norm1, norm2, norm_f, w_in, w_out,
              hy_conv, hy_w1, hy_b1, hy_w2, hy_b2, hy_w3, hy_freq, hy_bias,
              wa_sink, na_rpb, gdn_conv, gdn_a_log, gdn_dt_bias, gdn_norm,
              moe_router, moe_bias, moe_gate, moe_up, moe_down, sh_gate, sh_up, sh_down):
    b, s, d = x.shape
    lc = ctx.shape[1]
    pos = jnp.arange(s)
    row, col = pos // GRID_W, pos % GRID_W
    xc = ctx
    silu_c = jax.nn.silu(c)
    silu_cc = jax.nn.silu(c_ctx)
    o1, o2, o3 = HY_IN, HY_IN + WA_IN, HY_IN + WA_IN + NA_IN
    for l in range(DEPTH):
        need_ctx = l < DEPTH - 1
        sh1, sc1, g1, sh2, sc2, g2 = [m[:, None, :] for m in jnp.split(silu_c @ w_ada[l] + b_ada[l], 6, axis=-1)]
        sh1c, sc1c, g1c, sh2c, sc2c, g2c = jnp.split(silu_cc @ w_ada[l] + b_ada[l], 6, axis=-1)
        h = rmsnorm(x, norm1[l]) * (1.0 + sc1) + sh1
        hc = rmsnorm(xc, norm1[l]) * (1.0 + sc1c) + sh1c
        p = h @ w_in[l]
        pc = hc @ w_in[l]
        hy_args = (hy_conv[l], hy_w1[l], hy_b1[l], hy_w2[l], hy_b2[l], hy_w3[l], hy_freq[l], hy_bias[l])
        y_hy = hyena_mixer(p[..., :o1], *hy_args)
        y_wa, yc_wa = window_attention(p[..., o1:o2], pc[..., o1:o2], wa_sink[l], row, col, need_ctx)
        y_na, yc_na = neighborhood_attention(p[..., o2:o3], pc[..., o2:o3], na_rpb[l], need_ctx)
        y_gd, yc_gd = gdn_mixer(p[..., o3:], pc[..., o3:], gdn_conv[l], gdn_a_log[l], gdn_dt_bias[l], gdn_norm[l], need_ctx)
        x = x + g1 * (jnp.concatenate([y_hy, y_wa, y_na, y_gd], axis=-1) @ w_out[l])
        moe_args = (moe_router[l], moe_bias[l], moe_gate[l], moe_up[l], moe_down[l], sh_gate[l], sh_up[l], sh_down[l])
        h2 = rmsnorm(x, norm2[l]) * (1.0 + sc2) + sh2
        if need_ctx:
            yc_hy = hyena_mixer(pc[..., :o1], *hy_args)
            xc = xc + g1c * (jnp.concatenate([yc_hy, yc_wa, yc_na, yc_gd], axis=-1) @ w_out[l])
            h2c = rmsnorm(xc, norm2[l]) * (1.0 + sc2c) + sh2c
            f = moe_ffn(jnp.concatenate([h2.reshape(b * s, d), h2c.reshape(b * lc, d)], axis=0), *moe_args)
            x = x + g2 * f[:b * s].reshape(b, s, d)
            xc = xc + g2c * f[b * s:].reshape(b, lc, d)
        else:
            x = x + g2 * moe_ffn(h2.reshape(b * s, d), *moe_args).reshape(b, s, d)
    return rmsnorm(x, norm_f)


_drawn_inputs = setup_inputs


def setup_inputs(seed=0):
    import zlib

    import numpy as np

    out = dict(_drawn_inputs(seed))
    spreads = {}
    factors = {'norm_f': 8.563, 'wa_sink': 64.0, 'na_rpb': 25.879, 'gdn_norm': 3.284}
    for name, (base, spread) in spreads.items():
        noise = np.random.default_rng([zlib.crc32(name.encode()), seed]).standard_normal(out[name].shape)
        drawn = base * np.exp(spread * noise) if base else spread * noise
        out[name] = jnp.asarray(drawn.astype(out[name].dtype))
    for name, factor in factors.items():
        out[name] = (out[name] * factor).astype(out[name].dtype)
    return out
```

```python
import math
from contextlib import ExitStack

import numpy as np

import concourse.bass as bass
from concourse import mybir

F32 = mybir.dt.float32
U32 = mybir.dt.uint32
ALU = mybir.AluOpType
ACT = mybir.ActivationFunctionType
AX = mybir.AxisListType

P = 128
D = 1024
KD = D // P
SEQ = 1024
CTX = 256
NTL = SEQ // P
NTC = CTX // P
NT = NTL + NTC
TOK = SEQ + CTX
DEPTH = 2
BANK = 512
HD = 64

HY_CH = 256
HY_BANDS = 16
HY_EMB = 1 + 2 * HY_BANDS
HY_FFN = 64
HY_IN = 3 * HY_CH
WA_IN = 512
NA_IN = 768
GW = 256
GDN_IN = 4 * GW + 16
WA0, NA0, GD0 = HY_IN, HY_IN + WA_IN, HY_IN + WA_IN + NA_IN
D_IN = GD0 + GDN_IN
NE = 32
DE = 256
NEG = -1e30
EPS = 1e-6
SCALE = HD ** -0.5
GRID_W = 64
NA_KR, NA_KC = 8, 16
ROUTED_SCALE = 2.5
MAGIC = 1.5 * 2.0 ** 23
CHUNKS = [(0, BANK), (BANK, BANK), (SEQ, CTX)]


def wait(eng, sem, value):
    if not isinstance(value, int) or value > 0:
        eng.wait_ge(sem, value)


class Chain:

    def __init__(self, eng, sem):
        self.eng, self.sem, self.n = eng, sem, 0

    def __call__(self, instruction):
        self.n += 1
        instruction.then_inc(self.sem, 1)
        self.eng.wait_ge(self.sem, self.n)


class Stage:

    def __init__(self, nc, tag):
        self.nc, self.tag, self.sems, self.stack = nc, tag, [], ExitStack()

    def __enter__(self):
        self.stack.__enter__()
        return self

    def __exit__(self, *a):
        self.nc.clear_and_free_semaphores(self.sems)
        self.nc.all_engine_barrier()
        return self.stack.__exit__(*a)

    def sb(self, name, shape, dt=F32):
        return self.stack.enter_context(self.nc.sbuf_tensor(f"{name}_{self.tag}", shape, dt))

    def sem(self, name):
        s = self.nc.alloc_semaphore(f"{name}_{self.tag}")
        self.sems.append(s)
        return s


def stage_setup(nc, g):
    with Stage(nc, "setup") as st:
        cT = st.sb("cT", [P, KD, 2])
        e = st.sb("e", [P, KD, 2])
        loaded, c_loaded, exp_ready, silu_step = (st.sem(n) for n in ("loaded", "c_loaded", "exp_ready", "silu_step"))
        with nc.Block() as block:
            @block.sync
            def _(sp):
                sp.dma_start(g.ident[:], g.t_ident).then_inc(loaded, 16)

                with nc.allow_non_contiguous_dma("conditioning vectors, once"):
                    sp.dma_start(cT[:, :, 0], g.c.rearrange("o (k p) -> p (o k)", p=P)).then_inc(c_loaded, 16)
                    sp.dma_start(cT[:, :, 1], g.c_ctx.rearrange("(k p) -> p k", p=P)).then_inc(c_loaded, 16)
                sp.wait_ge(loaded, 16)

            @block.scalar
            def _(act):
                act.wait_ge(c_loaded, 32)
                nc.scalar.activation(e[:], cT[:], ACT.Exp, scale=-1.0).then_inc(exp_ready, 1)

            @block.vector
            def _(dve):
                link = Chain(dve, silu_step)
                dve.wait_ge(exp_ready, 1)
                link(nc.vector.tensor_scalar_add(e[:], e[:], 1.0))
                link(nc.vector.reciprocal(e[:], e[:]))
                link(nc.vector.tensor_tensor(g.siluT[:], e[:], cT[:], ALU.mult))


def stage_modulation(nc, g, l):
    NCH = 6 * D // BANK
    with Stage(nc, f"mod{l}") as st:
        w = st.sb("w", [P, 3, KD, BANK])
        rows = st.sb("rows", [2, 6 * D])
        bias = st.sb("bias", [2, 6 * D])
        normT = st.sb("normT", [P, 2, KD])
        w_loaded = [st.sem(f"w_loaded{i}") for i in range(3)]
        bias_loaded, norm_loaded, chunk_ready, row_ready, turned, stored, mod_step = (
            st.sem(n) for n in ("bias_loaded", "norm_loaded", "chunk_ready", "row_ready", "turned", "stored", "mod_step"))
        wv = g.w_ada[l].rearrange("(k p) n -> p k n", p=P)
        with nc.Block() as block:
            @block.sync
            def _(sp):
                sp.dma_start(bias[:], g.b_ada[l].rearrange("(o n) -> o n", o=1).to_broadcast([2, 6 * D])).then_inc(bias_loaded, 16)
                with nc.allow_non_contiguous_dma("norm gains, once a layer"):
                    sp.dma_start(normT[:, 0, :], g.norm1[l].rearrange("(k p) -> p k", p=P)).then_inc(norm_loaded, 16)
                    sp.dma_start(normT[:, 1, :], g.norm2[l].rearrange("(k p) -> p k", p=P)).then_inc(norm_loaded, 16)
                for n in range(NCH):
                    wait(sp, chunk_ready, n - 2)
                    sp.dma_start(w[:, n % 3], wv[:, :, n * BANK:(n + 1) * BANK]).then_inc(w_loaded[n % 3], 16)
                sp.wait_ge(row_ready, NCH)
                sp.dma_start(g.mod_rows, rows[:]).then_inc(stored, 16)
                sp.wait_ge(stored, 16)

            @block.tensor
            def _(pe):
                for n in range(NCH):
                    pe.wait_ge(w_loaded[n % 3], 16 * (n // 3 + 1))
                    wait(pe, row_ready, n - 1)
                    for k in range(KD):
                        mm = nc.tensor.matmul(g.ps[0:2, n % 2, :], g.siluT[:, k, :], w[:, n % 3, k, :],
                                              start=k == 0, stop=k == KD - 1)
                    mm.then_inc(chunk_ready, 1)
                pe.wait_ge(row_ready, NCH)
                for k in range(6 * KD):
                    mm = nc.tensor.transpose(g.ps[:, 2, 2 * k:2 * k + 2], rows[:, k * P:(k + 1) * P], g.ident[0:2, 0:2])
                mm.then_inc(turned, 1)

            @block.vector
            def _(dve):
                link = Chain(dve, mod_step)
                dve.wait_ge(bias_loaded, 16)
                for n in range(NCH):
                    dve.wait_ge(chunk_ready, n + 1)
                    cols = slice(n * BANK, (n + 1) * BANK)
                    nc.vector.tensor_tensor(rows[:, cols], g.ps[0:2, n % 2, :], bias[:, cols], ALU.add).then_inc(row_ready, 1)
                dve.wait_ge(turned, 1)
                link(nc.vector.tensor_copy(g.modT[:], g.ps[:, 2, 0:12 * KD].rearrange("p (k s) -> p k s", s=2)))
                dve.wait_ge(norm_loaded, 32)
                for i, sc0 in ((0, KD), (1, 4 * KD)):
                    link(nc.vector.scalar_tensor_tensor(
                        out=g.gain[:, i], in0=g.modT[:, sc0:sc0 + KD, :], scalar=1.0,
                        in1=normT[:, i, :].unsqueeze(2).to_broadcast([P, KD, 2]), op0=ALU.add, op1=ALU.mult))


def token_tile(latent, context, t):
    return latent[t * P:(t + 1) * P, :] if t < NTL else context[(t - NTL) * P:(t - NTL + 1) * P, :]


def stage_norm(nc, g, l, which, tiles, latent, context):
    with Stage(nc, f"norm{which}_{l}") as st:
        x = st.sb("x", [P, 3, D])
        xn = st.sb("xn", [P, 2, D])
        sq = st.sb("sq", [P, D])
        ss = st.sb("ss", [P, tiles])
        rs = st.sb("rs", [P, tiles])
        rt = st.sb("rt", [P, tiles])
        x_loaded = [st.sem(f"x_loaded{i}") for i in range(3)]
        names = "squares_summed mean_ready root_ready rstd_ready scaled turned taken_lo taken_hi step".split()
        squares_summed, mean_ready, root_ready, rstd_ready, scaled, turned, taken_lo, taken_hi, step = (st.sem(n) for n in names)
        sh0 = 0 if which == 0 else 3 * KD
        with nc.Block() as block:
            @block.sync
            def _(sp):
                for t in range(tiles):
                    wait(sp, scaled, t - 2)
                    sp.dma_start(x[:, t % 3], token_tile(latent, context, t)).then_inc(x_loaded[t % 3], 16)

            @block.scalar
            def _(act):
                for t in range(tiles + 1):
                    if t < tiles:
                        act.wait_ge(x_loaded[t % 3], 16 * (t // 3 + 1))
                        wait(act, squares_summed, t)
                        nc.scalar.activation(sq[:], x[:, t % 3], ACT.Square, accum_out=ss[:, t:t + 1]).then_inc(squares_summed, 1)
                        act.wait_ge(mean_ready, t + 1)
                        nc.scalar.activation(rs[:, t:t + 1], ss[:, t:t + 1], ACT.Sqrt).then_inc(root_ready, 1)
                    if t >= 1:
                        u = t - 1
                        s = u // NTL
                        act.wait_ge(turned, u + 1)
                        for k in range(KD // 2, KD):
                            o = nc.scalar.activation(g.hT[:, k, u * P:(u + 1) * P],
                                                     g.ps[:, 2 * (u % 2) + 1, (k % 4) * P:(k % 4 + 1) * P], ACT.Identity,
                                                     scale=g.gain[:, which, k, s:s + 1], bias=g.modT[:, sh0 + k, s:s + 1])
                        o.then_inc(taken_hi, 1)

            @block.vector
            def _(dve):
                for t in range(tiles + 1):
                    if t < tiles:
                        dve.wait_ge(squares_summed, t + 1)
                        nc.vector.tensor_scalar(ss[:, t:t + 1], ss[:, t:t + 1], 1.0 / D, EPS, ALU.mult, ALU.add).then_inc(mean_ready, 1)
                        dve.wait_ge(root_ready, t + 1)
                        nc.vector.reciprocal(rt[:, t:t + 1], rs[:, t:t + 1]).then_inc(rstd_ready, 1)
                        dve.wait_ge(rstd_ready, t + 1)
                        wait(dve, turned, t - 1)
                        nc.vector.tensor_scalar(xn[:, t % 2], x[:, t % 3], rt[:, t:t + 1], None, ALU.mult).then_inc(scaled, 1)
                    if t >= 1:
                        u = t - 1
                        s = u // NTL
                        dst = g.hT[:, 0:4, u * P:(u + 1) * P]
                        dve.wait_ge(turned, u + 1)
                        nc.vector.tensor_tensor(dst, g.ps[:, 2 * (u % 2), :].rearrange("p (k n) -> p k n", k=4),
                                                g.gain[:, which, 0:4, s:s + 1].to_broadcast([P, 4, P]), ALU.mult).then_inc(step, 1)
                        dve.wait_ge(step, t)
                        nc.vector.tensor_tensor(dst, dst, g.modT[:, sh0:sh0 + 4, s:s + 1].to_broadcast([P, 4, P]),
                                                ALU.add).then_inc(taken_lo, 1)

            @block.tensor
            def _(pe):
                for t in range(tiles):
                    pe.wait_ge(scaled, t + 1)
                    wait(pe, taken_lo, t - 1)
                    wait(pe, taken_hi, t - 1)
                    for k in range(KD):
                        mm = nc.tensor.transpose(g.ps[:, 2 * (t % 2) + k // 4, (k % 4) * P:(k % 4 + 1) * P],
                                                 xn[:, t % 2, k * P:(k + 1) * P], g.ident[:])
                    mm.then_inc(turned, 1)


def stage_hyena(nc, g, l, ctx):
    L = CTX if ctx else SEQ
    tok0 = SEQ if ctx else 0
    NL = L // P
    CH = min(L, BANK)
    NC = L // CH
    fil_z, fil_dec, t_dft, t_dft2 = g.hy_tables[ctx]
    with Stage(nc, f"hy{l}{'c' if ctx else ''}") as st:
        Kf = st.sb("Kf", [P, NL, 3 * HY_CH])
        x0 = st.sb("x0", [P, 2, L])
        gv = st.sb("gv", [P, 2, L])
        gT = st.sb("gT", [P, NL, HY_CH])
        with ExitStack() as filt:
            def sb(name, shape):
                return filt.enter_context(nc.sbuf_tensor(f"{name}_{st.tag}", shape, F32))
            zT = sb("zT", [HY_EMB, L])
            w1 = sb("w1", [HY_EMB, HY_FFN])
            w2 = sb("w2", [HY_FFN, HY_FFN])
            w3 = sb("w3", [HY_FFN, 2 * HY_CH])
            cols = sb("cols", [HY_FFN, 3])
            arg = sb("arg", [HY_FFN, L])
            rnd = sb("rnd", [HY_FFN, L])
            hid = sb("hid", [HY_FFN, L])
            dec = sb("dec", [P, 2, 2 * HY_CH])
            fb = sb("fb", [P, 2, 2 * HY_CH])
            kpm = sb("kpm", [P, 2, NL, HY_CH])
            dft = sb("dft", [P, 2, 2, NL, P])
            names = ("small_loaded sin_in sin_ready layer_ready filt_ready filt_taken fb_ready kpm_ready spec_ready spec_taken arg_step").split()
            small_loaded, sin_in, sin_ready, layer_ready, filt_ready, filt_taken, fb_ready, kpm_ready, spec_ready, spec_taken, arg_step = (
                st.sem(n) for n in names)
            dec_loaded = [st.sem(f"dec_loaded{i}") for i in range(2)]
            dft_loaded = [st.sem(f"dft_loaded{i}") for i in range(2)]
            with nc.Block() as block:
                @block.sync
                def _(sp):
                    for dst, src in ((zT[:], fil_z), (w1[:], g.hy_w1[l]), (w2[:], g.hy_w2[l]), (w3[:], g.hy_w3[l]),
                                     (cols[:, 0:1], g.hy_b1[l].rearrange("(p o) -> p o", o=1)),
                                     (cols[:, 1:2], g.hy_b2[l].rearrange("(p o) -> p o", o=1)),
                                     (cols[:, 2:3], g.hy_freq[l].rearrange("(p o) -> p o", o=1))):
                        sp.dma_start(dst, src).then_inc(small_loaded, 16)
                    for t in range(NL):
                        wait(sp, fb_ready, t - 1)
                        sp.dma_start(dec[:, t % 2], fil_dec[t * P:(t + 1) * P, :]).then_inc(dec_loaded[t % 2], 16)
                    for t in range(NL):
                        wait(sp, spec_ready, t - 1)
                        for i in range(2):
                            sp.dma_start(dft[:, t % 2, i], t_dft[i, t]).then_inc(dft_loaded[t % 2], 16)

                @block.tensor
                def _(pe):
                    pe.wait_ge(small_loaded, 16 * 7)
                    for layer in range(2):
                        if layer:
                            pe.wait_ge(sin_ready, 1)
                        for c in range(NC):
                            mm = nc.tensor.matmul(g.ps[0:HY_FFN, c, 0:CH], w2[:] if layer else w1[:],
                                                  (hid if layer else zT)[:, c * CH:(c + 1) * CH], start=True, stop=True)
                        mm.then_inc(layer_ready, 1)
                    pe.wait_ge(sin_ready, 2)
                    for t in range(NL):
                        wait(pe, fb_ready, t - 1)
                        nc.tensor.matmul(g.ps[:, 2 + t % 2, :], hid[:, t * P:(t + 1) * P], w3[:], start=True, stop=True).then_inc(filt_ready, 1)
                    pe.wait_ge(kpm_ready, NL)
                    for t in range(NL):
                        pe.wait_ge(dft_loaded[t % 2], 32 * (t // 2 + 1))
                        wait(pe, spec_taken, t - 1)
                        for i in range(2):
                            for j in range(NL):
                                mm = nc.tensor.matmul(g.ps[:, 4 + 2 * (t % 2) + i, 0:HY_CH], dft[:, t % 2, i, j, :], kpm[:, i, j, :],
                                                      start=j == 0, stop=j == NL - 1)
                        mm.then_inc(spec_ready, 1)

                @block.scalar
                def _(act):
                    for layer in range(2):
                        act.wait_ge(sin_in, layer + 1)
                        nc.scalar.activation(hid[:], arg[:], ACT.Sin).then_inc(sin_ready, 1)

                @block.vector
                def _(dve):
                    link = Chain(dve, arg_step)
                    dve.wait_ge(small_loaded, 16 * 7)
                    for layer in range(2):
                        dve.wait_ge(layer_ready, layer + 1)
                        link(nc.vector.tensor_scalar(arg[:].rearrange("p (c n) -> p c n", c=NC), g.ps[0:HY_FFN, 0:NC, 0:CH],
                                                     cols[:, layer:layer + 1], cols[:, 2:3], ALU.add, ALU.mult))
                        link(nc.vector.tensor_scalar(rnd[:], arg[:], 1.0 / (2 * math.pi), MAGIC, ALU.mult, ALU.add))
                        link(nc.vector.tensor_scalar(rnd[:], rnd[:], -MAGIC, None, ALU.add))
                        for part in TWO_PI_PARTS:
                            link(nc.vector.scalar_tensor_tensor(out=arg[:], in0=rnd[:], scalar=-part, in1=arg[:],
                                                                op0=ALU.mult, op1=ALU.add))
                        nc.vector.tensor_scalar(arg[:], arg[:], PI_DOWN, -PI_DOWN, ALU.min, ALU.max).then_inc(sin_in, 1)
                    for t in range(NL):
                        dve.wait_ge(filt_ready, t + 1)
                        dve.wait_ge(dec_loaded[t % 2], 16 * (t // 2 + 1))
                        wait(dve, kpm_ready, t - 1)
                        nc.vector.tensor_tensor(fb[:, t % 2], g.ps[:, 2 + t % 2, :], dec[:, t % 2], ALU.mult).then_inc(fb_ready, 1)
                        dve.wait_ge(fb_ready, t + 1)
                        nc.vector.tensor_tensor(kpm[:, 0, t], fb[:, t % 2, 0:HY_CH], fb[:, t % 2, HY_CH:], ALU.add)
                        nc.vector.tensor_tensor(kpm[:, 1, t], fb[:, t % 2, 0:HY_CH], fb[:, t % 2, HY_CH:], ALU.subtract).then_inc(kpm_ready, 1)
                    for t in range(NL):
                        dve.wait_ge(spec_ready, t + 1)
                        b = 4 + 2 * (t % 2)
                        nc.vector.tensor_copy(Kf[:, t, 0:2 * HY_CH].rearrange("p (i n) -> p i n", i=2), g.ps[:, b:b + 2, 0:HY_CH])
                        nc.vector.tensor_copy(Kf[:, t, 2 * HY_CH:], g.ps[:, b, 0:HY_CH]).then_inc(spec_taken, 1)
        hb = st.sb("hb", [P, 2])
        with ExitStack() as early:
            def sb(name, shape):
                return early.enter_context(nc.sbuf_tensor(f"{name}_{st.tag}", shape, F32))
            w = sb("w", [P, KD, HY_IN])
            raw = sb("raw", [P, 2, L + 2])
            u1 = sb("u1", [P, L])
            cw = sb("cw", [P, 6, 3])
            names = ("w_in_loaded cw_loaded padded proj_ready proj_taken conv_step tile_ready gv_turned gt_ready").split()
            w_in_loaded, cw_loaded, padded, proj_ready, proj_taken, conv_step, tile_ready, gv_turned, gt_ready = (st.sem(n) for n in names)
            order = [0, 1, 2, 4, 3, 5]
            with nc.Block() as block:
                @block.sync
                def _(sp):
                    sp.dma_start(w[:], g.w_in[l].rearrange("(k p) n -> p k n", p=P)[:, :, 0:HY_IN]).then_inc(w_in_loaded, 16)
                    with nc.allow_non_contiguous_dma("filter taps, once a layer"):
                        for i in range(3):
                            sp.dma_start(cw[:, :, i], g.hy_conv[l, i].rearrange("(f p) -> p f", p=P)).then_inc(cw_loaded, 16)
                        sp.dma_start(hb[:], g.hy_bias[l].rearrange("(f p) -> p f", p=P)).then_inc(cw_loaded, 16)

                @block.gpsimd
                def _(pool):
                    pool.memset(raw[:, :, 0:1], 0.0)
                    pool.memset(raw[:, :, L + 1:L + 2], 0.0).then_inc(padded, 1)

                @block.tensor
                def _(pe):
                    pe.wait_ge(w_in_loaded, 16)
                    n = 0
                    for f in order:
                        for c in range(NC):
                            wait(pe, proj_taken, n - 3)
                            for k in range(KD):
                                mm = nc.tensor.matmul(g.ps[:, n % 4, 0:CH], w[:, k, f * P:(f + 1) * P],
                                                      g.hT[:, k, tok0 + c * CH:tok0 + (c + 1) * CH], start=k == 0, stop=k == KD - 1)
                            mm.then_inc(proj_ready, 1)
                            n += 1
                    for ct in range(2):
                        pe.wait_ge(tile_ready, 4 + 2 * ct)
                        for t0 in range(0, NL, 4):
                            m = ct * ((NL + 3) // 4) + t0 // 4
                            wait(pe, gt_ready, m - 1)
                            for t in range(t0, min(t0 + 4, NL)):
                                mm = nc.tensor.transpose(g.ps[:, 4 + m % 2, (t - t0) * P:(t - t0 + 1) * P],
                                                         gv[:, ct, t * P:(t + 1) * P], g.ident[:])
                            mm.then_inc(gv_turned, 1)

                @block.scalar
                def _(act):
                    n = 0
                    for j, f in enumerate(order):
                        wait(act, tile_ready, j - 1)
                        for c in range(NC):
                            act.wait_ge(proj_ready, n + 1)
                            nc.scalar.copy(raw[:, j % 2, 1 + c * CH:1 + (c + 1) * CH], g.ps[:, n % 4, 0:CH]).then_inc(proj_taken, 1)
                            n += 1
                    m = 0
                    for ct in range(2):
                        for t0 in range(0, NL, 4):
                            nt = min(4, NL - t0)
                            act.wait_ge(gv_turned, m + 1)
                            nc.scalar.copy(gT[:, t0:t0 + nt, ct * P:(ct + 1) * P],
                                           g.ps[:, 4 + m % 2, 0:nt * P].rearrange("p (t n) -> p t n", n=P)).then_inc(gt_ready, 1)
                            m += 1

                @block.vector
                def _(dve):
                    link = Chain(dve, conv_step)
                    dve.wait_ge(padded, 1)
                    dve.wait_ge(cw_loaded, 64)
                    for j, f in enumerate(order):
                        dve.wait_ge(proj_taken, NC * (j + 1))
                        dst = x0[:, f] if f < 2 else (gv[:, f % 2] if f < 4 else u1[:])
                        r = raw[:, j % 2]
                        link(nc.vector.tensor_scalar(dst, r[:, 0:L], cw[:, f, 0:1], None, ALU.mult))
                        link(nc.vector.scalar_tensor_tensor(out=dst, in0=r[:, 1:L + 1], scalar=cw[:, f, 1:2], in1=dst, op0=ALU.mult, op1=ALU.add))
                        last = nc.vector.scalar_tensor_tensor(out=dst, in0=r[:, 2:L + 2], scalar=cw[:, f, 2:3], in1=dst, op0=ALU.mult, op1=ALU.add)
                        if f < 4:
                            last.then_inc(tile_ready, 1)
                        else:
                            link(last)
                            nc.vector.tensor_tensor(gv[:, f % 2], gv[:, f % 2], u1[:], ALU.mult).then_inc(tile_ready, 1)
                        if f >= 2:
                            dve.wait_ge(tile_ready, j + 1)
        dft2 = st.sb("dft2", [P, 2, 2, NL, P])
        Y = st.sb("Y", [P, 2, NL, HY_CH])
        prod = st.sb("prod", [P, 2, 2, 2 * HY_CH])
        zb = st.sb("zb", [P, 2, L])
        names = "u_ready prod_ready y_ready inv_ready z_step".split()
        u_ready, prod_ready, y_ready, inv_ready, z_step = (st.sem(n) for n in names)
        dft2_loaded = [st.sem(f"dft2_loaded{i}") for i in range(2)]
        with nc.Block() as block:
            @block.sync
            def _(sp):
                for t in range(NL):
                    wait(sp, u_ready, t - 1)
                    for i in range(2):
                        sp.dma_start(dft2[:, t % 2, i], t_dft2[i, t]).then_inc(dft2_loaded[t % 2], 16)
                for t in range(NL):
                    wait(sp, u_ready, NL)
                    wait(sp, inv_ready, t - 1)
                    for i in range(2):
                        sp.dma_start(dft2[:, t % 2, i], g.hy_rows[ctx][i, t * P:(t + 1) * P, :].rearrange("p (j n) -> p j n", n=P)).then_inc(dft2_loaded[t % 2], 16)

            @block.tensor
            def _(pe):
                for t in range(NL):
                    pe.wait_ge(dft2_loaded[t % 2], 32 * (t // 2 + 1))
                    wait(pe, prod_ready, t - 1)
                    for i in range(2):
                        for j in range(NL):
                            mm = nc.tensor.matmul(g.ps[:, t % 2, i * HY_CH:(i + 1) * HY_CH], dft2[:, t % 2, i, j, :], gT[:, j, :],
                                                  start=j == 0, stop=j == NL - 1)
                    mm.then_inc(u_ready, 1)
                for t in range(NL):
                    pe.wait_ge(dft2_loaded[t % 2], 32 * ((NL + t) // 2 + 1))
                    pe.wait_ge(y_ready, NL)
                    for ct in range(2):
                        for c in range(NC):
                            for i in range(2):
                                mm = nc.tensor.matmul(g.ps[:, 4 + 2 * ct + c, 0:CH], Y[:, i, t, ct * P:(ct + 1) * P],
                                                      dft2[:, t % 2, i].rearrange("p j n -> p (j n)")[:, c * CH:(c + 1) * CH],
                                                      start=t == 0 and i == 0, stop=t == NL - 1 and i == 1)
                    mm.then_inc(inv_ready, 1)

            @block.vector
            def _(dve):
                for t in range(NL):
                    dve.wait_ge(u_ready, t + 1)
                    wait(dve, y_ready, t - 1)
                    nc.vector.tensor_tensor(prod[:, t % 2, 0], g.ps[:, t % 2, :], Kf[:, t, 0:2 * HY_CH], ALU.mult)
                    nc.vector.tensor_tensor(prod[:, t % 2, 1], g.ps[:, t % 2, :], Kf[:, t, HY_CH:], ALU.mult).then_inc(prod_ready, 1)
                    dve.wait_ge(prod_ready, t + 1)
                    nc.vector.tensor_tensor(Y[:, 0, t], prod[:, t % 2, 0, 0:HY_CH], prod[:, t % 2, 0, HY_CH:], ALU.subtract)
                    nc.vector.tensor_tensor(Y[:, 1, t], prod[:, t % 2, 1, 0:HY_CH], prod[:, t % 2, 1, HY_CH:], ALU.add).then_inc(y_ready, 1)
                link = Chain(dve, z_step)
                for ct in range(2):
                    link(nc.vector.tensor_scalar(zb[:, ct], gv[:, ct], hb[:, ct:ct + 1], None, ALU.mult))
                dve.wait_ge(inv_ready, NL)
                for ct in range(2):
                    z = zb[:, ct].rearrange("p (c n) -> p c n", c=NC)
                    link(nc.vector.scalar_tensor_tensor(out=z, in0=g.ps[:, 4 + 2 * ct:4 + 2 * ct + NC, 0:CH], scalar=1.0 / L, in1=z,
                                                        op0=ALU.mult, op1=ALU.add))
                    link(nc.vector.tensor_tensor(g.yT[:, ct, tok0:tok0 + L], zb[:, ct], x0[:, ct], ALU.mult))


TWO_PI_PARTS = [6.28125, 2 * math.pi - 6.28125]
PI_DOWN = float(np.nextafter(np.float32(math.pi), np.float32(0)))


def project(nc, g, st, tag, load, loads, groups):
    names = "w_loaded group_ready dve_took act_took".split()
    w_loaded, group_ready, dve_took, act_took = (st.sem(f"{n}_{tag}") for n in names)
    took = (dve_took, act_took)
    with nc.Block() as block:
        @block.sync
        def _(sp):
            load(sp, w_loaded)

        @block.tensor
        def _(pe):
            pe.wait_ge(w_loaded, 16 * loads)
            for n, (products, dst, view) in enumerate(groups):
                wait(pe, took[n % 2], n // 2 - 1)
                for c0, width, lhs, rhs in products:
                    for k in range(KD):
                        mm = nc.tensor.matmul(g.ps[:, n % 4, c0:c0 + width], lhs(k), rhs(k), start=k == 0, stop=k == KD - 1)
                mm.then_inc(group_ready, 1)

        @block.vector
        def _(dve):
            for n in range(0, len(groups), 2):
                dve.wait_ge(group_ready, n + 1)
                nc.vector.tensor_copy(groups[n][1], groups[n][2](g.ps[:, n % 4, :])).then_inc(dve_took, 1)

        @block.scalar
        def _(act):
            for n in range(1, len(groups), 2):
                act.wait_ge(group_ready, n + 1)
                nc.scalar.copy(groups[n][1], groups[n][2](g.ps[:, n % 4, :])).then_inc(act_took, 1)


def feature_groups(g, dsts, lhs):
    return [([(0, n, lambda k, f=f: lhs(f, k), lambda k, c0=c0, n=n: g.hT[:, k, c0:c0 + n])],
             dst[:, c0:c0 + n], lambda bank, n=n: bank[:, 0:n])
            for f, dst in enumerate(dsts) for c0, n in CHUNKS]


def token_groups(g, dst, width, rhs):
    per = BANK // width
    out = []
    for t0 in range(0, NT, per):
        ts = range(t0, min(t0 + per, NT))
        out.append(([((t - t0) * width, width, lambda k, t=t: g.hT[:, k, t * P:(t + 1) * P], rhs) for t in ts],
                    dst[:, t0:t0 + len(ts), :],
                    lambda bank, m=len(ts): bank[:, 0:m * width].rearrange("p (t n) -> p t n", n=width)))
    return out


class Job:

    def __init__(self, q, scores, soft, values, sink=None):
        self.q, self.scores, self.soft, self.values, self.sink = q, scores, soft, values, sink
        self.cols = soft[-1][1]
        self.lo = min(4, len(values) - 1)


def attend(nc, g, st, jobs, out_tiles, scale):
    NJ = len(jobs)
    width = max(j.cols for j in jobs) + 1
    NPT = max(len(j.values) for j in jobs)
    S = st.sb("S", [P, 2, width])
    PR = st.sb("PR", [P, 2, width])
    PT = st.sb("PT", [P, 2, NPT, P])
    mx = st.sb("mx", [P, 2, 4])
    sums = st.sb("sums", [P, 2, 4])
    inv = st.sb("inv", [P, 4])
    on = st.sb("on", [P, 2, 2 * P])
    names = ("scores_ready soft_ready sink_put max_step exp_ready turned_lo turned_hi copied_lo copied_hi "
             "pv_ready inv_ready normed out_turned out_put").split()
    (scores_ready, soft_ready, sink_put, max_step, exp_ready, turned_lo, turned_hi, copied_lo, copied_hi,
     pv_ready, inv_ready, normed, out_turned, out_put) = (st.sem(n) for n in names)
    with nc.Block() as block:
        @block.tensor
        def _(pe):
            def scores(j):
                wait(pe, soft_ready, j - 1)
                for c0, k, n in jobs[j].scores:
                    bank = 2 * (j % 2) + c0 // BANK
                    mm = nc.tensor.matmul(g.ps[:, bank, c0 % BANK:c0 % BANK + n], jobs[j].q, k, start=True, stop=True)
                mm.then_inc(scores_ready, 1)

            def turn(j):
                pe.wait_ge(exp_ready, j + 1)
                wait(pe, copied_lo, j)
                wait(pe, copied_hi, j)
                lo = jobs[j].lo
                for i, (c0, n, _) in enumerate(jobs[j].values):
                    at = (i if i < lo else i - lo) * P
                    mm = nc.tensor.transpose(g.ps[0:n, 4 if i < lo else 5, at:at + P], PR[:, j % 2, c0:c0 + n], g.ident[:])
                    if i == lo - 1:
                        mm.then_inc(turned_lo, 1)
                mm.then_inc(turned_hi, 1)

            def weigh(j):
                pe.wait_ge(copied_lo, j + 1)
                pe.wait_ge(copied_hi, j + 1)
                if j % 4 == 0:
                    wait(pe, normed, j // 4)
                vals = jobs[j].values
                for i, (c0, n, v) in enumerate(vals):
                    mm = nc.tensor.matmul(g.ps[:, 6, (j % 4) * HD:(j % 4 + 1) * HD], PT[0:n, j % 2, i, :], v,
                                          start=i == 0, stop=i == len(vals) - 1)
                mm.then_inc(pv_ready, 1)
                if j % 4 == 3:
                    b = j // 4
                    pe.wait_ge(normed, b + 1)
                    wait(pe, out_put, b)
                    for i in range(2):
                        mm = nc.tensor.transpose(g.ps[:, 7, i * P:(i + 1) * P], on[:, b % 2, i * P:(i + 1) * P], g.ident[:])
                    mm.then_inc(out_turned, 1)

            scores(0)
            for j in range(NJ):
                if j + 1 < NJ:
                    scores(j + 1)
                turn(j)
                if j >= 1:
                    weigh(j - 1)
            weigh(NJ - 1)

        @block.vector
        def _(dve):
            link = Chain(dve, max_step)

            def soft(j):
                job = jobs[j]
                dve.wait_ge(scores_ready, j + 1)
                wait(dve, exp_ready, j - 1)
                if job.sink is not None:
                    nc.vector.tensor_copy(S[:, j % 2, job.cols:job.cols + 1], job.sink).then_inc(sink_put, 1)
                flat = g.ps[:, 2 * (j % 2):2 * (j % 2) + 2, :].rearrange("p b n -> p (b n)")
                for i, (a, b, addend) in enumerate(job.soft):
                    first = -3e38 if job.sink is None else job.sink
                    link(nc.vector.tensor_tensor_reduce(S[:, j % 2, a:b], flat[:, a:b], addend, scale,
                                                        mx[:, j % 2, i - 1:i] if i else first, ALU.add, ALU.max,
                                                        mx[:, j % 2, i:i + 1]))
                i = len(job.soft) - 1
                nc.vector.tensor_scalar(mx[:, j % 2, 3:4], mx[:, j % 2, i:i + 1], -1.0, None, ALU.mult).then_inc(soft_ready, 1)

            def copy(j):
                dve.wait_ge(turned_lo, j + 1)
                wait(dve, pv_ready, j - 1)
                m = jobs[j].lo
                nc.vector.tensor_copy(PT[:, j % 2, 0:m, :], g.ps[:, 4, 0:m * P].rearrange("p (i n) -> p i n", n=P)).then_inc(copied_lo, 1)

            def norm(b):
                dve.wait_ge(exp_ready, 4 * b + 4)
                wait(dve, inv_ready, b)
                nc.vector.reciprocal(inv[:], sums[:, b % 2, :]).then_inc(inv_ready, 1)
                dve.wait_ge(inv_ready, b + 1)
                dve.wait_ge(pv_ready, 4 * b + 4)
                wait(dve, out_turned, b - 1)
                nc.vector.tensor_tensor(on[:, b % 2, :].rearrange("p (h n) -> p h n", h=4),
                                        g.ps[:, 6, 0:4 * HD].rearrange("p (h n) -> p h n", h=4),
                                        inv[:].unsqueeze(2).to_broadcast([P, 4, HD]), ALU.mult).then_inc(normed, 1)

            for j in range(NJ + 1):
                if j < NJ:
                    soft(j)
                if j >= 1:
                    copy(j - 1)
                if j >= 2 and (j - 2) % 4 == 3:
                    norm((j - 2) // 4)
            norm(NJ // 4 - 1)

        @block.scalar
        def _(act):
            def exp(j):
                job = jobs[j]
                act.wait_ge(soft_ready, j + 1)
                if job.sink is not None:
                    act.wait_ge(sink_put, j + 1)
                wait(act, turned_lo, j - 1)
                wait(act, turned_hi, j - 1)
                if j % 4 == 0:
                    wait(act, inv_ready, j // 4 - 1)
                n = job.cols + (job.sink is not None)
                nc.scalar.activation(PR[:, j % 2, 0:n], S[:, j % 2, 0:n], ACT.Exp, bias=mx[:, j % 2, 3:4],
                                     accum_out=sums[:, (j // 4) % 2, j % 4:j % 4 + 1]).then_inc(exp_ready, 1)

            def copy(j):
                act.wait_ge(turned_hi, j + 1)
                wait(act, pv_ready, j - 1)
                vals = jobs[j].values
                lo, full = jobs[j].lo, sum(n == P for _, n, _ in vals)
                m = full - lo
                last = nc.scalar.copy(PT[:, j % 2, lo:full, :], g.ps[:, 5, 0:m * P].rearrange("p (i n) -> p i n", n=P)) if m else None
                if full < len(vals):
                    n = vals[-1][1]
                    last = nc.scalar.copy(PT[0:n, j % 2, full, :], g.ps[0:n, 5, m * P:(m + 1) * P])
                last.then_inc(copied_hi, 1)

            def put(b):
                f, tok = out_tiles[b]
                act.wait_ge(out_turned, b + 1)
                nc.scalar.copy(g.yT[:, f:f + 2, tok:tok + P], g.ps[:, 7, 0:2 * P].rearrange("p (f n) -> p f n", f=2)).then_inc(out_put, 1)

            for j in range(NJ):
                exp(j)
                if j >= 1:
                    copy(j - 1)
                if j >= 8 and j % 4 == 0:
                    put(j // 4 - 2)
            copy(NJ - 1)
            for b in range(max(0, (NJ - 1) // 4 - 1), NJ // 4):
                put(b)


def stage_window(nc, g, l, ctx):
    with Stage(nc, f"wa{l}") as st:
        qk = st.sb("qk", [P, 3, TOK])
        v = st.sb("v", [P, NT, P])
        mask = st.sb("mask", [P, CTX + 3 * P])
        sinks = st.sb("sinks", [P, 4])
        zero = st.sb("zero", [P, CTX])
        small_loaded = st.sem("small_loaded")
        with ExitStack() as early:
            w = early.enter_context(nc.sbuf_tensor(f"w_{st.tag}", [P, KD, WA_IN], F32))

            def load(sp, w_loaded):
                wv = g.w_in[l].rearrange("(k p) n -> p k n", p=P)[:, :, WA0:WA0 + WA_IN]
                for h in range(4):
                    to = (h % 2 * 2 + h // 2) * HD
                    sp.dma_start(w[:, :, to:to + HD], wv[:, :, h * HD:(h + 1) * HD]).then_inc(w_loaded, 16)
                sp.dma_start(w[:, :, 256:], wv[:, :, 256:]).then_inc(w_loaded, 16)
                sp.dma_start(mask[:], g.t_wa_mask).then_inc(small_loaded, 16)
                sp.dma_start(sinks[:], g.wa_sink[l].rearrange("(o n) -> o n", o=1).to_broadcast([P, 4])).then_inc(small_loaded, 16)
                sp.wait_ge(small_loaded, 32)

            project(nc, g, st, "p", load, 5,
                    feature_groups(g, [qk[:, f] for f in range(3)], lambda f, k: w[:, k, f * P:(f + 1) * P]) + token_groups(g, v, P, lambda k: w[:, k, 384:512]))
        with ExitStack() as early:
            rope = early.enter_context(nc.sbuf_tensor(f"rope_{st.tag}", [P, 2, SEQ], F32))
            rot = early.enter_context(nc.sbuf_tensor(f"rot_{st.tag}", [P, P], F32))
            tmp = early.enter_context(nc.sbuf_tensor(f"tmp_{st.tag}", [P, 2, BANK], F32))
            rope_loaded, rotated, tmp_ready, scaled, roped = (st.sem(n) for n in "rope_loaded rotated tmp_ready scaled roped".split())
            spans = [(f, c) for f in range(3) for c in range(2)]
            with nc.Block() as block:
                @block.sync
                def _(sp):
                    sp.dma_start(rope[:], g.t_rope.rearrange("i p n -> p i n")).then_inc(rope_loaded, 16)
                    sp.dma_start(rot[:], g.t_rot).then_inc(rope_loaded, 16)

                @block.gpsimd
                def _(pool):
                    pool.memset(zero[:], 0.0)

                @block.tensor
                def _(pe):
                    pe.wait_ge(rope_loaded, 32)
                    for n, (f, c) in enumerate(spans):
                        wait(pe, tmp_ready, n - 1)
                        nc.tensor.matmul(g.ps[:, n % 2, :], rot[:], qk[:, f, c * BANK:(c + 1) * BANK], start=True, stop=True).then_inc(rotated, 1)

                @block.vector
                def _(dve):
                    dve.wait_ge(rope_loaded, 32)
                    for n, (f, c) in enumerate(spans):
                        cols = slice(c * BANK, (c + 1) * BANK)
                        dve.wait_ge(rotated, n + 1)
                        wait(dve, roped, n - 1)
                        nc.vector.tensor_tensor(tmp[:, n % 2], g.ps[:, n % 2, :], rope[:, 1, cols], ALU.mult).then_inc(tmp_ready, 1)
                        nc.vector.tensor_tensor(qk[:, f, cols], qk[:, f, cols], rope[:, 0, cols], ALU.mult).then_inc(scaled, 1)
                        dve.wait_ge(tmp_ready, n + 1)
                        dve.wait_ge(scaled, n + 1)
                        nc.vector.tensor_tensor(qk[:, f, cols], qk[:, f, cols], tmp[:, n % 2], ALU.add).then_inc(roped, 1)
        jobs, outs = [], []
        for t in range(NTL + (NTC if ctx else 0)):
            for grp in range(2):
                for r in range(2):
                    half = slice(grp * HD, (grp + 1) * HD)
                    q = qk[half, r, t * P:(t + 1) * P]
                    key, dv = qk[half, 2], slice(grp * HD, (grp + 1) * HD)
                    scores = [(0, key[:, SEQ:TOK], CTX)]
                    values = [(i * P, P, v[:, NTL + i, dv]) for i in range(NTC)]
                    m0, cols = CTX, CTX
                    if t < NTL:
                        lo, hi = max(t - 1, 0), min(t + 2, NTL)
                        m0 = CTX + (lo - (t - 1)) * P
                        for i, u in enumerate(range(lo, hi)):
                            scores.append((CTX + i * P, key[:, u * P:(u + 1) * P], P))
                            values.append((CTX + i * P, P, v[:, u, dv]))
                        cols = CTX + (hi - lo) * P
                    h = 2 * grp + r
                    if m0 == CTX:
                        soft = [(0, cols, mask[:, 0:cols])] if t < NTL else [(0, CTX, zero[:])]
                    else:
                        soft = [(0, CTX, zero[:]), (CTX, cols, mask[:, m0:m0 + cols - CTX])]
                    jobs.append(Job(q, scores, soft, values, sinks[:, h:h + 1]))
            outs.append((2, t * P))
        attend(nc, g, st, jobs, outs, SCALE)


def stage_neighbour(nc, g, l, ctx):
    NR = 2 * NA_KR - 1
    NB = 2 * NA_KR
    with Stage(nc, f"na{l}") as st:
        qk = st.sb("qk", [P, 4, TOK])
        v = st.sb("v", [P, NT, 2 * P])
        bias = st.sb("bias", [P, 4, NB, GRID_W])
        inner = st.sb("inner", [P, 4, NA_KR + 1, GRID_W])
        zero = st.sb("zero", [P, CTX])
        with ExitStack() as early:
            sel = early.enter_context(nc.sbuf_tensor(f"sel_{st.tag}", [32, GRID_W * P], F32))
            rpb = early.enter_context(nc.sbuf_tensor(f"rpb_{st.tag}", [4 * NR, 2 * NA_KC - 1], F32))
            rpbT = early.enter_context(nc.sbuf_tensor(f"rpbT_{st.tag}", [32, 4 * NR], F32))
            names = "sel_loaded rpb_turned rpb_filled rpb_ready bias_ready bias_taken cleared copied".split()
            sel_loaded, rpb_turned, rpb_filled, rpb_ready, bias_ready, bias_taken, cleared, copied = (st.sem(n) for n in names)
            with nc.Block() as block:
                @block.sync
                def _(sp):
                    sp.dma_start(rpb[:], g.na_rpb[l].rearrange("h r c -> (h r) c")).then_inc(sel_loaded, 16)
                    sp.dma_start(sel[:], g.t_na_sel).then_inc(sel_loaded, 16)

                @block.gpsimd
                def _(pool):
                    pool.memset(zero[:], 0.0).then_inc(cleared, 1)
                    pool.memset(rpbT[:], NEG).then_inc(rpb_filled, 1)

                @block.tensor
                def _(pe):
                    pe.wait_ge(sel_loaded, 32)
                    nc.tensor.transpose(g.ps[0:31, 4, 0:4 * NR], rpb[:], g.ident[0:4 * NR, 0:4 * NR]).then_inc(rpb_turned, 1)
                    pe.wait_ge(rpb_ready, 1)
                    for n in range(8):
                        wait(pe, bias_taken, n - 1)
                        for i in range(8):
                            ck = 8 * n + i
                            mm = nc.tensor.matmul(g.ps[:, n % 2, i * 4 * NR:(i + 1) * 4 * NR], sel[:, ck * P:(ck + 1) * P], rpbT[:],
                                                  start=True, stop=True)
                        mm.then_inc(bias_ready, 1)

                @block.vector
                def _(dve):
                    dve.wait_ge(rpb_filled, 1)
                    dve.wait_ge(rpb_turned, 1)
                    nc.vector.tensor_scalar(rpbT[0:31, :], g.ps[0:31, 4, 0:4 * NR], 1.0 / SCALE, None, ALU.mult).then_inc(rpb_ready, 1)
                    for n in range(8):
                        dve.wait_ge(bias_ready, n + 1)
                        for rr in range(2):
                            half = slice(rr * HD, (rr + 1) * HD)
                            for h in range(4):
                                src = g.ps[half, n % 2, 0:32 * NR].rearrange("p (c h r) -> p h r c", h=4, r=NR)[:, h]
                                last = nc.vector.tensor_copy(bias[half, h, rr:rr + NR, 8 * n:8 * n + 8], src)
                        last.then_inc(bias_taken, 1)
                    dve.wait_ge(bias_taken, 8)
                    for rr in range(2):
                        half = slice(rr * HD, (rr + 1) * HD)
                        nc.vector.tensor_copy(inner[half, :, rr:rr + NA_KR, :], bias[half, :, 3 + rr:3 + rr + NA_KR, :])
                        edge = NA_KR if rr == 0 else 0
                        last = nc.vector.memset(inner[half, :, edge:edge + 1, :], NEG)
        with ExitStack() as early:
            w = early.enter_context(nc.sbuf_tensor(f"w_{st.tag}", [P, KD, NA_IN], F32))

            def load(sp, w_loaded):
                sp.dma_start(w[:], g.w_in[l].rearrange("(k p) n -> p k n", p=P)[:, :, NA0:NA0 + NA_IN]).then_inc(w_loaded, 16)

            project(nc, g, st, "p", load, 1,
                    feature_groups(g, [qk[:, f] for f in range(4)], lambda f, k: w[:, k, f * P:(f + 1) * P])
                    + token_groups(g, v, 2 * P, lambda k: w[:, k, 512:768]))
        jobs, outs = [], []
        for t in range(NTL + (NTC if ctx else 0)):
            for h in range(4):
                half = slice(h % 2 * HD, (h % 2 + 1) * HD)
                dv = slice(h * HD, (h + 1) * HD)
                q = qk[half, h // 2, t * P:(t + 1) * P]
                key = qk[half, 2 + h // 2]
                scores = [(0, key[:, SEQ:TOK], CTX)]
                values = [(i * P, P, v[:, NTL + i, dv]) for i in range(NTC)]
                soft = [(0, CTX, zero[:])]
                if t < NTL:
                    first = min(max(2 * t - NA_KR // 2, 0), SEQ // GRID_W - NA_KR)
                    last = min(max(2 * t + 1 - NA_KR // 2, 0), SEQ // GRID_W - NA_KR)
                    rows = last - first + NA_KR
                    k0, n = first * GRID_W, rows * GRID_W
                    scores += [(CTX, key[:, k0:k0 + CTX], CTX), (BANK, key[:, k0 + CTX:k0 + n], n - CTX)]
                    for i in range(0, n, P):
                        m = min(P, n - i)
                        values.append((CTX + i, m, v[0:m, (k0 + i) // P, dv]))
                    b = first - 2 * t + NA_KR - 1
                    table = inner[:, h] if rows > NA_KR else bias[:, h, b:b + NA_KR, :]
                    soft.append((CTX, CTX + n, table.rearrange("p r c -> p (r c)")))
                jobs.append(Job(q, scores, soft, values))
            outs.append((4, t * P))
        attend(nc, g, st, jobs, outs, SCALE)


def stage_gdn(nc, g, l):
    C = 64
    FW = 4 * C
    GV = 7
    SEG = SEQ + 3
    with Stage(nc, f"gd{l}") as st:
        qkv = st.sb("qkv", [P, NT, 3 * GW])
        gate = st.sb("gate", [P, NT, GW])
        ab = st.sb("ab", [P, NT, 16])
        with ExitStack() as early:
            def sb(name, shape):
                return early.enter_context(nc.sbuf_tensor(f"{name}_{st.tag}", shape, F32))
            w = sb("w", [P, 2, KD, P])
            wg = sb("wg", [P, KD, GW + 16])
            raw = sb("raw", [P, 2, SEG + CTX + 3])
            u = sb("u", [P, TOK])
            s = sb("s", [P, 2, TOK])
            cw = sb("cw", [P, 6, 4])
            names = "cw_loaded wg_loaded padded proj_ready proj_taken conv_ready silu_ready turned tm_dve tm_act gate_ready gate_taken ab_ready ab_taken conv_step".split()
            (cw_loaded, wg_loaded, padded, proj_ready, proj_taken, conv_ready, silu_ready, turned, tm_dve, tm_act, gate_ready,
             gate_taken, ab_ready, ab_taken, conv_step) = (st.sem(n) for n in names)
            w_loaded = [st.sem(f"w_loaded{i}") for i in range(2)]
            wv = g.w_in[l].rearrange("(k p) n -> p k n", p=P)
            starts = [(2, 0, SEQ), (SEG + 2, SEQ, CTX)]
            TS = [(0, 4), (4, 8), (8, 10)]
            with nc.Block() as block:
                @block.sync
                def _(sp):
                    with nc.allow_non_contiguous_dma("filter taps, once a layer"):
                        for i in range(4):
                            sp.dma_start(cw[:, :, i], g.gdn_conv[l, i].rearrange("(f p) -> p f", p=P)).then_inc(cw_loaded, 16)
                    for f in range(6):
                        wait(sp, proj_ready, 3 * (f - 1))
                        sp.dma_start(w[:, f % 2], wv[:, :, GD0 + f * P:GD0 + (f + 1) * P]).then_inc(w_loaded[f % 2], 16)
                    sp.dma_start(wg[:], wv[:, :, GD0 + 3 * GW:]).then_inc(wg_loaded, 16)

                @block.gpsimd
                def _(pool):
                    pool.memset(raw[:, :, 0:2], 0.0)
                    pool.memset(raw[:, :, SEQ + 2:SEQ + 5], 0.0)
                    pool.memset(raw[:, :, SEG + CTX + 2:SEG + CTX + 3], 0.0).then_inc(padded, 1)

                @block.tensor
                def _(pe):
                    def project_tile(f):
                        pe.wait_ge(w_loaded[f % 2], 16 * (f // 2 + 1))
                        for i, (c0, n) in enumerate(CHUNKS):
                            m = 3 * f + i
                            wait(pe, proj_taken, m - 1)
                            for k in range(KD):
                                mm = nc.tensor.matmul(g.ps[:, m % 2, 0:n], w[:, f % 2, k, :], g.hT[:, k, c0:c0 + n],
                                                      start=k == 0, stop=k == KD - 1)
                            mm.then_inc(proj_ready, 1)

                    def turn_tile(f):
                        pe.wait_ge(silu_ready, f + 1)
                        wait(pe, tm_dve, 2 * f)
                        wait(pe, tm_act, f)
                        for i, (t0, t1) in enumerate(TS):
                            for t in range(t0, t1):
                                mm = nc.tensor.transpose(g.ps[:, 2 + i, (t - t0) * P:(t - t0 + 1) * P],
                                                         s[:, f % 2, t * P:(t + 1) * P], g.ident[:])
                        mm.then_inc(turned, 1)

                    for f in range(6):
                        project_tile(f)
                        if f >= 1:
                            turn_tile(f - 1)
                    turn_tile(5)
                    pe.wait_ge(wg_loaded, 16)
                    for t in range(NT):
                        for k in range(KD):
                            mm = nc.tensor.matmul(g.ps[:, 7, t * 16:(t + 1) * 16], g.hT[:, k, t * P:(t + 1) * P],
                                                  wg[:, k, GW:GW + 16], start=k == 0, stop=k == KD - 1)
                    mm.then_inc(ab_ready, 1)
                    for t in range(NT):
                        wait(pe, gate_taken, t - 1)
                        for k in range(KD):
                            mm = nc.tensor.matmul(g.ps[:, 5 + t % 2, 0:GW], g.hT[:, k, t * P:(t + 1) * P],
                                                  wg[:, k, 0:GW], start=k == 0, stop=k == KD - 1)
                        mm.then_inc(gate_ready, 1)

                @block.scalar
                def _(act):
                    def take(f):
                        wait(act, conv_ready, f - 1)
                        for i, (c0, n) in enumerate(CHUNKS):
                            at = c0 + 2 if c0 < SEQ else SEG + 2
                            act.wait_ge(proj_ready, 3 * f + i + 1)
                            nc.scalar.copy(raw[:, f % 2, at:at + n], g.ps[:, (3 * f + i) % 2, 0:n]).then_inc(proj_taken, 1)

                    def silu(f):
                        act.wait_ge(conv_ready, f + 1)
                        wait(act, turned, f - 1)
                        nc.scalar.activation(s[:, f % 2], u[:], ACT.Silu).then_inc(silu_ready, 1)

                    def place(f):
                        act.wait_ge(turned, f + 1)
                        nc.scalar.copy(qkv[:, 8:10, f * P:(f + 1) * P], g.ps[:, 4, 0:2 * P].rearrange("p (t n) -> p t n", n=P)).then_inc(tm_act, 1)

                    for f in range(6):
                        take(f)
                        if f >= 1:
                            silu(f - 1)
                        if f >= 2:
                            place(f - 2)
                    silu(5)
                    place(4)
                    place(5)
                    for t in range(NT):
                        act.wait_ge(gate_ready, t + 1)
                        nc.scalar.activation(gate[:, t, :], g.ps[:, 5 + t % 2, 0:GW], ACT.Silu).then_inc(gate_taken, 1)

                @block.vector
                def _(dve):
                    link = Chain(dve, conv_step)

                    def conv(f):
                        dve.wait_ge(proj_taken, 3 * f + 3)
                        wait(dve, silu_ready, f)
                        for tap in range(4):
                            for a, c0, n in starts:
                                r = raw[:, f % 2, a - 2 + tap:a - 2 + tap + n]
                                dst = u[:, c0:c0 + n]
                                if tap == 0:
                                    o = nc.vector.tensor_scalar(dst, r, cw[:, f, 0:1], None, ALU.mult)
                                else:
                                    o = nc.vector.scalar_tensor_tensor(out=dst, in0=r, scalar=cw[:, f, tap:tap + 1], in1=dst, op0=ALU.mult, op1=ALU.add)
                                if tap < 3:
                                    link(o)
                        o.then_inc(conv_ready, 1)

                    def place(f):
                        dve.wait_ge(turned, f + 1)
                        for i in range(2):
                            nc.vector.tensor_copy(qkv[:, 4 * i:4 * i + 4, f * P:(f + 1) * P],
                                                  g.ps[:, 2 + i, :].rearrange("p (t n) -> p t n", n=P)).then_inc(tm_dve, 1)

                    dve.wait_ge(padded, 1)
                    dve.wait_ge(cw_loaded, 64)
                    for f in range(6):
                        conv(f)
                        if f >= 2:
                            place(f - 2)
                    place(4)
                    place(5)
                    dve.wait_ge(ab_ready, 1)
                    nc.vector.tensor_copy(ab[:], g.ps[:, 7, 0:NT * 16].rearrange("p (t n) -> p t n", n=16)).then_inc(ab_taken, 1)
        scal = st.sb("scal", [P, NT, 2, GV, 4])
        o_sum = st.sb("o_sum", [P, NT, GW])
        M = {n: st.sb(n, [P] + s) for n, s in g.gdn_masks.items()}
        with ExitStack() as early:
            def sb(name, shape):
                return early.enter_context(nc.sbuf_tensor(f"{name}_{st.tag}", shape, F32))
            cum = sb("cum", [P, 3, P])
            sq = sb("sq", [P, 2, 2 * GW])
            nrm = sb("nrm", [P, NT, 8])
            al = sb("al", [P, 2, 8])
            xs = sb("xs", [P, NT, 8])
            ax = sb("ax", [P, NT, 8])
            names = "masks_loaded al_loaded a_ready al_exp soft_in soft_exp soft_ln ln_in g_ready sums_ready sums_copied decay_ready root_in root_ready l2_step gate_step cleared".split()
            (masks_loaded, al_loaded, a_ready, al_exp, soft_in, soft_exp, soft_ln, ln_in, g_ready, sums_ready, sums_copied, decay_ready,
             root_in, root_ready, l2_step, gate_step, cleared) = (st.sem(n) for n in names)
            with nc.Block() as block:
                @block.sync
                def _(sp):
                    for n in M:
                        sp.dma_start(M[n][:], g.tables[f"t_{n}"]).then_inc(masks_loaded, 16)
                    sp.dma_start(cum[:], g.tables["t_gd_cum"]).then_inc(masks_loaded, 16)
                    for i, src in enumerate((g.gdn_a_log, g.gdn_dt_bias)):
                        sp.dma_start(al[:, i], src[l].rearrange("(o d) h -> o (d h)", o=1).to_broadcast([P, 8])).then_inc(al_loaded, 16)
                    sp.wait_ge(masks_loaded, 16 * (len(M) + 1))

                @block.gpsimd
                def _(pool):
                    pool.memset(o_sum[:], 0.0)

                @block.tensor
                def _(pe):
                    pe.wait_ge(masks_loaded, 16 * (len(M) + 1))
                    pe.wait_ge(g_ready, 1)
                    for d in range(2):
                        gd = scal[:, :, d, 0, :]
                        nc.tensor.matmul(g.ps[:, 0, d * 40:d * 40 + 40], cum[:, d, :], gd, start=True, stop=True)
                        mm = nc.tensor.matmul(g.ps[:, 0, 80 + d * 40:120 + d * 40], cum[:, 2, :], gd, start=True, stop=True)
                    mm.then_inc(sums_ready, 1)

                @block.scalar
                def _(act):
                    act.wait_ge(al_loaded, 32)
                    nc.scalar.activation(al[:, 0], al[:, 0], ACT.Exp).then_inc(al_exp, 1)
                    act.wait_ge(soft_in, 1)
                    nc.scalar.activation(ax[:], ax[:], ACT.Exp).then_inc(soft_exp, 1)
                    nc.scalar.activation(ab[:, :, 8:16], ab[:, :, 8:16], ACT.Exp, scale=-1.0).then_inc(soft_exp, 1)
                    act.wait_ge(ln_in, 1)
                    nc.scalar.activation(ax[:], ax[:], ACT.Ln).then_inc(soft_ln, 1)
                    act.wait_ge(decay_ready, 1)
                    for v in (3, 4, 6):
                        nc.scalar.activation(scal[:, :, :, v, :], scal[:, :, :, v, :], ACT.Exp).then_inc(decay_ready, 1)
                    act.wait_ge(root_in, 1)
                    nc.scalar.activation(nrm[:], nrm[:], ACT.Sqrt).then_inc(root_ready, 1)

                @block.vector
                def _(dve):
                    link = Chain(dve, gate_step)
                    dve.wait_ge(al_loaded, 32)
                    link(nc.vector.tensor_tensor(xs[:], ab[:, :, 0:8], al[:, 1:2, :].to_broadcast([P, NT, 8]), ALU.add))
                    link(nc.vector.tensor_scalar(ax[:], xs[:], -1.0, None, ALU.mult))
                    nc.vector.tensor_tensor(ax[:], ax[:], xs[:], ALU.min).then_inc(soft_in, 1)
                    for t in range(NT):
                        nc.vector.tensor_tensor(sq[:, t % 2], qkv[:, t, 0:2 * GW], qkv[:, t, 0:2 * GW], ALU.mult).then_inc(l2_step, 1)
                        dve.wait_ge(l2_step, t + 1)
                        last = nc.vector.tensor_reduce(nrm[:, t, :], sq[:, t % 2].rearrange("p (h n) -> p h n", h=8), AX.X, ALU.add)
                    link(last)
                    nc.vector.tensor_scalar(nrm[:], nrm[:], EPS, None, ALU.add).then_inc(root_in, 1)
                    dve.wait_ge(soft_exp, 2)
                    nc.vector.tensor_scalar(ax[:], ax[:], 1.0, None, ALU.add).then_inc(ln_in, 1)
                    link(nc.vector.tensor_scalar(ab[:, :, 8:16], ab[:, :, 8:16], 1.0, None, ALU.add))
                    for d in range(2):
                        link(nc.vector.reciprocal(scal[:, :, d, 1, :], ab[:, :, 8 + 4 * d:12 + 4 * d]))
                    link(nc.vector.tensor_scalar(xs[:], xs[:], 0.0, None, ALU.max))
                    dve.wait_ge(soft_ln, 1)
                    dve.wait_ge(al_exp, 1)
                    link(nc.vector.tensor_tensor(xs[:], xs[:], ax[:], ALU.add))
                    for d in range(2):
                        o = nc.vector.scalar_tensor_tensor(out=scal[:, :, d, 0, :], in0=xs[:, :, 4 * d:4 * d + 4], scalar=-1.0,
                                                           in1=al[:, 0:1, 4 * d:4 * d + 4].to_broadcast([P, NT, 4]), op0=ALU.mult, op1=ALU.mult)
                    o.then_inc(g_ready, 1)
                    dve.wait_ge(sums_ready, 1)
                    for d in range(2):
                        gc = g.ps[:, 0, d * 40:d * 40 + 40].rearrange("p (t h) -> p t h", h=4)
                        tot = g.ps[:, 0, 80 + d * 40:120 + d * 40].rearrange("p (t h) -> p t h", h=4)
                        link(nc.vector.tensor_copy(scal[:, :, d, 2, :], gc))
                        nc.vector.tensor_copy(scal[:, :, d, 3, :], gc)
                        link(nc.vector.tensor_copy(scal[:, :, d, 6, :], tot))
                        link(nc.vector.tensor_tensor(scal[:, :, d, 4, :], scal[:, :, d, 6, :], scal[:, :, d, 2, :], ALU.subtract))
                    nc.vector.tensor_copy(al[:, 1, 0:1], al[:, 1, 1:2]).then_inc(decay_ready, 1)
                    dve.wait_ge(decay_ready, 4)
                    link(nc.vector.tensor_tensor(scal[:, :, :, 5, :], scal[:, :, :, 3, :], scal[:, :, :, 1, :], ALU.mult))
                    dve.wait_ge(root_ready, 1)
                    link(nc.vector.reciprocal(nrm[:], nrm[:]))
                    link(nc.vector.tensor_scalar(nrm[:, :, 0:4], nrm[:, :, 0:4], SCALE, None, ALU.mult))
                    for t in range(NT):
                        x = qkv[:, t, 0:2 * GW].rearrange("p (h n) -> p h n", h=8)
                        nc.vector.tensor_tensor(x, x, nrm[:, t, :].unsqueeze(2).to_broadcast([P, 8, C]), ALU.mult)
        gdn_steps(nc, g, st, qkv, scal, o_sum, M)
        sqo = st.sb("sqo", [P, 2, GW])
        no = st.sb("no", [P, NT, 4])
        ng = st.sb("ng", [P, C])
        names = "ng_loaded root_in2 root_ready2 fin_step tile_ready out_turned out_put sq_step".split()
        ng_loaded, root_in2, root_ready2, fin_step, tile_ready, out_turned, out_put, sq_step = (st.sem(n) for n in names)
        with nc.Block() as block:
            @block.sync
            def _(sp):
                sp.dma_start(ng[:], g.gdn_norm[l].rearrange("(o n) -> o n", o=1).to_broadcast([P, C])).then_inc(ng_loaded, 16)

            @block.vector
            def _(dve):
                link = Chain(dve, fin_step)
                for t in range(NT):
                    nc.vector.tensor_tensor(sqo[:, t % 2], o_sum[:, t, :], o_sum[:, t, :], ALU.mult).then_inc(sq_step, 1)
                    dve.wait_ge(sq_step, t + 1)
                    last = nc.vector.tensor_reduce(no[:, t, :], sqo[:, t % 2].rearrange("p (h n) -> p h n", h=4), AX.X, ALU.add)
                link(last)
                nc.vector.tensor_scalar(no[:], no[:], 1.0 / C, EPS, ALU.mult, ALU.add).then_inc(root_in2, 1)
                dve.wait_ge(ng_loaded, 16)
                for t in range(NT):
                    x = gate[:, t, :].rearrange("p (h n) -> p h n", h=4)
                    last = nc.vector.tensor_tensor(x, x, ng[:].unsqueeze(1).to_broadcast([P, 4, C]), ALU.mult)
                link(last)
                dve.wait_ge(root_ready2, 1)
                link(nc.vector.reciprocal(no[:], no[:]))
                for t in range(NT):
                    x = o_sum[:, t, :].rearrange("p (h n) -> p h n", h=4)
                    link(nc.vector.tensor_tensor(x, x, no[:, t, :].unsqueeze(2).to_broadcast([P, 4, C]), ALU.mult))
                    nc.vector.tensor_tensor(o_sum[:, t, :], o_sum[:, t, :], gate[:, t, :], ALU.mult).then_inc(tile_ready, 1)

            @block.scalar
            def _(act):
                act.wait_ge(root_in2, 1)
                nc.scalar.activation(no[:], no[:], ACT.Sqrt).then_inc(root_ready2, 1)
                for t in range(NT):
                    act.wait_ge(out_turned, t + 1)
                    nc.scalar.copy(g.yT[:, 6:8, t * P:(t + 1) * P], g.ps[:, t % 2, 0:2 * P].rearrange("p (f n) -> p f n", f=2)).then_inc(out_put, 1)

            @block.tensor
            def _(pe):
                for t in range(NT):
                    pe.wait_ge(tile_ready, t + 1)
                    wait(pe, out_put, t - 1)
                    for i in range(2):
                        mm = nc.tensor.transpose(g.ps[:, t % 2, i * P:(i + 1) * P], o_sum[:, t, i * P:(i + 1) * P], g.ident[:])
                    mm.then_inc(out_turned, 1)


def gdn_steps(nc, g, st, qkv, scal, o_sum, M):
    C, FW, W2 = 64, 256, 512
    LEVELS = 5
    RS = [slice(0, C), slice(C, P)]

    def sb(name, shape=(2, 4, C)):
        return st.sb(name, [P] + list(shape))

    x3 = st.sb("x3", [P, 2, 3 * FW])
    sc = st.sb("sc", [P, 2, 7, 4])
    glz = st.sb("glz", [P, 2, 4])
    DG, E, kT, qT, L, At, LT, AtT, T, TT, X, tmp, vb, kbe, kd, qd, U, wT, qdT = (
        sb(n) for n in "DG E kT qT L At LT AtT T TT X tmp vb kbe kd qd U wT qdT".split())
    S = st.sb("S", [P, 4, C])
    Sg = st.sb("Sg", [P, 4, C])
    un = st.sb("un", [P, 4, C])
    names = ("gathered scaled dg_ready gj_ready e_in e_ready kt_turned kt_ready qt_turned qt_ready gram_ready qk_ready l_ready at_ready "
             "lt_turned lt_ready att_turned att_ready t_ready x_prod x_ready txt_prod tx_prod t_next u_prod w_prod qd_prod u_ready "
             "wq_ready ws_prod un_ready s_prod s_ready o_prod o_taken waits_met vec_step").split()
    (gathered, scaled, dg_ready, gj_ready, e_in, e_ready, kt_turned, kt_ready, qt_turned, qt_ready, gram_ready, qk_ready, l_ready, at_ready,
     lt_turned, lt_ready, att_turned, att_ready, t_ready, x_prod, x_ready, txt_prod, tx_prod, t_next, u_prod, w_prod, qd_prod, u_ready,
     wq_ready, ws_prod, un_ready, s_prod, s_ready, o_prod, o_taken, waits_met, vec_step) = (st.sem(n) for n in names)

    def all_steps(eng, body):
        body(0, NTL, NTL + 1)
        body(1, NTL + 1, NTL)
        with eng.Fori(0, NTL) as i:
            body(i + 2, i, NTL - 1 - i)

    def dhc():
        return [(d, h, c) for d in range(2) for h in range(4) for c in range(2)]

    ps = g.ps

    def bank(b):
        return ps[:, b, :].rearrange("p (d h n) -> p d h n", d=2, h=4)

    def per_head(a, v):
        return a[:, :, v, :].unsqueeze(3).to_broadcast([P, 2, 4, C])

    def mask(m):
        return m.unsqueeze(2).to_broadcast([P, 2, 4, C])

    with nc.Block() as block:
        @block.tensor
        def _(pe):
            def wait_step(sem, value):
                pe.wait_ge(sem, value)
                pe.sem_inc(waits_met, 1)

            def body(s, a, b):
                def mms(bk, lhs, rhs, z=False, start=True, stop=True):
                    for d, h, c in dhc():
                        col = (d ^ c if z else d) * FW + h * C
                        mm = nc.tensor.matmul(ps[RS[c], bk, col:col + C], lhs(d, h, c), rhs(d, h, c), start=start, stop=stop)
                    return mm

                pe.wait_ge(dg_ready, s + 1)
                nc.tensor.matmul(ps[:, 0, :], M["gd_negblk"][:], DG[:].rearrange("p d h n -> p (d h n)"), start=True, stop=True).then_inc(gj_ready, 1)
                wait_step(gathered, 4 * s + 4)
                eye = lambda d, h, c: M["gd_eye"][RS[c], :]
                mms(1, lambda d, h, c: x3[RS[c], d, FW + h * C:FW + (h + 1) * C], eye).then_inc(kt_turned, 1)
                mms(2, lambda d, h, c: x3[RS[c], d, h * C:(h + 1) * C], eye).then_inc(qt_turned, 1)
                wait_step(kt_ready, s + 1)
                mms(3, lambda d, h, c: kT[RS[c], d, h, :], lambda d, h, c: kT[RS[c], d, h, :]).then_inc(gram_ready, 1)
                wait_step(qt_ready, s + 1)
                mms(4, lambda d, h, c: qT[RS[c], d, h, :], lambda d, h, c: kT[RS[c], d, h, :]).then_inc(qk_ready, 1)
                wait_step(l_ready, s + 1)
                mms(5, lambda d, h, c: L[RS[c], d, h, :], eye).then_inc(lt_turned, 1)
                wait_step(at_ready, s + 1)
                mms(6, lambda d, h, c: At[RS[c], d, h, :], eye, z=True).then_inc(att_turned, 1)
                wait_step(scaled, s + 1)
                mms(7, lambda d, h, c: qd[RS[c], d, h, :], eye, z=True).then_inc(qd_prod, 1)
                for lv in range(LEVELS):
                    wait_step(t_next, s * LEVELS + lv + 1)
                    mms(0, lambda d, h, c: LT[RS[c], d, h, :], lambda d, h, c: T[RS[c], d, h, :]).then_inc(x_prod, 1)
                    wait_step(x_ready, s * LEVELS + lv + 1)
                    mms(1, lambda d, h, c: X[RS[c], d, h, :], lambda d, h, c: TT[RS[c], d, h, :]).then_inc(txt_prod, 1)
                    if lv < LEVELS - 1:
                        mms(2, lambda d, h, c: TT[RS[c], d, h, :], lambda d, h, c: X[RS[c], d, h, :]).then_inc(tx_prod, 1)
                wait_step(t_ready, s + 1)
                mms(3, lambda d, h, c: TT[RS[c], d, h, :], lambda d, h, c: vb[RS[c], d, h, :], z=True).then_inc(u_prod, 1)
                mms(4, lambda d, h, c: kbe[RS[c], d, h, :], lambda d, h, c: TT[RS[c], d, h, :], z=True).then_inc(w_prod, 1)
                wait_step(wq_ready, 2 * s + 2)
                for z in range(2):
                    wait_step(s_ready, 2 * s + z + 1)
                    for h in range(4):
                        for c in range(2):
                            mm = nc.tensor.matmul(ps[RS[c], 0, h * C:(h + 1) * C], wT[RS[c], z, h, :], S[RS[c], h, :], start=True, stop=True)
                    mm.then_inc(ws_prod, 1)
                    wait_step(un_ready, 2 * s + z + 1)
                    for h in range(4):
                        for c in range(2):
                            d = z ^ c
                            mm = nc.tensor.matmul(ps[RS[1 - c], 1, h * C:(h + 1) * C], kd[RS[c], d, h, :], un[RS[c], h, :], start=True, stop=True)
                    mm.then_inc(s_prod, 1)
                    for h in range(4):
                        for c in range(2):
                            col = z * FW + h * C
                            nc.tensor.matmul(ps[RS[c], 2, col:col + C], qdT[RS[c], z, h, :], S[RS[c], h, :], start=True, stop=False)
                            mm = nc.tensor.matmul(ps[RS[c], 2, col:col + C], AtT[RS[c], z, h, :], un[RS[c], h, :], start=False, stop=True)
                    mm.then_inc(o_prod, 1)

            all_steps(pe, body)

        @block.gpsimd
        def _(pool):
            pool.memset(S[:], 0.0).then_inc(s_ready, 1)

            def body(s, a, b):
                pool.wait_ge(gathered, 4 * s + 4)
                wait(pool, o_taken, s)
                q, k, v = (x3[:, :, i * FW:(i + 1) * FW].rearrange("p d (h n) -> p d h n", h=4) for i in range(3))
                nc.gpsimd.tensor_tensor(qd[:], q, per_head(sc, 3), ALU.mult)
                nc.gpsimd.tensor_tensor(vb[:], v, per_head(sc, 1), ALU.mult)
                nc.gpsimd.tensor_tensor(kbe[:], k, per_head(sc, 5), ALU.mult)
                nc.gpsimd.tensor_tensor(kd[:], k, per_head(sc, 4), ALU.mult).then_inc(scaled, 1)

            all_steps(pool, body)

        @block.scalar
        def _(act):
            def body(s, a, b):
                wait(act, o_taken, s)
                wait(act, scaled, s)
                for d, t in ((0, a), (1, b)):
                    nc.scalar.copy(x3[:, d, :], qkv[:, t, :] if isinstance(t, int) else qkv[:, bass.ds(t, 1), :].rearrange("p o n -> p (o n)")).then_inc(gathered, 1)
                    nc.scalar.copy(sc[:, d], scal[:, t, d] if isinstance(t, int) else scal[:, bass.ds(t, 1), d].rearrange("p o v h -> p (o v) h")).then_inc(gathered, 1)
                act.wait_ge(kt_turned, s + 1)
                nc.scalar.copy(kT[:], bank(1)).then_inc(kt_ready, 1)
                act.wait_ge(e_in, s + 1)
                nc.scalar.activation(E[:], E[:], ACT.Exp).then_inc(e_ready, 1)
                act.wait_ge(att_turned, s + 1)
                nc.scalar.copy(AtT[:], bank(6)).then_inc(att_ready, 1)
                act.wait_ge(qd_prod, s + 1)
                nc.scalar.copy(qdT[:], bank(7)).then_inc(wq_ready, 1)
                act.wait_ge(w_prod, s + 1)
                nc.scalar.copy(wT[:], bank(4)).then_inc(wq_ready, 1)

            all_steps(act, body)

        @block.vector
        def _(dve):
            def body(s, a, b):
                V = nc.vector
                n = [0]
                PER = 13

                def link(ins):
                    n[0] += 1
                    ins.then_inc(vec_step, 1)
                    dve.wait_ge(vec_step, s * PER + n[0])

                dve.wait_ge(gathered, 4 * s + 4)
                V.tensor_tensor(DG[:], mask(M["gd_tri"][:]), per_head(sc, 0), ALU.mult).then_inc(dg_ready, 1)
                for c in range(2):
                    for d in range(2):
                        z = c ^ d
                        V.tensor_copy(glz[RS[c], z, :], sc[RS[c], d, 6, :])
                dve.wait_ge(gj_ready, s + 1)
                link(V.tensor_tensor(E[:], bank(0), per_head(sc, 2), ALU.add))
                V.tensor_tensor(E[:], E[:], mask(M["gd_allow"][:]), ALU.min).then_inc(e_in, 1)
                dve.wait_ge(qt_turned, s + 1)
                V.tensor_copy(qT[:], bank(2)).then_inc(qt_ready, 1)
                dve.wait_ge(e_ready, s + 1)
                link(V.tensor_tensor(tmp[:], E[:], per_head(sc, 1), ALU.mult))
                link(V.tensor_tensor(tmp[:], tmp[:], mask(M["gd_strict"][:]), ALU.mult))
                dve.wait_ge(gram_ready, s + 1)
                V.tensor_tensor(L[:], tmp[:], bank(3), ALU.mult).then_inc(l_ready, 1)
                dve.wait_ge(qk_ready, s + 1)
                V.tensor_tensor(At[:], E[:], bank(4), ALU.mult).then_inc(at_ready, 1)
                eye = M["gd_eye"][:].unsqueeze(1).unsqueeze(1).to_broadcast([P, 2, 4, C])
                dve.wait_ge(l_ready, s + 1)
                link(V.tensor_tensor(T[:], L[:], mask(M["gd_lvl"][:, 0]), ALU.mult))
                link(V.tensor_tensor(T[:], eye, T[:], ALU.subtract))
                dve.wait_ge(lt_turned, s + 1)
                link(V.tensor_copy(LT[:], bank(5)))
                link(V.tensor_tensor(TT[:], LT[:], mask(M["gd_lvl"][:, 1]), ALU.mult))
                V.tensor_tensor(TT[:], eye, TT[:], ALU.subtract).then_inc(t_next, 1)
                for lv in range(LEVELS):
                    dve.wait_ge(x_prod, s * LEVELS + lv + 1)
                    V.tensor_tensor(X[:], bank(0), mask(M["gd_lvl"][:, lv + 2]), ALU.mult).then_inc(x_ready, 1)
                    dve.wait_ge(txt_prod, s * LEVELS + lv + 1)
                    dve.wait_ge(t_next, s * LEVELS + lv + 1)
                    if lv == LEVELS - 1:
                        V.tensor_tensor(TT[:], TT[:], bank(1), ALU.subtract).then_inc(t_ready, 1)
                        continue
                    dve.wait_ge(tx_prod, s * (LEVELS - 1) + lv + 1)
                    link(V.tensor_tensor(TT[:], TT[:], bank(1), ALU.subtract))
                    V.tensor_tensor(T[:], T[:], bank(2), ALU.subtract).then_inc(t_next, 1)
                dve.wait_ge(u_prod, s + 1)
                V.tensor_copy(U[:], bank(3)).then_inc(u_ready, 1)
                dve.wait_ge(u_ready, s + 1)
                for z in range(2):
                    dve.wait_ge(s_ready, 2 * s + z + 1)
                    for c in range(2):
                        last = V.tensor_tensor(Sg[RS[1 - c], :, :], S[RS[c], :, :], glz[RS[c], z, :].unsqueeze(2).to_broadcast([C, 4, C]), ALU.mult)
                    link(last)
                    dve.wait_ge(ws_prod, 2 * s + z + 1)
                    V.tensor_tensor(un[:], U[:, z], ps[:, 0, 0:FW].rearrange("p (h n) -> p h n", h=4), ALU.subtract).then_inc(un_ready, 1)
                    dve.wait_ge(o_prod, 2 * s + z + 1)
                    V.tensor_tensor(S[:], Sg[:], ps[:, 1, 0:FW].rearrange("p (h n) -> p h n", h=4), ALU.add).then_inc(s_ready, 1)
                for c in range(2):
                    for d, t in ((0, a), (1, b)):
                        z = c ^ d
                        o = o_sum[RS[c], t, :] if isinstance(t, int) else o_sum[RS[c], bass.ds(t, 1), :].rearrange("p o n -> p (o n)")
                        last = V.tensor_tensor(o, o, ps[RS[c], 2, z * FW:(z + 1) * FW], ALU.add)
                last.then_inc(o_taken, 1)
                assert n[0] == PER



            all_steps(dve, body)




def stage_mix_out(nc, g, l, tiles, latent, context):
    with Stage(nc, f"mix{l}") as st:
        w = st.sb("w", [P, KD, D])
        gb = st.sb("gb", [P, 2, D])
        x = st.sb("x", [P, 3, D])
        tmp = st.sb("tmp", [P, 2, D])
        w_loaded, gb_loaded, prod_ready, gated, summed = (st.sem(n) for n in "w_loaded gb_loaded prod_ready gated summed".split())
        x_loaded = [st.sem(f"x_loaded{i}") for i in range(3)]
        x_stored = [st.sem(f"x_stored{i}") for i in range(3)]
        with nc.Block() as block:
            @block.sync
            def _(sp):
                sp.dma_start(w[:], g.w_out[l].rearrange("(k p) n -> p k n", p=P)).then_inc(w_loaded, 16)
                for s in range(2):
                    sp.dma_start(gb[:, s], g.mod_rows[s:s + 1, 2 * D:3 * D].to_broadcast([P, D])).then_inc(gb_loaded, 16)
                for t in range(tiles):
                    wait(sp, x_stored[t % 3], 16 * (t // 3))
                    sp.dma_start(x[:, t % 3], token_tile(latent, context, t)).then_inc(x_loaded[t % 3], 16)

            @block.tensor
            def _(pe):
                pe.wait_ge(w_loaded, 16)
                for t in range(tiles):
                    wait(pe, gated, t - 1)
                    for half in range(2):
                        for k in range(KD):
                            mm = nc.tensor.matmul(g.ps[:, 2 * (t % 2) + half, :], g.yT[:, k, t * P:(t + 1) * P],
                                                  w[:, k, half * BANK:(half + 1) * BANK], start=k == 0, stop=k == KD - 1)
                    mm.then_inc(prod_ready, 1)

            @block.vector
            def _(dve):
                dve.wait_ge(gb_loaded, 32)
                for t in range(tiles):
                    dve.wait_ge(prod_ready, t + 1)
                    flat = g.ps[:, 2 * (t % 2):2 * (t % 2) + 2, :].rearrange("p b n -> p (b n)")
                    nc.vector.tensor_tensor(tmp[:, t % 2], flat, gb[:, t // NTL], ALU.mult).then_inc(gated, 1)
                    dve.wait_ge(gated, t + 1)
                    dve.wait_ge(x_loaded[t % 3], 16 * (t // 3 + 1))
                    nc.vector.tensor_tensor(x[:, t % 3], x[:, t % 3], tmp[:, t % 2], ALU.add).then_inc(summed, 1)

            @block.scalar
            def _(act):
                for t in range(tiles):
                    act.wait_ge(summed, t + 1)
                    act.dma_start(g.x_dram[t * P:(t + 1) * P, :], x[:, t % 3]).then_inc(x_stored[t % 3], 16)
                for i in range(3):
                    act.wait_ge(x_stored[i], 16 * len(range(i, tiles, 3)))


def stage_route(nc, g, l, tiles):
    with Stage(nc, f"route{l}") as st:
        w = st.sb("w", [P, KD, NE])
        bias = st.sb("bias", [P, NE])
        iota = st.sb("iota", [P, NE])
        sc = st.sb("sc", [P, tiles, NE])
        sel = st.sb("sel", [P, tiles, NE])
        eq = st.sb("eq", [P, tiles, NE])
        top = st.sb("top", [P, tiles, 8])
        idx = st.sb("idx", [P, tiles, 8], U32)
        idf = st.sb("idf", [P, tiles, 8])
        tot = st.sb("tot", [P, tiles])
        small_loaded, logits_ready, exp_ready, step = (st.sem(n) for n in "small_loaded logits_ready exp_ready step".split())
        with nc.Block() as block:
            @block.sync
            def _(sp):
                with nc.allow_non_contiguous_dma("router, once a layer"):
                    sp.dma_start(w[:], g.moe_router[l].rearrange("(k p) n -> p k n", p=P)).then_inc(small_loaded, 16)
                sp.dma_start(bias[:], g.moe_bias[l].rearrange("(o n) -> o n", o=1).to_broadcast([P, NE])).then_inc(small_loaded, 16)
                sp.dma_start(iota[:], g.t_iota.to_broadcast([P, NE])).then_inc(small_loaded, 16)

            @block.tensor
            def _(pe):
                pe.wait_ge(small_loaded, 48)
                for t in range(tiles):
                    for k in range(KD):
                        mm = nc.tensor.matmul(g.ps[:, 0, t * NE:(t + 1) * NE], g.hT[:, k, t * P:(t + 1) * P], w[:, k, :],
                                              start=k == 0, stop=k == KD - 1)
                mm.then_inc(logits_ready, 1)

            @block.scalar
            def _(act):
                act.wait_ge(logits_ready, 1)
                nc.scalar.activation(sc[:], g.ps[:, 0, 0:tiles * NE].rearrange("p (t n) -> p t n", n=NE), ACT.Exp, scale=-1.0).then_inc(exp_ready, 1)

            @block.vector
            def _(dve):
                V = nc.vector
                link = Chain(dve, step)
                dve.wait_ge(exp_ready, 1)
                dve.wait_ge(small_loaded, 48)
                link(V.tensor_scalar(sc[:], sc[:], 1.0, None, ALU.add))
                link(V.reciprocal(sc[:], sc[:]))
                link(V.tensor_tensor(sel[:], sc[:], bias[:].unsqueeze(1).to_broadcast([P, tiles, NE]), ALU.add))
                for t in range(tiles):
                    last = V.max(top[:, t, :], sel[:, t, :])
                link(last)
                for t in range(tiles):
                    last = V.max_index(idx[:, t, :], top[:, t, :], sel[:, t, :])
                link(last)
                link(V.tensor_copy(idf[:], idx[:]))
                for j in range(4):
                    dst = sel if j == 0 else eq
                    link(V.tensor_tensor(dst[:], iota[:].unsqueeze(1).to_broadcast([P, tiles, NE]),
                                         idf[:, :, j:j + 1].to_broadcast([P, tiles, NE]), ALU.is_equal))
                    if j:
                        link(V.tensor_tensor(sel[:], sel[:], eq[:], ALU.add))
                link(V.tensor_tensor(sel[:], sel[:], sc[:], ALU.mult))
                link(V.tensor_reduce(tot[:], sel[:], AX.X, ALU.add))
                link(V.reciprocal(tot[:], tot[:]))
                link(V.tensor_scalar(tot[:], tot[:], ROUTED_SCALE, None, ALU.mult))
                link(V.tensor_tensor(g.moe_w[:, 0:tiles, :], sel[:], tot[:].unsqueeze(2).to_broadcast([P, tiles, NE]), ALU.mult))


def stage_experts(nc, g, l, tiles):
    chunks = CHUNKS if tiles == NT else CHUNKS[:2]
    NCK = len(chunks)
    acc = g.acc
    with Stage(nc, f"moe{l}") as st:
        wg = st.sb("wg", [P, 2, KD, DE])
        wu = st.sb("wu", [P, 2, KD, DE])
        wd = st.sb("wd", [P, 2, 2, D])
        sg = st.sb("sg", [P, 2, BANK])
        hid = st.sb("hid", [P, 2, 2, TOK])
        one = st.sb("one", [P, 1])
        names = "up_ready silu_ready hid_ready up_done down_ready added cleared".split()
        up_ready, silu_ready, hid_ready, up_done, down_ready, added, cleared = (st.sem(n) for n in names)
        w_loaded = [st.sem(f"w_loaded{i}") for i in range(2)]

        def all_experts(eng, body):
            with eng.Fori(0, NE // 2) as i:
                for b in range(2):
                    body(i * 2 + b, b, True)
            body(NE, 0, False)

        U = 2 * NCK
        with nc.Block() as block:
            @block.gpsimd
            def _(pool):
                pool.memset(acc[:], 0.0)
                pool.memset(one[:], 1.0).then_inc(cleared, 1)
                pool.sem_inc(down_ready, 2 * tiles)

            @block.sync
            def _(sp):
                def body(e, b, routed):
                    sp.wait_ge(down_ready, (e + 1) * tiles)
                    for dst, src, shared in ((wg, g.moe_gate, g.sh_gate), (wu, g.moe_up, g.sh_up), (wd, g.moe_down, g.sh_down)):
                        a = src[l][bass.ds(e, 1)] if routed else shared[l:l + 1]
                        k = dst.shape[2]
                        sp.dma_start(dst[:, b], a.rearrange("o (k p) n -> p (o k) n", p=P)).then_inc(w_loaded[b], 16)

                all_experts(sp, body)

            @block.tensor
            def _(pe):
                def body(e, b, routed):
                    if routed:
                        pe.wait_ge(w_loaded[b], (e - b) * 24 + 48)
                    else:
                        pe.wait_ge(w_loaded[b], NE * 24 + 48)

                    def up(c):
                        c0, n = chunks[c]
                        for f in range(2):
                            m = 2 * c + f
                            for i, w in enumerate((wg, wu)):
                                bank = 2 * (m % 2) + i
                                if i == 0:
                                    pe.wait_ge(hid_ready, e * U + m + 1)
                                for k in range(KD):
                                    mm = nc.tensor.matmul(g.ps[:, bank, 0:n], w[:, b, k, f * P:(f + 1) * P], g.hT[:, k, c0:c0 + n],
                                                          start=k == 0, stop=k == KD - 1)
                            mm.then_inc(up_ready, 1)

                    def down(c):
                        c0, n = chunks[c]
                        pe.wait_ge(hid_ready, e * U + 2 * c + 4)
                        for t in range(c0 // P, (c0 + n) // P):
                            pe.wait_ge(added, e * tiles + t + 1)
                            for half in range(2):
                                for f in range(2):
                                    mm = nc.tensor.matmul(g.ps[:, 4 + 2 * (t % 2) + half, :], hid[:, b, f, t * P:(t + 1) * P],
                                                          wd[:, b, f, half * BANK:(half + 1) * BANK], start=f == 0, stop=f == 1)
                            mm.then_inc(down_ready, 1)

                    for c in range(NCK):
                        up(c)
                        if c >= 1:
                            down(c - 1)
                    down(NCK - 1)

                all_experts(pe, body)

            @block.scalar
            def _(act):
                act.sem_inc(hid_ready, 2)

                def body(e, b, routed):
                    for c, (c0, n) in enumerate(chunks):
                        for f in range(2):
                            m = 2 * c + f
                            act.wait_ge(up_ready, e * U + m + 1)
                            act.wait_ge(hid_ready, e * U + m + 1)
                            nc.scalar.activation(sg[:, m % 2, 0:n], g.ps[:, 2 * (m % 2), 0:n], ACT.Silu).then_inc(silu_ready, 1)

                all_experts(act, body)

            @block.vector
            def _(dve):
                dve.sem_inc(added, 2)
                dve.wait_ge(cleared, 1)

                def body(e, b, routed):
                    def add(c):
                        c0, n = chunks[c]
                        for t in range(c0 // P, (c0 + n) // P):
                            dve.wait_ge(down_ready, e * tiles + t + 1 + 2 * tiles)
                            weight = g.moe_w[:, t, bass.ds(e, 1)] if routed else one[:]
                            flat = g.ps[:, 4 + 2 * (t % 2):6 + 2 * (t % 2), :].rearrange("p b n -> p (b n)")
                            dve.wait_ge(added, e * tiles + t + 2)
                            nc.vector.scalar_tensor_tensor(out=acc[:, t, :], in0=flat, scalar=weight, in1=acc[:, t, :],
                                                           op0=ALU.mult, op1=ALU.add).then_inc(added, 1)

                    for c, (c0, n) in enumerate(chunks):
                        for f in range(2):
                            m = 2 * c + f
                            dve.wait_ge(silu_ready, e * U + m + 1)
                            nc.vector.tensor_tensor(hid[:, b, f, c0:c0 + n], sg[:, m % 2, 0:n], g.ps[:, 2 * (m % 2) + 1, 0:n],
                                                    ALU.mult).then_inc(hid_ready, 1)
                        if c >= 1:
                            add(c - 1)
                    add(NCK - 1)

                all_experts(dve, body)


def stage_moe_out(nc, g, l, tiles, final):
    with Stage(nc, f"res{l}") as st:
        gb = st.sb("gb", [P, 2, D])
        nf = st.sb("nf", [P, D])
        x = st.sb("x", [P, 3, D])
        tmp = st.sb("tmp", [P, 2, D])
        ss = st.sb("ss", [P, tiles])
        names = "gb_loaded gated summed squared mean_ready root_ready rstd_ready normed out_ready".split()
        gb_loaded, gated, summed, squared, mean_ready, root_ready, rstd_ready, normed, out_ready = (st.sem(n) for n in names)
        x_loaded = [st.sem(f"x_loaded{i}") for i in range(3)]
        x_stored = [st.sem(f"x_stored{i}") for i in range(3)]
        with nc.Block() as block:
            @block.sync
            def _(sp):
                for s in range(2):
                    sp.dma_start(gb[:, s], g.mod_rows[s:s + 1, 5 * D:6 * D].to_broadcast([P, D])).then_inc(gb_loaded, 16)
                sp.dma_start(nf[:], g.norm_f.rearrange("(o n) -> o n", o=1).to_broadcast([P, D])).then_inc(gb_loaded, 16)
                for t in range(tiles):
                    wait(sp, x_stored[t % 3], 16 * (t // 3))
                    sp.dma_start(x[:, t % 3], g.x_dram[t * P:(t + 1) * P, :]).then_inc(x_loaded[t % 3], 16)

            @block.vector
            def _(dve):
                dve.wait_ge(gb_loaded, 48)
                for t in range(tiles):
                    if final:
                        wait(dve, squared, t - 1)
                    nc.vector.tensor_tensor(tmp[:, t % 2], g.acc[:, t, :], gb[:, t // NTL], ALU.mult).then_inc(gated, 1)
                    dve.wait_ge(gated, t + 1)
                    dve.wait_ge(x_loaded[t % 3], 16 * (t // 3 + 1))
                    nc.vector.tensor_tensor(x[:, t % 3], x[:, t % 3], tmp[:, t % 2], ALU.add).then_inc(summed, 1)
                    if final:
                        dve.wait_ge(squared, t + 1)
                        nc.vector.tensor_scalar(ss[:, t:t + 1], ss[:, t:t + 1], 1.0 / D, EPS, ALU.mult, ALU.add).then_inc(mean_ready, 1)
                        dve.wait_ge(root_ready, t + 1)
                        nc.vector.reciprocal(ss[:, t:t + 1], ss[:, t:t + 1]).then_inc(rstd_ready, 1)
                        dve.wait_ge(rstd_ready, t + 1)
                        nc.vector.scalar_tensor_tensor(out=x[:, t % 3], in0=x[:, t % 3], scalar=ss[:, t:t + 1], in1=nf[:],
                                                       op0=ALU.mult, op1=ALU.mult).then_inc(out_ready, 1)

            @block.scalar
            def _(act):
                for t in range(tiles):
                    act.wait_ge(summed, t + 1)
                    if final:
                        nc.scalar.activation(tmp[:, t % 2], x[:, t % 3], ACT.Square, accum_out=ss[:, t:t + 1]).then_inc(squared, 1)
                        act.wait_ge(mean_ready, t + 1)
                        nc.scalar.activation(ss[:, t:t + 1], ss[:, t:t + 1], ACT.Sqrt).then_inc(root_ready, 1)
                        act.wait_ge(out_ready, t + 1)
                        dst = g.out[0, t * P:(t + 1) * P, :]
                    else:
                        dst = g.x_dram[t * P:(t + 1) * P, :]
                    act.dma_start(dst, x[:, t % 3]).then_inc(x_stored[t % 3], 16)
                for i in range(3):
                    act.wait_ge(x_stored[i], 16 * len(range(i, tiles, 3)))


def shape_tables():
    t = {}
    f32 = np.float32
    t["t_ident"] = np.eye(P, dtype=f32)

    for name, L in (("", SEQ), ("_c", CTX)):
        n = np.arange(L, dtype=f32)
        t_norm = n / f32(L - 1)
        bands = np.linspace(1e-4, HY_BANDS - 1, HY_BANDS, dtype=f32)
        ang = (f32(2.0 * math.pi / L) * n[:, None] * bands[None, :]).astype(f32)
        z = np.concatenate([t_norm[:, None], np.cos(ang), -np.sin(ang)], axis=-1).astype(f32)
        t["t_hy_z" + name] = np.ascontiguousarray(z.T)
        lo, hi = -math.log(1e-2) / 1.5, -math.log(1e-2) / 0.3
        decay = np.linspace(lo, hi, HY_CH, dtype=f32)
        d = np.exp(-t_norm[:, None] * decay[None, :]).astype(f32)
        db = d.copy()
        db[0] = 0
        t["t_hy_dec" + name] = np.concatenate([d, db], axis=1)
        j = np.arange(L)[:, None].astype(np.float64)
        k = np.arange(L)[None, :].astype(np.float64)

        def blocks(a):
            return a.reshape(L // P, P, L // P, P).transpose(2, 1, 0, 3)

        a = math.pi / (2 * L) * (2 * k + 1)
        t["t_dft" + name] = np.ascontiguousarray(np.stack([blocks(np.cos(a * j)), blocks(np.sin(a * j))]).astype(f32))
        C2 = np.stack([np.cos(a * (j + 0.5)), np.sin(a * (j + 0.5))]).astype(f32)
        t["t_dft2" + name] = np.ascontiguousarray(np.stack([blocks(C2[0]), blocks(C2[1])]))
        t["t_dft2r" + name] = C2
    quarter = HD // 4
    inv = (f32(10000.0) ** (-np.arange(quarter, dtype=f32) / f32(quarter))).astype(f32)
    pos = np.arange(SEQ)
    row, col = (pos // GRID_W).astype(f32), (pos % GRID_W).astype(f32)
    ang = np.concatenate([np.tile(row[:, None] * inv, 2), np.tile(col[:, None] * inv, 2)], axis=1).astype(f32)
    t["t_rope"] = np.ascontiguousarray(np.stack([np.tile(np.cos(ang), 2).T, np.tile(np.sin(ang), 2).T]).astype(f32))
    rot = np.zeros((P, P), f32)
    for base in range(0, P, 2 * quarter):
        for d in range(quarter):
            rot[base + quarter + d, base + d] = -1.0
            rot[base + d, base + quarter + d] = 1.0
    t["t_rot"] = rot
    q = np.arange(P)[:, None]
    k = np.arange(P)[None, :]
    m = np.zeros((P, CTX + 3 * P), f32)
    m[:, CTX:CTX + P] = np.where(k >= q, 0, NEG)
    m[:, CTX + 2 * P:] = np.where(k <= q, 0, NEG)
    t["t_wa_mask"] = m
    sel = np.zeros((32, GRID_W, 2, GRID_W), f32)
    cq = np.arange(GRID_W)
    start = np.clip(cq - NA_KC // 2, 0, GRID_W - NA_KC)
    for ck in range(GRID_W):
        for c in range(GRID_W):
            if start[c] <= ck < start[c] + NA_KC:
                sel[ck - c + NA_KC - 1, ck, :, c] = 1
            else:
                sel[31, ck, :, c] = 1
    t["t_na_sel"] = sel.reshape(32, GRID_W * P)
    return t


def gdn_tables():
    C = 64
    t = {}
    i = np.arange(C)[:, None]
    j = np.arange(C)[None, :]
    two = lambda a: np.tile(a, (2,) + (1,) * (a.ndim - 1)).astype(np.float32)
    dirs = lambda f, b: np.stack([f, b], axis=1)
    t["t_gd_tri"] = two(dirs(i <= j, i >= j))
    t["t_gd_allow"] = two(np.where(dirs(i >= j, i <= j), 1e30, NEG))
    t["t_gd_strict"] = two(dirs(i > j, i < j))
    t["t_gd_eye"] = two(np.eye(C))
    lv = []
    for s in (1, 2, 4, 8, 16, 32):
        m = (i // (2 * s) == j // (2 * s)) & (i // s % 2 == 1) & (j // s % 2 == 0)
        lv.append(dirs(m, m.T))
    lv.insert(1, lv[0][:, ::-1])
    t["t_gd_lvl"] = two(np.stack(lv, axis=1))
    blk = np.kron(np.eye(2), np.ones((C, C)))
    t["t_gd_negblk"] = -blk.astype(np.float32)
    a = np.arange(P)
    same = blk.astype(bool)
    t["t_gd_cum"] = np.stack([same & (a[:, None] <= a[None, :]), same & (a[:, None] >= a[None, :]), same], axis=1).astype(np.float32)
    return {k: np.ascontiguousarray(v) for k, v in t.items()}


NAMES = ["x", "c", "ctx", "c_ctx", "w_ada", "b_ada", "norm1", "norm2", "norm_f", "w_in", "w_out",
         "hy_conv", "hy_w1", "hy_b1", "hy_w2", "hy_b2", "hy_w3", "hy_freq", "hy_bias",
         "wa_sink", "na_rpb", "gdn_conv", "gdn_a_log", "gdn_dt_bias", "gdn_norm",
         "moe_router", "moe_bias", "moe_gate", "moe_up", "moe_down", "sh_gate", "sh_up", "sh_down"]


class Globals:

    def __init__(self, arrays):
        self.tables = arrays
        (self.x, self.c, self.ctx, self.c_ctx, self.w_ada, self.b_ada, self.norm1, self.norm2, self.norm_f, self.w_in,
         self.w_out, self.hy_conv, self.hy_w1, self.hy_b1, self.hy_w2, self.hy_b2, self.hy_w3, self.hy_freq, self.hy_bias,
         self.wa_sink, self.na_rpb, self.gdn_conv, self.gdn_a_log, self.gdn_dt_bias, self.gdn_norm,
         self.moe_router, self.moe_bias, self.moe_gate, self.moe_up, self.moe_down,
         self.sh_gate, self.sh_up, self.sh_down) = (arrays[n] for n in NAMES)
        self.t_ident, self.t_iota, self.t_rope, self.t_rot, self.t_wa_mask, self.t_na_sel = (
            arrays[n] for n in ("t_ident", "t_iota", "t_rope", "t_rot", "t_wa_mask", "t_na_sel"))


def hybrid_backbone(nc, arrays, out):
    g = Globals(arrays)
    g.out = out
    g.hy_tables = [(arrays["t_hy_z" + s], arrays["t_hy_dec" + s], arrays["t_dft" + s], arrays["t_dft2" + s]) for s in ("", "_c")]
    g.hy_rows = [arrays["t_dft2r"], arrays["t_dft2r_c"]]
    g.gdn_masks = {n: list(arrays["t_" + n].shape[1:]) for n in ("gd_tri", "gd_allow", "gd_strict", "gd_eye", "gd_lvl", "gd_negblk")}
    g.x_dram = nc.dram_tensor("x_dram", [TOK, D], F32, kind="Internal").ap()
    g.mod_rows = nc.dram_tensor("mod_rows", [2, 6 * D], F32, kind="Internal").ap()
    with ExitStack() as ctx:
        def sb(name, shape):
            return ctx.enter_context(nc.sbuf_tensor(name, shape, F32))
        g.ps = ctx.enter_context(nc.psum_tensor("ps", [P, 8, BANK], F32))
        g.ident = sb("ident", [P, P])
        g.siluT = sb("siluT", [P, KD, 2])
        g.modT = sb("modT", [P, 6 * KD, 2])
        g.gain = sb("gain", [P, 2, KD, 2])
        g.moe_w = sb("moe_w", [P, NT, NE])
        g.hT = sb("hT", [P, KD, TOK])
        mixed = sb("mixed", [P, NT * D])
        g.yT = mixed[:].rearrange("p (k n) -> p k n", k=KD)
        g.acc = mixed[:].rearrange("p (t n) -> p t n", t=NT)
        stage_setup(nc, g)
        for l in range(DEPTH):
            last = l == DEPTH - 1
            tiles = NTL if last else NT
            latent, context = (g.x[0], g.ctx[0]) if l == 0 else (g.x_dram[0:SEQ, :], g.x_dram[SEQ:TOK, :])
            stage_modulation(nc, g, l)
            stage_norm(nc, g, l, 0, NT, latent, context)
            stage_hyena(nc, g, l, False)
            if not last:
                stage_hyena(nc, g, l, True)
            stage_window(nc, g, l, not last)
            stage_neighbour(nc, g, l, not last)
            stage_gdn(nc, g, l)
            stage_mix_out(nc, g, l, tiles, latent, context)
            stage_norm(nc, g, l, 1, tiles, g.x_dram[0:SEQ, :], g.x_dram[SEQ:TOK, :])
            stage_route(nc, g, l, tiles)
            stage_experts(nc, g, l, tiles)
            stage_moe_out(nc, g, l, tiles, last)


def kernel(**inputs):
    import concourse.bacc as bacc
    from concourse.bass_utils import run_bass_kernel_spmd

    nc = bacc.Bacc("TRN2", target_bir_lowering=False, num_devices=1)
    tables = shape_tables()
    tables.update(gdn_tables())
    tables["t_iota"] = np.arange(NE, dtype=np.float32)[None, :]
    feeds, args = {}, {}
    for name in NAMES:
        feeds["in_" + name] = np.ascontiguousarray(inputs[name])
    for name, a in tables.items():
        feeds["in_" + name] = a
    for name, a in feeds.items():
        args[name[3:]] = nc.dram_tensor(name, a.shape, F32, kind="ExternalInput").ap()
    out = nc.dram_tensor("out", (1, SEQ, D), F32, kind="ExternalOutput").ap()
    hybrid_backbone(nc, args, out)
    nc.compile()
    r = run_bass_kernel_spmd(nc, [feeds], core_ids=[0])
    return r.results[0]["out"]
```

```python
import math
from contextlib import ExitStack

import numpy as np

import concourse.bass as bass
from concourse import mybir

F32 = mybir.dt.float32
U32 = mybir.dt.uint32
ALU = mybir.AluOpType
ACT = mybir.ActivationFunctionType
AX = mybir.AxisListType

P = 128
D = 1024
KD = D // P
SEQ = 1024
CTX = 256
NTL = SEQ // P
NTC = CTX // P
NT = NTL + NTC
TOK = SEQ + CTX
DEPTH = 2
BANK = 512
HD = 64

HY_CH = 256
HY_BANDS = 16
HY_EMB = 1 + 2 * HY_BANDS
HY_FFN = 64
HY_IN = 3 * HY_CH
WA_IN = 512
NA_IN = 768
GW = 256
GDN_IN = 4 * GW + 16
WA0, NA0, GD0 = HY_IN, HY_IN + WA_IN, HY_IN + WA_IN + NA_IN
D_IN = GD0 + GDN_IN
NE = 32
DE = 256
NEG = -1e30
EPS = 1e-6
SCALE = HD ** -0.5
GRID_W = 64
NA_KR, NA_KC = 8, 16
ROUTED_SCALE = 2.5
TOP_K = 4
RING = 3
MAGIC = 1.5 * 2.0 ** 23
CHUNKS = [(0, BANK), (BANK, BANK), (SEQ, CTX)]


def blocks_of(tiles):
    return (tiles * TOP_K + NE - 1 + 1) // 2 * 2


MAX_BLOCKS = blocks_of(NT)


def wait(eng, sem, value):
    if not isinstance(value, int) or value > 0:
        eng.wait_ge(sem, value)


class Chain:

    def __init__(self, eng, sem):
        self.eng, self.sem, self.n = eng, sem, 0

    def __call__(self, instruction):
        self.n += 1
        instruction.then_inc(self.sem, 1)
        self.eng.wait_ge(self.sem, self.n)


class Stage:

    def __init__(self, nc, tag):
        self.nc, self.tag, self.sems, self.stack = nc, tag, [], ExitStack()

    def __enter__(self):
        self.stack.__enter__()
        return self

    def __exit__(self, *a):
        self.nc.clear_and_free_semaphores(self.sems)
        self.nc.all_engine_barrier()
        return self.stack.__exit__(*a)

    def sb(self, name, shape, dt=F32):
        return self.stack.enter_context(self.nc.sbuf_tensor(f"{name}_{self.tag}", shape, dt))

    def sem(self, name):
        s = self.nc.alloc_semaphore(f"{name}_{self.tag}")
        self.sems.append(s)
        return s


def stage_setup(nc, g):
    with Stage(nc, "setup") as st:
        cT = st.sb("cT", [P, KD, 2])
        e = st.sb("e", [P, KD, 2])
        loaded, c_loaded, exp_ready, silu_step = (st.sem(n) for n in ("loaded", "c_loaded", "exp_ready", "silu_step"))
        with nc.Block() as block:
            @block.sync
            def _(sp):
                sp.dma_start(g.ident[:], g.t_ident).then_inc(loaded, 16)

                with nc.allow_non_contiguous_dma("conditioning vectors, once"):
                    sp.dma_start(cT[:, :, 0], g.c.rearrange("o (k p) -> p (o k)", p=P)).then_inc(c_loaded, 16)
                    sp.dma_start(cT[:, :, 1], g.c_ctx.rearrange("(k p) -> p k", p=P)).then_inc(c_loaded, 16)
                sp.wait_ge(loaded, 16)

            @block.scalar
            def _(act):
                act.wait_ge(c_loaded, 32)
                nc.scalar.activation(e[:], cT[:], ACT.Exp, scale=-1.0).then_inc(exp_ready, 1)

            @block.vector
            def _(dve):
                link = Chain(dve, silu_step)
                dve.wait_ge(exp_ready, 1)
                link(nc.vector.tensor_scalar_add(e[:], e[:], 1.0))
                link(nc.vector.reciprocal(e[:], e[:]))
                link(nc.vector.tensor_tensor(g.siluT[:], e[:], cT[:], ALU.mult))


def stage_modulation(nc, g, l):
    NCH = 6 * D // BANK
    with Stage(nc, f"mod{l}") as st:
        w = st.sb("w", [P, 3, KD, BANK])
        rows = st.sb("rows", [2, 6 * D])
        bias = st.sb("bias", [2, 6 * D])
        normT = st.sb("normT", [P, 2, KD])
        w_loaded = [st.sem(f"w_loaded{i}") for i in range(3)]
        bias_loaded, norm_loaded, chunk_ready, row_ready, turned, stored, mod_step = (
            st.sem(n) for n in ("bias_loaded", "norm_loaded", "chunk_ready", "row_ready", "turned", "stored", "mod_step"))
        wv = g.w_ada[l].rearrange("(k p) n -> p k n", p=P)
        with nc.Block() as block:
            @block.sync
            def _(sp):
                sp.dma_start(bias[:], g.b_ada[l].rearrange("(o n) -> o n", o=1).to_broadcast([2, 6 * D])).then_inc(bias_loaded, 16)
                with nc.allow_non_contiguous_dma("norm gains, once a layer"):
                    sp.dma_start(normT[:, 0, :], g.norm1[l].rearrange("(k p) -> p k", p=P)).then_inc(norm_loaded, 16)
                    sp.dma_start(normT[:, 1, :], g.norm2[l].rearrange("(k p) -> p k", p=P)).then_inc(norm_loaded, 16)
                for n in range(NCH):
                    wait(sp, chunk_ready, n - 2)
                    sp.dma_start(w[:, n % 3], wv[:, :, n * BANK:(n + 1) * BANK]).then_inc(w_loaded[n % 3], 16)
                sp.wait_ge(row_ready, NCH)
                sp.dma_start(g.mod_rows, rows[:]).then_inc(stored, 16)
                sp.wait_ge(stored, 16)

            @block.tensor
            def _(pe):
                for n in range(NCH):
                    pe.wait_ge(w_loaded[n % 3], 16 * (n // 3 + 1))
                    wait(pe, row_ready, n - 1)
                    for k in range(KD):
                        mm = nc.tensor.matmul(g.ps[0:2, n % 2, :], g.siluT[:, k, :], w[:, n % 3, k, :],
                                              start=k == 0, stop=k == KD - 1)
                    mm.then_inc(chunk_ready, 1)
                pe.wait_ge(row_ready, NCH)
                for k in range(6 * KD):
                    mm = nc.tensor.transpose(g.ps[:, 2, 2 * k:2 * k + 2], rows[:, k * P:(k + 1) * P], g.ident[0:2, 0:2])
                mm.then_inc(turned, 1)

            @block.vector
            def _(dve):
                link = Chain(dve, mod_step)
                dve.wait_ge(bias_loaded, 16)
                for n in range(NCH):
                    dve.wait_ge(chunk_ready, n + 1)
                    cols = slice(n * BANK, (n + 1) * BANK)
                    nc.vector.tensor_tensor(rows[:, cols], g.ps[0:2, n % 2, :], bias[:, cols], ALU.add).then_inc(row_ready, 1)
                dve.wait_ge(turned, 1)
                link(nc.vector.tensor_copy(g.modT[:], g.ps[:, 2, 0:12 * KD].rearrange("p (k s) -> p k s", s=2)))
                dve.wait_ge(norm_loaded, 32)
                for i, sc0 in ((0, KD), (1, 4 * KD)):
                    link(nc.vector.scalar_tensor_tensor(
                        out=g.gain[:, i], in0=g.modT[:, sc0:sc0 + KD, :], scalar=1.0,
                        in1=normT[:, i, :].unsqueeze(2).to_broadcast([P, KD, 2]), op0=ALU.add, op1=ALU.mult))


def token_tile(latent, context, t):
    return latent[t * P:(t + 1) * P, :] if t < NTL else context[(t - NTL) * P:(t - NTL + 1) * P, :]


def stage_norm(nc, g, l, which, tiles, latent, context):
    with Stage(nc, f"norm{which}_{l}") as st:
        x = st.sb("x", [P, 3, D])
        xn = st.sb("xn", [P, 2, D])
        sq = st.sb("sq", [P, D])
        if which:
            rows = st.sb("rows", [P, 2, 2, D])
            nrow = st.sb("nrow", [P, D])
            h = st.sb("h", [P, 2, D])
            rows_loaded, row_step, h_ready = st.sem("rows_loaded"), st.sem("row_step"), st.sem("h_ready")
            h_stored = [st.sem(f"h_stored{i}") for i in range(2)]
        ss = st.sb("ss", [P, tiles])
        rs = st.sb("rs", [P, tiles])
        rt = st.sb("rt", [P, tiles])
        x_loaded = [st.sem(f"x_loaded{i}") for i in range(3)]
        names = "squares_summed mean_ready root_ready rstd_ready scaled turned taken_lo taken_hi step".split()
        squares_summed, mean_ready, root_ready, rstd_ready, scaled, turned, taken_lo, taken_hi, step = (st.sem(n) for n in names)
        sh0 = 0 if which == 0 else 3 * KD
        with nc.Block() as block:
            @block.sync
            def _(sp):
                if which:
                    for s in range(2):
                        for i, m in ((0, 4), (1, 3)):
                            sp.dma_start(rows[:, i, s], g.mod_rows[s:s + 1, m * D:(m + 1) * D].to_broadcast([P, D])).then_inc(rows_loaded, 16)
                    sp.dma_start(nrow[:], g.norm2[l].rearrange("(o n) -> o n", o=1).to_broadcast([P, D])).then_inc(rows_loaded, 16)
                for t in range(tiles + 1):
                    if t < tiles:
                        wait(sp, scaled, t - 2)
                        sp.dma_start(x[:, t % 3], token_tile(latent, context, t)).then_inc(x_loaded[t % 3], 16)
                    if which and t >= 1:
                        sp.wait_ge(h_ready, t)
                        sp.dma_start(g.h_dram[(t - 1) * P:t * P, :], h[:, (t - 1) % 2]).then_inc(h_stored[(t - 1) % 2], 16)
                if which:
                    for i in range(2):
                        sp.wait_ge(h_stored[i], 16 * len(range(i, tiles, 2)))

            if which:
                @block.gpsimd
                def _(pool):
                    link = Chain(pool, row_step)
                    pool.wait_ge(rows_loaded, 80)
                    nr = nrow[:].unsqueeze(1).to_broadcast([P, 2, D])
                    link(nc.gpsimd.tensor_tensor(rows[:, 0], rows[:, 0], nr, ALU.mult))
                    link(nc.gpsimd.tensor_tensor(rows[:, 0], rows[:, 0], nr, ALU.add))
                    for t in range(tiles):
                        pool.wait_ge(scaled, t + 1)
                        wait(pool, h_stored[t % 2], 16 * (t // 2))
                        link(nc.gpsimd.tensor_tensor(h[:, t % 2], xn[:, t % 2], rows[:, 0, t // NTL], ALU.mult))
                        nc.gpsimd.tensor_tensor(h[:, t % 2], h[:, t % 2], rows[:, 1, t // NTL], ALU.add).then_inc(h_ready, 1)

            @block.scalar
            def _(act):
                for t in range(tiles + 1):
                    if t < tiles:
                        act.wait_ge(x_loaded[t % 3], 16 * (t // 3 + 1))
                        wait(act, squares_summed, t)
                        nc.scalar.activation(sq[:], x[:, t % 3], ACT.Square, accum_out=ss[:, t:t + 1]).then_inc(squares_summed, 1)
                        act.wait_ge(mean_ready, t + 1)
                        nc.scalar.activation(rs[:, t:t + 1], ss[:, t:t + 1], ACT.Sqrt).then_inc(root_ready, 1)
                    if t >= 1:
                        u = t - 1
                        s = u // NTL
                        act.wait_ge(turned, u + 1)
                        for k in range(KD // 2, KD):
                            o = nc.scalar.activation(g.hT[:, k, u * P:(u + 1) * P],
                                                     g.ps[:, 2 * (u % 2) + 1, (k % 4) * P:(k % 4 + 1) * P], ACT.Identity,
                                                     scale=g.gain[:, which, k, s:s + 1], bias=g.modT[:, sh0 + k, s:s + 1])
                        o.then_inc(taken_hi, 1)

            @block.vector
            def _(dve):
                for t in range(tiles + 1):
                    if t < tiles:
                        dve.wait_ge(squares_summed, t + 1)
                        nc.vector.tensor_scalar(ss[:, t:t + 1], ss[:, t:t + 1], 1.0 / D, EPS, ALU.mult, ALU.add).then_inc(mean_ready, 1)
                        dve.wait_ge(root_ready, t + 1)
                        nc.vector.reciprocal(rt[:, t:t + 1], rs[:, t:t + 1]).then_inc(rstd_ready, 1)
                        dve.wait_ge(rstd_ready, t + 1)
                        wait(dve, turned, t - 1)
                        if which:
                            wait(dve, h_ready, t - 1)
                        nc.vector.tensor_scalar(xn[:, t % 2], x[:, t % 3], rt[:, t:t + 1], None, ALU.mult).then_inc(scaled, 1)
                    if t >= 1:
                        u = t - 1
                        s = u // NTL
                        dst = g.hT[:, 0:4, u * P:(u + 1) * P]
                        dve.wait_ge(turned, u + 1)
                        nc.vector.tensor_tensor(dst, g.ps[:, 2 * (u % 2), :].rearrange("p (k n) -> p k n", k=4),
                                                g.gain[:, which, 0:4, s:s + 1].to_broadcast([P, 4, P]), ALU.mult).then_inc(step, 1)
                        dve.wait_ge(step, t)
                        nc.vector.tensor_tensor(dst, dst, g.modT[:, sh0:sh0 + 4, s:s + 1].to_broadcast([P, 4, P]),
                                                ALU.add).then_inc(taken_lo, 1)

            @block.tensor
            def _(pe):
                for t in range(tiles):
                    pe.wait_ge(scaled, t + 1)
                    wait(pe, taken_lo, t - 1)
                    wait(pe, taken_hi, t - 1)
                    for k in range(KD):
                        mm = nc.tensor.transpose(g.ps[:, 2 * (t % 2) + k // 4, (k % 4) * P:(k % 4 + 1) * P],
                                                 xn[:, t % 2, k * P:(k + 1) * P], g.ident[:])
                    mm.then_inc(turned, 1)


def stage_hyena(nc, g, l, ctx):
    L = CTX if ctx else SEQ
    tok0 = SEQ if ctx else 0
    NL = L // P
    CH = min(L, BANK)
    NC = L // CH
    fil_z, fil_dec, t_dft, t_dft2 = g.hy_tables[ctx]
    with Stage(nc, f"hy{l}{'c' if ctx else ''}") as st:
        Kf = st.sb("Kf", [P, NL, 3 * HY_CH])
        x0 = st.sb("x0", [P, 2, L])
        gv = st.sb("gv", [P, 2, L])
        gT = st.sb("gT", [P, NL, HY_CH])
        with ExitStack() as filt:
            def sb(name, shape):
                return filt.enter_context(nc.sbuf_tensor(f"{name}_{st.tag}", shape, F32))
            zT = sb("zT", [HY_EMB, L])
            w1 = sb("w1", [HY_EMB, HY_FFN])
            w2 = sb("w2", [HY_FFN, HY_FFN])
            w3 = sb("w3", [HY_FFN, 2 * HY_CH])
            cols = sb("cols", [HY_FFN, 3])
            arg = sb("arg", [HY_FFN, L])
            rnd = sb("rnd", [HY_FFN, L])
            hid = sb("hid", [HY_FFN, L])
            dec = sb("dec", [P, 2, 2 * HY_CH])
            fb = sb("fb", [P, 2, 2 * HY_CH])
            kpm = sb("kpm", [P, 2, NL, HY_CH])
            dft = sb("dft", [P, 2, 2, NL, P])
            names = ("small_loaded sin_in sin_ready layer_ready filt_ready filt_taken fb_ready kpm_ready spec_ready spec_taken arg_step").split()
            small_loaded, sin_in, sin_ready, layer_ready, filt_ready, filt_taken, fb_ready, kpm_ready, spec_ready, spec_taken, arg_step = (
                st.sem(n) for n in names)
            dec_loaded = [st.sem(f"dec_loaded{i}") for i in range(2)]
            dft_loaded = [st.sem(f"dft_loaded{i}") for i in range(2)]
            with nc.Block() as block:
                @block.sync
                def _(sp):
                    for dst, src in ((zT[:], fil_z), (w1[:], g.hy_w1[l]), (w2[:], g.hy_w2[l]), (w3[:], g.hy_w3[l]),
                                     (cols[:, 0:1], g.hy_b1[l].rearrange("(p o) -> p o", o=1)),
                                     (cols[:, 1:2], g.hy_b2[l].rearrange("(p o) -> p o", o=1)),
                                     (cols[:, 2:3], g.hy_freq[l].rearrange("(p o) -> p o", o=1))):
                        sp.dma_start(dst, src).then_inc(small_loaded, 16)
                    for t in range(NL):
                        wait(sp, fb_ready, t - 1)
                        sp.dma_start(dec[:, t % 2], fil_dec[t * P:(t + 1) * P, :]).then_inc(dec_loaded[t % 2], 16)
                    for t in range(NL):
                        wait(sp, spec_ready, t - 1)
                        for i in range(2):
                            sp.dma_start(dft[:, t % 2, i], t_dft[i, t]).then_inc(dft_loaded[t % 2], 16)

                @block.tensor
                def _(pe):
                    pe.wait_ge(small_loaded, 16 * 7)
                    for layer in range(2):
                        if layer:
                            pe.wait_ge(sin_ready, 1)
                        for c in range(NC):
                            mm = nc.tensor.matmul(g.ps[0:HY_FFN, c, 0:CH], w2[:] if layer else w1[:],
                                                  (hid if layer else zT)[:, c * CH:(c + 1) * CH], start=True, stop=True)
                        mm.then_inc(layer_ready, 1)
                    pe.wait_ge(sin_ready, 2)
                    for t in range(NL):
                        wait(pe, fb_ready, t - 1)
                        nc.tensor.matmul(g.ps[:, 2 + t % 2, :], hid[:, t * P:(t + 1) * P], w3[:], start=True, stop=True).then_inc(filt_ready, 1)
                    pe.wait_ge(kpm_ready, NL)
                    for t in range(NL):
                        pe.wait_ge(dft_loaded[t % 2], 32 * (t // 2 + 1))
                        wait(pe, spec_taken, t - 1)
                        for i in range(2):
                            for j in range(NL):
                                mm = nc.tensor.matmul(g.ps[:, 4 + 2 * (t % 2) + i, 0:HY_CH], dft[:, t % 2, i, j, :], kpm[:, i, j, :],
                                                      start=j == 0, stop=j == NL - 1)
                        mm.then_inc(spec_ready, 1)

                @block.scalar
                def _(act):
                    for layer in range(2):
                        act.wait_ge(sin_in, layer + 1)
                        nc.scalar.activation(hid[:], arg[:], ACT.Sin).then_inc(sin_ready, 1)

                @block.vector
                def _(dve):
                    link = Chain(dve, arg_step)
                    dve.wait_ge(small_loaded, 16 * 7)
                    for layer in range(2):
                        dve.wait_ge(layer_ready, layer + 1)
                        link(nc.vector.tensor_scalar(arg[:].rearrange("p (c n) -> p c n", c=NC), g.ps[0:HY_FFN, 0:NC, 0:CH],
                                                     cols[:, layer:layer + 1], cols[:, 2:3], ALU.add, ALU.mult))
                        link(nc.vector.tensor_scalar(rnd[:], arg[:], 1.0 / (2 * math.pi), MAGIC, ALU.mult, ALU.add))
                        link(nc.vector.tensor_scalar(rnd[:], rnd[:], -MAGIC, None, ALU.add))
                        for part in TWO_PI_PARTS:
                            link(nc.vector.scalar_tensor_tensor(out=arg[:], in0=rnd[:], scalar=-part, in1=arg[:],
                                                                op0=ALU.mult, op1=ALU.add))
                        nc.vector.tensor_scalar(arg[:], arg[:], PI_DOWN, -PI_DOWN, ALU.min, ALU.max).then_inc(sin_in, 1)
                    for t in range(NL):
                        dve.wait_ge(filt_ready, t + 1)
                        dve.wait_ge(dec_loaded[t % 2], 16 * (t // 2 + 1))
                        wait(dve, kpm_ready, t - 1)
                        nc.vector.tensor_tensor(fb[:, t % 2], g.ps[:, 2 + t % 2, :], dec[:, t % 2], ALU.mult).then_inc(fb_ready, 1)
                        dve.wait_ge(fb_ready, t + 1)
                        nc.vector.tensor_tensor(kpm[:, 0, t], fb[:, t % 2, 0:HY_CH], fb[:, t % 2, HY_CH:], ALU.add)
                        nc.vector.tensor_tensor(kpm[:, 1, t], fb[:, t % 2, 0:HY_CH], fb[:, t % 2, HY_CH:], ALU.subtract).then_inc(kpm_ready, 1)
                    for t in range(NL):
                        dve.wait_ge(spec_ready, t + 1)
                        b = 4 + 2 * (t % 2)
                        nc.vector.tensor_copy(Kf[:, t, 0:2 * HY_CH].rearrange("p (i n) -> p i n", i=2), g.ps[:, b:b + 2, 0:HY_CH])
                        nc.vector.tensor_copy(Kf[:, t, 2 * HY_CH:], g.ps[:, b, 0:HY_CH]).then_inc(spec_taken, 1)
        hb = st.sb("hb", [P, 2])
        with ExitStack() as early:
            def sb(name, shape):
                return early.enter_context(nc.sbuf_tensor(f"{name}_{st.tag}", shape, F32))
            w = sb("w", [P, KD, HY_IN])
            raw = sb("raw", [P, 2, L + 2])
            u1 = sb("u1", [P, L])
            cw = sb("cw", [P, 6, 3])
            names = ("w_in_loaded cw_loaded padded proj_ready proj_taken conv_step tile_ready gv_turned gt_ready").split()
            w_in_loaded, cw_loaded, padded, proj_ready, proj_taken, conv_step, tile_ready, gv_turned, gt_ready = (st.sem(n) for n in names)
            order = [0, 1, 2, 4, 3, 5]
            with nc.Block() as block:
                @block.sync
                def _(sp):
                    sp.dma_start(w[:], g.w_in[l].rearrange("(k p) n -> p k n", p=P)[:, :, 0:HY_IN]).then_inc(w_in_loaded, 16)
                    with nc.allow_non_contiguous_dma("filter taps, once a layer"):
                        for i in range(3):
                            sp.dma_start(cw[:, :, i], g.hy_conv[l, i].rearrange("(f p) -> p f", p=P)).then_inc(cw_loaded, 16)
                        sp.dma_start(hb[:], g.hy_bias[l].rearrange("(f p) -> p f", p=P)).then_inc(cw_loaded, 16)

                @block.gpsimd
                def _(pool):
                    pool.memset(raw[:, :, 0:1], 0.0)
                    pool.memset(raw[:, :, L + 1:L + 2], 0.0).then_inc(padded, 1)

                @block.tensor
                def _(pe):
                    pe.wait_ge(w_in_loaded, 16)
                    n = 0
                    for f in order:
                        for c in range(NC):
                            wait(pe, proj_taken, n - 3)
                            for k in range(KD):
                                mm = nc.tensor.matmul(g.ps[:, n % 4, 0:CH], w[:, k, f * P:(f + 1) * P],
                                                      g.hT[:, k, tok0 + c * CH:tok0 + (c + 1) * CH], start=k == 0, stop=k == KD - 1)
                            mm.then_inc(proj_ready, 1)
                            n += 1
                    for ct in range(2):
                        pe.wait_ge(tile_ready, 4 + 2 * ct)
                        for t0 in range(0, NL, 4):
                            m = ct * ((NL + 3) // 4) + t0 // 4
                            wait(pe, gt_ready, m - 1)
                            for t in range(t0, min(t0 + 4, NL)):
                                mm = nc.tensor.transpose(g.ps[:, 4 + m % 2, (t - t0) * P:(t - t0 + 1) * P],
                                                         gv[:, ct, t * P:(t + 1) * P], g.ident[:])
                            mm.then_inc(gv_turned, 1)

                @block.scalar
                def _(act):
                    n = 0
                    for j, f in enumerate(order):
                        wait(act, tile_ready, j - 1)
                        for c in range(NC):
                            act.wait_ge(proj_ready, n + 1)
                            nc.scalar.copy(raw[:, j % 2, 1 + c * CH:1 + (c + 1) * CH], g.ps[:, n % 4, 0:CH]).then_inc(proj_taken, 1)
                            n += 1
                    m = 0
                    for ct in range(2):
                        for t0 in range(0, NL, 4):
                            nt = min(4, NL - t0)
                            act.wait_ge(gv_turned, m + 1)
                            nc.scalar.copy(gT[:, t0:t0 + nt, ct * P:(ct + 1) * P],
                                           g.ps[:, 4 + m % 2, 0:nt * P].rearrange("p (t n) -> p t n", n=P)).then_inc(gt_ready, 1)
                            m += 1

                @block.vector
                def _(dve):
                    link = Chain(dve, conv_step)
                    dve.wait_ge(padded, 1)
                    dve.wait_ge(cw_loaded, 64)
                    for j, f in enumerate(order):
                        dve.wait_ge(proj_taken, NC * (j + 1))
                        dst = x0[:, f] if f < 2 else (gv[:, f % 2] if f < 4 else u1[:])
                        r = raw[:, j % 2]
                        link(nc.vector.tensor_scalar(dst, r[:, 0:L], cw[:, f, 0:1], None, ALU.mult))
                        link(nc.vector.scalar_tensor_tensor(out=dst, in0=r[:, 1:L + 1], scalar=cw[:, f, 1:2], in1=dst, op0=ALU.mult, op1=ALU.add))
                        last = nc.vector.scalar_tensor_tensor(out=dst, in0=r[:, 2:L + 2], scalar=cw[:, f, 2:3], in1=dst, op0=ALU.mult, op1=ALU.add)
                        if f < 4:
                            last.then_inc(tile_ready, 1)
                        else:
                            link(last)
                            nc.vector.tensor_tensor(gv[:, f % 2], gv[:, f % 2], u1[:], ALU.mult).then_inc(tile_ready, 1)
                        if f >= 2:
                            dve.wait_ge(tile_ready, j + 1)
        dft2 = st.sb("dft2", [P, 2, 2, NL, P])
        Y = st.sb("Y", [P, 2, NL, HY_CH])
        prod = st.sb("prod", [P, 2, 2, 2 * HY_CH])
        zb = st.sb("zb", [P, 2, L])
        names = "u_ready prod_ready y_ready inv_ready z_step".split()
        u_ready, prod_ready, y_ready, inv_ready, z_step = (st.sem(n) for n in names)
        dft2_loaded = [st.sem(f"dft2_loaded{i}") for i in range(2)]
        with nc.Block() as block:
            @block.sync
            def _(sp):
                for t in range(NL):
                    wait(sp, u_ready, t - 1)
                    for i in range(2):
                        sp.dma_start(dft2[:, t % 2, i], t_dft2[i, t]).then_inc(dft2_loaded[t % 2], 16)
                for t in range(NL):
                    wait(sp, u_ready, NL)
                    wait(sp, inv_ready, t - 1)
                    for i in range(2):
                        sp.dma_start(dft2[:, t % 2, i], g.hy_rows[ctx][i, t * P:(t + 1) * P, :].rearrange("p (j n) -> p j n", n=P)).then_inc(dft2_loaded[t % 2], 16)

            @block.tensor
            def _(pe):
                for t in range(NL):
                    pe.wait_ge(dft2_loaded[t % 2], 32 * (t // 2 + 1))
                    wait(pe, prod_ready, t - 1)
                    for i in range(2):
                        for j in range(NL):
                            mm = nc.tensor.matmul(g.ps[:, t % 2, i * HY_CH:(i + 1) * HY_CH], dft2[:, t % 2, i, j, :], gT[:, j, :],
                                                  start=j == 0, stop=j == NL - 1)
                    mm.then_inc(u_ready, 1)
                for t in range(NL):
                    pe.wait_ge(dft2_loaded[t % 2], 32 * ((NL + t) // 2 + 1))
                    pe.wait_ge(y_ready, NL)
                    for ct in range(2):
                        for c in range(NC):
                            for i in range(2):
                                mm = nc.tensor.matmul(g.ps[:, 4 + 2 * ct + c, 0:CH], Y[:, i, t, ct * P:(ct + 1) * P],
                                                      dft2[:, t % 2, i].rearrange("p j n -> p (j n)")[:, c * CH:(c + 1) * CH],
                                                      start=t == 0 and i == 0, stop=t == NL - 1 and i == 1)
                    mm.then_inc(inv_ready, 1)

            @block.vector
            def _(dve):
                for t in range(NL):
                    dve.wait_ge(u_ready, t + 1)
                    wait(dve, y_ready, t - 1)
                    nc.vector.tensor_tensor(prod[:, t % 2, 0], g.ps[:, t % 2, :], Kf[:, t, 0:2 * HY_CH], ALU.mult)
                    nc.vector.tensor_tensor(prod[:, t % 2, 1], g.ps[:, t % 2, :], Kf[:, t, HY_CH:], ALU.mult).then_inc(prod_ready, 1)
                    dve.wait_ge(prod_ready, t + 1)
                    nc.vector.tensor_tensor(Y[:, 0, t], prod[:, t % 2, 0, 0:HY_CH], prod[:, t % 2, 0, HY_CH:], ALU.subtract)
                    nc.vector.tensor_tensor(Y[:, 1, t], prod[:, t % 2, 1, 0:HY_CH], prod[:, t % 2, 1, HY_CH:], ALU.add).then_inc(y_ready, 1)
                link = Chain(dve, z_step)
                for ct in range(2):
                    link(nc.vector.tensor_scalar(zb[:, ct], gv[:, ct], hb[:, ct:ct + 1], None, ALU.mult))
                dve.wait_ge(inv_ready, NL)
                for ct in range(2):
                    z = zb[:, ct].rearrange("p (c n) -> p c n", c=NC)
                    link(nc.vector.scalar_tensor_tensor(out=z, in0=g.ps[:, 4 + 2 * ct:4 + 2 * ct + NC, 0:CH], scalar=1.0 / L, in1=z,
                                                        op0=ALU.mult, op1=ALU.add))
                    link(nc.vector.tensor_tensor(g.yT[:, ct, tok0:tok0 + L], zb[:, ct], x0[:, ct], ALU.mult))


TWO_PI_PARTS = [6.28125, 2 * math.pi - 6.28125]
PI_DOWN = float(np.nextafter(np.float32(math.pi), np.float32(0)))


def project(nc, g, st, tag, load, loads, groups):
    names = "w_loaded group_ready dve_took act_took".split()
    w_loaded, group_ready, dve_took, act_took = (st.sem(f"{n}_{tag}") for n in names)
    took = (dve_took, act_took)
    with nc.Block() as block:
        @block.sync
        def _(sp):
            load(sp, w_loaded)

        @block.tensor
        def _(pe):
            pe.wait_ge(w_loaded, 16 * loads)
            for n, (products, dst, view) in enumerate(groups):
                wait(pe, took[n % 2], n // 2 - 1)
                for c0, width, lhs, rhs in products:
                    for k in range(KD):
                        mm = nc.tensor.matmul(g.ps[:, n % 4, c0:c0 + width], lhs(k), rhs(k), start=k == 0, stop=k == KD - 1)
                mm.then_inc(group_ready, 1)

        @block.vector
        def _(dve):
            for n in range(0, len(groups), 2):
                dve.wait_ge(group_ready, n + 1)
                nc.vector.tensor_copy(groups[n][1], groups[n][2](g.ps[:, n % 4, :])).then_inc(dve_took, 1)

        @block.scalar
        def _(act):
            for n in range(1, len(groups), 2):
                act.wait_ge(group_ready, n + 1)
                nc.scalar.copy(groups[n][1], groups[n][2](g.ps[:, n % 4, :])).then_inc(act_took, 1)


def feature_groups(g, dsts, lhs):
    return [([(0, n, lambda k, f=f: lhs(f, k), lambda k, c0=c0, n=n: g.hT[:, k, c0:c0 + n])],
             dst[:, c0:c0 + n], lambda bank, n=n: bank[:, 0:n])
            for f, dst in enumerate(dsts) for c0, n in CHUNKS]


def token_groups(g, dst, width, rhs):
    per = BANK // width
    out = []
    for t0 in range(0, NT, per):
        ts = range(t0, min(t0 + per, NT))
        out.append(([((t - t0) * width, width, lambda k, t=t: g.hT[:, k, t * P:(t + 1) * P], rhs) for t in ts],
                    dst[:, t0:t0 + len(ts), :],
                    lambda bank, m=len(ts): bank[:, 0:m * width].rearrange("p (t n) -> p t n", n=width)))
    return out


class Job:

    def __init__(self, q, scores, soft, values, sink=None):
        self.q, self.scores, self.soft, self.values, self.sink = q, scores, soft, values, sink
        self.cols = soft[-1][1]
        self.lo = min(4, len(values) - 1)


def attend(nc, g, st, jobs, out_tiles, scale):
    NJ = len(jobs)
    width = max(j.cols for j in jobs) + 1
    NPT = max(len(j.values) for j in jobs)
    S = st.sb("S", [P, 2, width])
    PR = st.sb("PR", [P, 2, width])
    PT = st.sb("PT", [P, 2, NPT, P])
    mx = st.sb("mx", [P, 2, 4])
    sums = st.sb("sums", [P, 2, 4])
    inv = st.sb("inv", [P, 4])
    on = st.sb("on", [P, 2, 2 * P])
    names = ("scores_ready soft_ready sink_put max_step exp_ready turned_lo turned_hi copied_lo copied_hi "
             "pv_ready inv_ready normed out_turned out_put").split()
    (scores_ready, soft_ready, sink_put, max_step, exp_ready, turned_lo, turned_hi, copied_lo, copied_hi,
     pv_ready, inv_ready, normed, out_turned, out_put) = (st.sem(n) for n in names)
    with nc.Block() as block:
        @block.tensor
        def _(pe):
            def scores(j):
                wait(pe, soft_ready, j - 1)
                for c0, k, n in jobs[j].scores:
                    bank = 2 * (j % 2) + c0 // BANK
                    mm = nc.tensor.matmul(g.ps[:, bank, c0 % BANK:c0 % BANK + n], jobs[j].q, k, start=True, stop=True)
                mm.then_inc(scores_ready, 1)

            def turn(j):
                pe.wait_ge(exp_ready, j + 1)
                wait(pe, copied_lo, j)
                wait(pe, copied_hi, j)
                lo = jobs[j].lo
                for i, (c0, n, _) in enumerate(jobs[j].values):
                    at = (i if i < lo else i - lo) * P
                    mm = nc.tensor.transpose(g.ps[0:n, 4 if i < lo else 5, at:at + P], PR[:, j % 2, c0:c0 + n], g.ident[:])
                    if i == lo - 1:
                        mm.then_inc(turned_lo, 1)
                mm.then_inc(turned_hi, 1)

            def weigh(j):
                pe.wait_ge(copied_lo, j + 1)
                pe.wait_ge(copied_hi, j + 1)
                if j % 4 == 0:
                    wait(pe, normed, j // 4)
                vals = jobs[j].values
                for i, (c0, n, v) in enumerate(vals):
                    mm = nc.tensor.matmul(g.ps[:, 6, (j % 4) * HD:(j % 4 + 1) * HD], PT[0:n, j % 2, i, :], v,
                                          start=i == 0, stop=i == len(vals) - 1)
                mm.then_inc(pv_ready, 1)
                if j % 4 == 3:
                    b = j // 4
                    pe.wait_ge(normed, b + 1)
                    wait(pe, out_put, b)
                    for i in range(2):
                        mm = nc.tensor.transpose(g.ps[:, 7, i * P:(i + 1) * P], on[:, b % 2, i * P:(i + 1) * P], g.ident[:])
                    mm.then_inc(out_turned, 1)

            scores(0)
            for j in range(NJ):
                if j + 1 < NJ:
                    scores(j + 1)
                turn(j)
                if j >= 1:
                    weigh(j - 1)
            weigh(NJ - 1)

        @block.vector
        def _(dve):
            link = Chain(dve, max_step)

            def soft(j):
                job = jobs[j]
                dve.wait_ge(scores_ready, j + 1)
                wait(dve, exp_ready, j - 1)
                if job.sink is not None:
                    nc.vector.tensor_copy(S[:, j % 2, job.cols:job.cols + 1], job.sink).then_inc(sink_put, 1)
                flat = g.ps[:, 2 * (j % 2):2 * (j % 2) + 2, :].rearrange("p b n -> p (b n)")
                for i, (a, b, addend) in enumerate(job.soft):
                    first = -3e38 if job.sink is None else job.sink
                    link(nc.vector.tensor_tensor_reduce(S[:, j % 2, a:b], flat[:, a:b], addend, scale,
                                                        mx[:, j % 2, i - 1:i] if i else first, ALU.add, ALU.max,
                                                        mx[:, j % 2, i:i + 1]))
                i = len(job.soft) - 1
                nc.vector.tensor_scalar(mx[:, j % 2, 3:4], mx[:, j % 2, i:i + 1], -1.0, None, ALU.mult).then_inc(soft_ready, 1)

            def copy(j):
                dve.wait_ge(turned_lo, j + 1)
                wait(dve, pv_ready, j - 1)
                m = jobs[j].lo
                nc.vector.tensor_copy(PT[:, j % 2, 0:m, :], g.ps[:, 4, 0:m * P].rearrange("p (i n) -> p i n", n=P)).then_inc(copied_lo, 1)

            def norm(b):
                dve.wait_ge(exp_ready, 4 * b + 4)
                wait(dve, inv_ready, b)
                nc.vector.reciprocal(inv[:], sums[:, b % 2, :]).then_inc(inv_ready, 1)
                dve.wait_ge(inv_ready, b + 1)
                dve.wait_ge(pv_ready, 4 * b + 4)
                wait(dve, out_turned, b - 1)
                nc.vector.tensor_tensor(on[:, b % 2, :].rearrange("p (h n) -> p h n", h=4),
                                        g.ps[:, 6, 0:4 * HD].rearrange("p (h n) -> p h n", h=4),
                                        inv[:].unsqueeze(2).to_broadcast([P, 4, HD]), ALU.mult).then_inc(normed, 1)

            for j in range(NJ + 1):
                if j < NJ:
                    soft(j)
                if j >= 1:
                    copy(j - 1)
                if j >= 2 and (j - 2) % 4 == 3:
                    norm((j - 2) // 4)
            norm(NJ // 4 - 1)

        @block.scalar
        def _(act):
            def exp(j):
                job = jobs[j]
                act.wait_ge(soft_ready, j + 1)
                if job.sink is not None:
                    act.wait_ge(sink_put, j + 1)
                wait(act, turned_lo, j - 1)
                wait(act, turned_hi, j - 1)
                if j % 4 == 0:
                    wait(act, inv_ready, j // 4 - 1)
                n = job.cols + (job.sink is not None)
                nc.scalar.activation(PR[:, j % 2, 0:n], S[:, j % 2, 0:n], ACT.Exp, bias=mx[:, j % 2, 3:4],
                                     accum_out=sums[:, (j // 4) % 2, j % 4:j % 4 + 1]).then_inc(exp_ready, 1)

            def copy(j):
                act.wait_ge(turned_hi, j + 1)
                wait(act, pv_ready, j - 1)
                vals = jobs[j].values
                lo, full = jobs[j].lo, sum(n == P for _, n, _ in vals)
                m = full - lo
                last = nc.scalar.copy(PT[:, j % 2, lo:full, :], g.ps[:, 5, 0:m * P].rearrange("p (i n) -> p i n", n=P)) if m else None
                if full < len(vals):
                    n = vals[-1][1]
                    last = nc.scalar.copy(PT[0:n, j % 2, full, :], g.ps[0:n, 5, m * P:(m + 1) * P])
                last.then_inc(copied_hi, 1)

            def put(b):
                f, tok = out_tiles[b]
                act.wait_ge(out_turned, b + 1)
                nc.scalar.copy(g.yT[:, f:f + 2, tok:tok + P], g.ps[:, 7, 0:2 * P].rearrange("p (f n) -> p f n", f=2)).then_inc(out_put, 1)

            for j in range(NJ):
                exp(j)
                if j >= 1:
                    copy(j - 1)
                if j >= 8 and j % 4 == 0:
                    put(j // 4 - 2)
            copy(NJ - 1)
            for b in range(max(0, (NJ - 1) // 4 - 1), NJ // 4):
                put(b)


def stage_window(nc, g, l, ctx):
    with Stage(nc, f"wa{l}") as st:
        qk = st.sb("qk", [P, 3, TOK])
        v = st.sb("v", [P, NT, P])
        mask = st.sb("mask", [P, CTX + 3 * P])
        sinks = st.sb("sinks", [P, 4])
        zero = st.sb("zero", [P, CTX])
        small_loaded = st.sem("small_loaded")
        with ExitStack() as early:
            w = early.enter_context(nc.sbuf_tensor(f"w_{st.tag}", [P, KD, WA_IN], F32))

            def load(sp, w_loaded):
                wv = g.w_in[l].rearrange("(k p) n -> p k n", p=P)[:, :, WA0:WA0 + WA_IN]
                for h in range(4):
                    to = (h % 2 * 2 + h // 2) * HD
                    sp.dma_start(w[:, :, to:to + HD], wv[:, :, h * HD:(h + 1) * HD]).then_inc(w_loaded, 16)
                sp.dma_start(w[:, :, 256:], wv[:, :, 256:]).then_inc(w_loaded, 16)
                sp.dma_start(mask[:], g.t_wa_mask).then_inc(small_loaded, 16)
                sp.dma_start(sinks[:], g.wa_sink[l].rearrange("(o n) -> o n", o=1).to_broadcast([P, 4])).then_inc(small_loaded, 16)
                sp.wait_ge(small_loaded, 32)

            project(nc, g, st, "p", load, 5,
                    feature_groups(g, [qk[:, f] for f in range(3)], lambda f, k: w[:, k, f * P:(f + 1) * P]) + token_groups(g, v, P, lambda k: w[:, k, 384:512]))
        with ExitStack() as early:
            rope = early.enter_context(nc.sbuf_tensor(f"rope_{st.tag}", [P, 2, SEQ], F32))
            rot = early.enter_context(nc.sbuf_tensor(f"rot_{st.tag}", [P, P], F32))
            tmp = early.enter_context(nc.sbuf_tensor(f"tmp_{st.tag}", [P, 2, BANK], F32))
            rope_loaded, rotated, tmp_ready, scaled, roped = (st.sem(n) for n in "rope_loaded rotated tmp_ready scaled roped".split())
            spans = [(f, c) for f in range(3) for c in range(2)]
            with nc.Block() as block:
                @block.sync
                def _(sp):
                    sp.dma_start(rope[:], g.t_rope.rearrange("i p n -> p i n")).then_inc(rope_loaded, 16)
                    sp.dma_start(rot[:], g.t_rot).then_inc(rope_loaded, 16)

                @block.gpsimd
                def _(pool):
                    pool.memset(zero[:], 0.0)

                @block.tensor
                def _(pe):
                    pe.wait_ge(rope_loaded, 32)
                    for n, (f, c) in enumerate(spans):
                        wait(pe, tmp_ready, n - 1)
                        nc.tensor.matmul(g.ps[:, n % 2, :], rot[:], qk[:, f, c * BANK:(c + 1) * BANK], start=True, stop=True).then_inc(rotated, 1)

                @block.vector
                def _(dve):
                    dve.wait_ge(rope_loaded, 32)
                    for n, (f, c) in enumerate(spans):
                        cols = slice(c * BANK, (c + 1) * BANK)
                        dve.wait_ge(rotated, n + 1)
                        wait(dve, roped, n - 1)
                        nc.vector.tensor_tensor(tmp[:, n % 2], g.ps[:, n % 2, :], rope[:, 1, cols], ALU.mult).then_inc(tmp_ready, 1)
                        nc.vector.tensor_tensor(qk[:, f, cols], qk[:, f, cols], rope[:, 0, cols], ALU.mult).then_inc(scaled, 1)
                        dve.wait_ge(tmp_ready, n + 1)
                        dve.wait_ge(scaled, n + 1)
                        nc.vector.tensor_tensor(qk[:, f, cols], qk[:, f, cols], tmp[:, n % 2], ALU.add).then_inc(roped, 1)
        jobs, outs = [], []
        for t in range(NTL + (NTC if ctx else 0)):
            for grp in range(2):
                for r in range(2):
                    half = slice(grp * HD, (grp + 1) * HD)
                    q = qk[half, r, t * P:(t + 1) * P]
                    key, dv = qk[half, 2], slice(grp * HD, (grp + 1) * HD)
                    scores = [(0, key[:, SEQ:TOK], CTX)]
                    values = [(i * P, P, v[:, NTL + i, dv]) for i in range(NTC)]
                    m0, cols = CTX, CTX
                    if t < NTL:
                        lo, hi = max(t - 1, 0), min(t + 2, NTL)
                        m0 = CTX + (lo - (t - 1)) * P
                        for i, u in enumerate(range(lo, hi)):
                            scores.append((CTX + i * P, key[:, u * P:(u + 1) * P], P))
                            values.append((CTX + i * P, P, v[:, u, dv]))
                        cols = CTX + (hi - lo) * P
                    h = 2 * grp + r
                    if m0 == CTX:
                        soft = [(0, cols, mask[:, 0:cols])] if t < NTL else [(0, CTX, zero[:])]
                    else:
                        soft = [(0, CTX, zero[:]), (CTX, cols, mask[:, m0:m0 + cols - CTX])]
                    jobs.append(Job(q, scores, soft, values, sinks[:, h:h + 1]))
            outs.append((2, t * P))
        attend(nc, g, st, jobs, outs, SCALE)


def stage_neighbour(nc, g, l, ctx):
    NR = 2 * NA_KR - 1
    NB = 2 * NA_KR
    with Stage(nc, f"na{l}") as st:
        qk = st.sb("qk", [P, 4, TOK])
        v = st.sb("v", [P, NT, 2 * P])
        bias = st.sb("bias", [P, 4, NB, GRID_W])
        inner = st.sb("inner", [P, 4, NA_KR + 1, GRID_W])
        zero = st.sb("zero", [P, CTX])
        with ExitStack() as early:
            sel = early.enter_context(nc.sbuf_tensor(f"sel_{st.tag}", [32, GRID_W * P], F32))
            rpb = early.enter_context(nc.sbuf_tensor(f"rpb_{st.tag}", [4 * NR, 2 * NA_KC - 1], F32))
            rpbT = early.enter_context(nc.sbuf_tensor(f"rpbT_{st.tag}", [32, 4 * NR], F32))
            names = "sel_loaded rpb_turned rpb_filled rpb_ready bias_ready bias_taken cleared copied".split()
            sel_loaded, rpb_turned, rpb_filled, rpb_ready, bias_ready, bias_taken, cleared, copied = (st.sem(n) for n in names)
            with nc.Block() as block:
                @block.sync
                def _(sp):
                    sp.dma_start(rpb[:], g.na_rpb[l].rearrange("h r c -> (h r) c")).then_inc(sel_loaded, 16)
                    sp.dma_start(sel[:], g.t_na_sel).then_inc(sel_loaded, 16)

                @block.gpsimd
                def _(pool):
                    pool.memset(zero[:], 0.0).then_inc(cleared, 1)
                    pool.memset(rpbT[:], NEG).then_inc(rpb_filled, 1)

                @block.tensor
                def _(pe):
                    pe.wait_ge(sel_loaded, 32)
                    nc.tensor.transpose(g.ps[0:31, 4, 0:4 * NR], rpb[:], g.ident[0:4 * NR, 0:4 * NR]).then_inc(rpb_turned, 1)
                    pe.wait_ge(rpb_ready, 1)
                    for n in range(8):
                        wait(pe, bias_taken, n - 1)
                        for i in range(8):
                            ck = 8 * n + i
                            mm = nc.tensor.matmul(g.ps[:, n % 2, i * 4 * NR:(i + 1) * 4 * NR], sel[:, ck * P:(ck + 1) * P], rpbT[:],
                                                  start=True, stop=True)
                        mm.then_inc(bias_ready, 1)

                @block.vector
                def _(dve):
                    dve.wait_ge(rpb_filled, 1)
                    dve.wait_ge(rpb_turned, 1)
                    nc.vector.tensor_scalar(rpbT[0:31, :], g.ps[0:31, 4, 0:4 * NR], 1.0 / SCALE, None, ALU.mult).then_inc(rpb_ready, 1)
                    for n in range(8):
                        dve.wait_ge(bias_ready, n + 1)
                        for rr in range(2):
                            half = slice(rr * HD, (rr + 1) * HD)
                            for h in range(4):
                                src = g.ps[half, n % 2, 0:32 * NR].rearrange("p (c h r) -> p h r c", h=4, r=NR)[:, h]
                                last = nc.vector.tensor_copy(bias[half, h, rr:rr + NR, 8 * n:8 * n + 8], src)
                        last.then_inc(bias_taken, 1)
                    dve.wait_ge(bias_taken, 8)
                    for rr in range(2):
                        half = slice(rr * HD, (rr + 1) * HD)
                        nc.vector.tensor_copy(inner[half, :, rr:rr + NA_KR, :], bias[half, :, 3 + rr:3 + rr + NA_KR, :])
                        edge = NA_KR if rr == 0 else 0
                        last = nc.vector.memset(inner[half, :, edge:edge + 1, :], NEG)
        with ExitStack() as early:
            w = early.enter_context(nc.sbuf_tensor(f"w_{st.tag}", [P, KD, NA_IN], F32))

            def load(sp, w_loaded):
                sp.dma_start(w[:], g.w_in[l].rearrange("(k p) n -> p k n", p=P)[:, :, NA0:NA0 + NA_IN]).then_inc(w_loaded, 16)

            project(nc, g, st, "p", load, 1,
                    feature_groups(g, [qk[:, f] for f in range(4)], lambda f, k: w[:, k, f * P:(f + 1) * P])
                    + token_groups(g, v, 2 * P, lambda k: w[:, k, 512:768]))
        jobs, outs = [], []
        for t in range(NTL + (NTC if ctx else 0)):
            for h in range(4):
                half = slice(h % 2 * HD, (h % 2 + 1) * HD)
                dv = slice(h * HD, (h + 1) * HD)
                q = qk[half, h // 2, t * P:(t + 1) * P]
                key = qk[half, 2 + h // 2]
                scores = [(0, key[:, SEQ:TOK], CTX)]
                values = [(i * P, P, v[:, NTL + i, dv]) for i in range(NTC)]
                soft = [(0, CTX, zero[:])]
                if t < NTL:
                    first = min(max(2 * t - NA_KR // 2, 0), SEQ // GRID_W - NA_KR)
                    last = min(max(2 * t + 1 - NA_KR // 2, 0), SEQ // GRID_W - NA_KR)
                    rows = last - first + NA_KR
                    k0, n = first * GRID_W, rows * GRID_W
                    scores += [(CTX, key[:, k0:k0 + CTX], CTX), (BANK, key[:, k0 + CTX:k0 + n], n - CTX)]
                    for i in range(0, n, P):
                        m = min(P, n - i)
                        values.append((CTX + i, m, v[0:m, (k0 + i) // P, dv]))
                    b = first - 2 * t + NA_KR - 1
                    table = inner[:, h] if rows > NA_KR else bias[:, h, b:b + NA_KR, :]
                    soft.append((CTX, CTX + n, table.rearrange("p r c -> p (r c)")))
                jobs.append(Job(q, scores, soft, values))
            outs.append((4, t * P))
        attend(nc, g, st, jobs, outs, SCALE)


def stage_gdn(nc, g, l):
    C = 64
    FW = 4 * C
    GV = 7
    SEG = SEQ + 3
    with Stage(nc, f"gd{l}") as st:
        qkv = st.sb("qkv", [P, NT, 3 * GW])
        gate = st.sb("gate", [P, NT, GW])
        ab = st.sb("ab", [P, NT, 16])
        with ExitStack() as early:
            def sb(name, shape):
                return early.enter_context(nc.sbuf_tensor(f"{name}_{st.tag}", shape, F32))
            w = sb("w", [P, 2, KD, P])
            wg = sb("wg", [P, KD, GW + 16])
            raw = sb("raw", [P, 2, SEG + CTX + 3])
            u = sb("u", [P, TOK])
            s = sb("s", [P, 2, TOK])
            cw = sb("cw", [P, 6, 4])
            names = "cw_loaded wg_loaded padded proj_ready proj_taken conv_ready silu_ready turned tm_dve tm_act gate_ready gate_taken ab_ready ab_taken conv_step".split()
            (cw_loaded, wg_loaded, padded, proj_ready, proj_taken, conv_ready, silu_ready, turned, tm_dve, tm_act, gate_ready,
             gate_taken, ab_ready, ab_taken, conv_step) = (st.sem(n) for n in names)
            w_loaded = [st.sem(f"w_loaded{i}") for i in range(2)]
            wv = g.w_in[l].rearrange("(k p) n -> p k n", p=P)
            starts = [(2, 0, SEQ), (SEG + 2, SEQ, CTX)]
            TS = [(0, 4), (4, 8), (8, 10)]
            with nc.Block() as block:
                @block.sync
                def _(sp):
                    with nc.allow_non_contiguous_dma("filter taps, once a layer"):
                        for i in range(4):
                            sp.dma_start(cw[:, :, i], g.gdn_conv[l, i].rearrange("(f p) -> p f", p=P)).then_inc(cw_loaded, 16)
                    for f in range(6):
                        wait(sp, proj_ready, 3 * (f - 1))
                        sp.dma_start(w[:, f % 2], wv[:, :, GD0 + f * P:GD0 + (f + 1) * P]).then_inc(w_loaded[f % 2], 16)
                    sp.dma_start(wg[:], wv[:, :, GD0 + 3 * GW:]).then_inc(wg_loaded, 16)

                @block.gpsimd
                def _(pool):
                    pool.memset(raw[:, :, 0:2], 0.0)
                    pool.memset(raw[:, :, SEQ + 2:SEQ + 5], 0.0)
                    pool.memset(raw[:, :, SEG + CTX + 2:SEG + CTX + 3], 0.0).then_inc(padded, 1)

                @block.tensor
                def _(pe):
                    def project_tile(f):
                        pe.wait_ge(w_loaded[f % 2], 16 * (f // 2 + 1))
                        for i, (c0, n) in enumerate(CHUNKS):
                            m = 3 * f + i
                            wait(pe, proj_taken, m - 1)
                            for k in range(KD):
                                mm = nc.tensor.matmul(g.ps[:, m % 2, 0:n], w[:, f % 2, k, :], g.hT[:, k, c0:c0 + n],
                                                      start=k == 0, stop=k == KD - 1)
                            mm.then_inc(proj_ready, 1)

                    def turn_tile(f):
                        pe.wait_ge(silu_ready, f + 1)
                        wait(pe, tm_dve, 2 * f)
                        wait(pe, tm_act, f)
                        for i, (t0, t1) in enumerate(TS):
                            for t in range(t0, t1):
                                mm = nc.tensor.transpose(g.ps[:, 2 + i, (t - t0) * P:(t - t0 + 1) * P],
                                                         s[:, f % 2, t * P:(t + 1) * P], g.ident[:])
                        mm.then_inc(turned, 1)

                    for f in range(6):
                        project_tile(f)
                        if f >= 1:
                            turn_tile(f - 1)
                    turn_tile(5)
                    pe.wait_ge(wg_loaded, 16)
                    for t in range(NT):
                        for k in range(KD):
                            mm = nc.tensor.matmul(g.ps[:, 7, t * 16:(t + 1) * 16], g.hT[:, k, t * P:(t + 1) * P],
                                                  wg[:, k, GW:GW + 16], start=k == 0, stop=k == KD - 1)
                    mm.then_inc(ab_ready, 1)
                    for t in range(NT):
                        wait(pe, gate_taken, t - 1)
                        for k in range(KD):
                            mm = nc.tensor.matmul(g.ps[:, 5 + t % 2, 0:GW], g.hT[:, k, t * P:(t + 1) * P],
                                                  wg[:, k, 0:GW], start=k == 0, stop=k == KD - 1)
                        mm.then_inc(gate_ready, 1)

                @block.scalar
                def _(act):
                    def take(f):
                        wait(act, conv_ready, f - 1)
                        for i, (c0, n) in enumerate(CHUNKS):
                            at = c0 + 2 if c0 < SEQ else SEG + 2
                            act.wait_ge(proj_ready, 3 * f + i + 1)
                            nc.scalar.copy(raw[:, f % 2, at:at + n], g.ps[:, (3 * f + i) % 2, 0:n]).then_inc(proj_taken, 1)

                    def silu(f):
                        act.wait_ge(conv_ready, f + 1)
                        wait(act, turned, f - 1)
                        nc.scalar.activation(s[:, f % 2], u[:], ACT.Silu).then_inc(silu_ready, 1)

                    def place(f):
                        act.wait_ge(turned, f + 1)
                        nc.scalar.copy(qkv[:, 8:10, f * P:(f + 1) * P], g.ps[:, 4, 0:2 * P].rearrange("p (t n) -> p t n", n=P)).then_inc(tm_act, 1)

                    for f in range(6):
                        take(f)
                        if f >= 1:
                            silu(f - 1)
                        if f >= 2:
                            place(f - 2)
                    silu(5)
                    place(4)
                    place(5)
                    for t in range(NT):
                        act.wait_ge(gate_ready, t + 1)
                        nc.scalar.activation(gate[:, t, :], g.ps[:, 5 + t % 2, 0:GW], ACT.Silu).then_inc(gate_taken, 1)

                @block.vector
                def _(dve):
                    link = Chain(dve, conv_step)

                    def conv(f):
                        dve.wait_ge(proj_taken, 3 * f + 3)
                        wait(dve, silu_ready, f)
                        for tap in range(4):
                            for a, c0, n in starts:
                                r = raw[:, f % 2, a - 2 + tap:a - 2 + tap + n]
                                dst = u[:, c0:c0 + n]
                                if tap == 0:
                                    o = nc.vector.tensor_scalar(dst, r, cw[:, f, 0:1], None, ALU.mult)
                                else:
                                    o = nc.vector.scalar_tensor_tensor(out=dst, in0=r, scalar=cw[:, f, tap:tap + 1], in1=dst, op0=ALU.mult, op1=ALU.add)
                                if tap < 3:
                                    link(o)
                        o.then_inc(conv_ready, 1)

                    def place(f):
                        dve.wait_ge(turned, f + 1)
                        for i in range(2):
                            nc.vector.tensor_copy(qkv[:, 4 * i:4 * i + 4, f * P:(f + 1) * P],
                                                  g.ps[:, 2 + i, :].rearrange("p (t n) -> p t n", n=P)).then_inc(tm_dve, 1)

                    dve.wait_ge(padded, 1)
                    dve.wait_ge(cw_loaded, 64)
                    for f in range(6):
                        conv(f)
                        if f >= 2:
                            place(f - 2)
                    place(4)
                    place(5)
                    dve.wait_ge(ab_ready, 1)
                    nc.vector.tensor_copy(ab[:], g.ps[:, 7, 0:NT * 16].rearrange("p (t n) -> p t n", n=16)).then_inc(ab_taken, 1)
        scal = st.sb("scal", [P, NT, 2, GV, 4])
        o_sum = st.sb("o_sum", [P, NT, GW])
        M = {n: st.sb(n, [P] + s) for n, s in g.gdn_masks.items()}
        with ExitStack() as early:
            def sb(name, shape):
                return early.enter_context(nc.sbuf_tensor(f"{name}_{st.tag}", shape, F32))
            cum = sb("cum", [P, 3, P])
            sq = sb("sq", [P, 2, 2 * GW])
            nrm = sb("nrm", [P, NT, 8])
            al = sb("al", [P, 2, 8])
            xs = sb("xs", [P, NT, 8])
            ax = sb("ax", [P, NT, 8])
            names = "masks_loaded al_loaded a_ready al_exp soft_in soft_exp soft_ln ln_in g_ready sums_ready sums_copied decay_ready root_in root_ready l2_step gate_step cleared".split()
            (masks_loaded, al_loaded, a_ready, al_exp, soft_in, soft_exp, soft_ln, ln_in, g_ready, sums_ready, sums_copied, decay_ready,
             root_in, root_ready, l2_step, gate_step, cleared) = (st.sem(n) for n in names)
            with nc.Block() as block:
                @block.sync
                def _(sp):
                    for n in M:
                        sp.dma_start(M[n][:], g.tables[f"t_{n}"]).then_inc(masks_loaded, 16)
                    sp.dma_start(cum[:], g.tables["t_gd_cum"]).then_inc(masks_loaded, 16)
                    for i, src in enumerate((g.gdn_a_log, g.gdn_dt_bias)):
                        sp.dma_start(al[:, i], src[l].rearrange("(o d) h -> o (d h)", o=1).to_broadcast([P, 8])).then_inc(al_loaded, 16)
                    sp.wait_ge(masks_loaded, 16 * (len(M) + 1))

                @block.gpsimd
                def _(pool):
                    pool.memset(o_sum[:], 0.0)

                @block.tensor
                def _(pe):
                    pe.wait_ge(masks_loaded, 16 * (len(M) + 1))
                    pe.wait_ge(g_ready, 1)
                    for d in range(2):
                        gd = scal[:, :, d, 0, :]
                        nc.tensor.matmul(g.ps[:, 0, d * 40:d * 40 + 40], cum[:, d, :], gd, start=True, stop=True)
                        mm = nc.tensor.matmul(g.ps[:, 0, 80 + d * 40:120 + d * 40], cum[:, 2, :], gd, start=True, stop=True)
                    mm.then_inc(sums_ready, 1)

                @block.scalar
                def _(act):
                    act.wait_ge(al_loaded, 32)
                    nc.scalar.activation(al[:, 0], al[:, 0], ACT.Exp).then_inc(al_exp, 1)
                    act.wait_ge(soft_in, 1)
                    nc.scalar.activation(ax[:], ax[:], ACT.Exp).then_inc(soft_exp, 1)
                    nc.scalar.activation(ab[:, :, 8:16], ab[:, :, 8:16], ACT.Exp, scale=-1.0).then_inc(soft_exp, 1)
                    act.wait_ge(ln_in, 1)
                    nc.scalar.activation(ax[:], ax[:], ACT.Ln).then_inc(soft_ln, 1)
                    act.wait_ge(decay_ready, 1)
                    for v in (3, 4, 6):
                        nc.scalar.activation(scal[:, :, :, v, :], scal[:, :, :, v, :], ACT.Exp).then_inc(decay_ready, 1)
                    act.wait_ge(root_in, 1)
                    nc.scalar.activation(nrm[:], nrm[:], ACT.Sqrt).then_inc(root_ready, 1)

                @block.vector
                def _(dve):
                    link = Chain(dve, gate_step)
                    dve.wait_ge(al_loaded, 32)
                    link(nc.vector.tensor_tensor(xs[:], ab[:, :, 0:8], al[:, 1:2, :].to_broadcast([P, NT, 8]), ALU.add))
                    link(nc.vector.tensor_scalar(ax[:], xs[:], -1.0, None, ALU.mult))
                    nc.vector.tensor_tensor(ax[:], ax[:], xs[:], ALU.min).then_inc(soft_in, 1)
                    for t in range(NT):
                        nc.vector.tensor_tensor(sq[:, t % 2], qkv[:, t, 0:2 * GW], qkv[:, t, 0:2 * GW], ALU.mult).then_inc(l2_step, 1)
                        dve.wait_ge(l2_step, t + 1)
                        last = nc.vector.tensor_reduce(nrm[:, t, :], sq[:, t % 2].rearrange("p (h n) -> p h n", h=8), AX.X, ALU.add)
                    link(last)
                    nc.vector.tensor_scalar(nrm[:], nrm[:], EPS, None, ALU.add).then_inc(root_in, 1)
                    dve.wait_ge(soft_exp, 2)
                    nc.vector.tensor_scalar(ax[:], ax[:], 1.0, None, ALU.add).then_inc(ln_in, 1)
                    link(nc.vector.tensor_scalar(ab[:, :, 8:16], ab[:, :, 8:16], 1.0, None, ALU.add))
                    for d in range(2):
                        link(nc.vector.reciprocal(scal[:, :, d, 1, :], ab[:, :, 8 + 4 * d:12 + 4 * d]))
                    link(nc.vector.tensor_scalar(xs[:], xs[:], 0.0, None, ALU.max))
                    dve.wait_ge(soft_ln, 1)
                    dve.wait_ge(al_exp, 1)
                    link(nc.vector.tensor_tensor(xs[:], xs[:], ax[:], ALU.add))
                    for d in range(2):
                        o = nc.vector.scalar_tensor_tensor(out=scal[:, :, d, 0, :], in0=xs[:, :, 4 * d:4 * d + 4], scalar=-1.0,
                                                           in1=al[:, 0:1, 4 * d:4 * d + 4].to_broadcast([P, NT, 4]), op0=ALU.mult, op1=ALU.mult)
                    o.then_inc(g_ready, 1)
                    dve.wait_ge(sums_ready, 1)
                    for d in range(2):
                        gc = g.ps[:, 0, d * 40:d * 40 + 40].rearrange("p (t h) -> p t h", h=4)
                        tot = g.ps[:, 0, 80 + d * 40:120 + d * 40].rearrange("p (t h) -> p t h", h=4)
                        link(nc.vector.tensor_copy(scal[:, :, d, 2, :], gc))
                        nc.vector.tensor_copy(scal[:, :, d, 3, :], gc)
                        link(nc.vector.tensor_copy(scal[:, :, d, 6, :], tot))
                        link(nc.vector.tensor_tensor(scal[:, :, d, 4, :], scal[:, :, d, 6, :], scal[:, :, d, 2, :], ALU.subtract))
                    nc.vector.tensor_copy(al[:, 1, 0:1], al[:, 1, 1:2]).then_inc(decay_ready, 1)
                    dve.wait_ge(decay_ready, 4)
                    link(nc.vector.tensor_tensor(scal[:, :, :, 5, :], scal[:, :, :, 3, :], scal[:, :, :, 1, :], ALU.mult))
                    dve.wait_ge(root_ready, 1)
                    link(nc.vector.reciprocal(nrm[:], nrm[:]))
                    link(nc.vector.tensor_scalar(nrm[:, :, 0:4], nrm[:, :, 0:4], SCALE, None, ALU.mult))
                    for t in range(NT):
                        x = qkv[:, t, 0:2 * GW].rearrange("p (h n) -> p h n", h=8)
                        nc.vector.tensor_tensor(x, x, nrm[:, t, :].unsqueeze(2).to_broadcast([P, 8, C]), ALU.mult)
        gdn_steps(nc, g, st, qkv, scal, o_sum, M)
        sqo = st.sb("sqo", [P, 2, GW])
        no = st.sb("no", [P, NT, 4])
        ng = st.sb("ng", [P, C])
        names = "ng_loaded root_in2 root_ready2 fin_step tile_ready out_turned out_put sq_step".split()
        ng_loaded, root_in2, root_ready2, fin_step, tile_ready, out_turned, out_put, sq_step = (st.sem(n) for n in names)
        with nc.Block() as block:
            @block.sync
            def _(sp):
                sp.dma_start(ng[:], g.gdn_norm[l].rearrange("(o n) -> o n", o=1).to_broadcast([P, C])).then_inc(ng_loaded, 16)

            @block.vector
            def _(dve):
                link = Chain(dve, fin_step)
                for t in range(NT):
                    nc.vector.tensor_tensor(sqo[:, t % 2], o_sum[:, t, :], o_sum[:, t, :], ALU.mult).then_inc(sq_step, 1)
                    dve.wait_ge(sq_step, t + 1)
                    last = nc.vector.tensor_reduce(no[:, t, :], sqo[:, t % 2].rearrange("p (h n) -> p h n", h=4), AX.X, ALU.add)
                link(last)
                nc.vector.tensor_scalar(no[:], no[:], 1.0 / C, EPS, ALU.mult, ALU.add).then_inc(root_in2, 1)
                dve.wait_ge(ng_loaded, 16)
                for t in range(NT):
                    x = gate[:, t, :].rearrange("p (h n) -> p h n", h=4)
                    last = nc.vector.tensor_tensor(x, x, ng[:].unsqueeze(1).to_broadcast([P, 4, C]), ALU.mult)
                link(last)
                dve.wait_ge(root_ready2, 1)
                link(nc.vector.reciprocal(no[:], no[:]))
                for t in range(NT):
                    x = o_sum[:, t, :].rearrange("p (h n) -> p h n", h=4)
                    link(nc.vector.tensor_tensor(x, x, no[:, t, :].unsqueeze(2).to_broadcast([P, 4, C]), ALU.mult))
                    nc.vector.tensor_tensor(o_sum[:, t, :], o_sum[:, t, :], gate[:, t, :], ALU.mult).then_inc(tile_ready, 1)

            @block.scalar
            def _(act):
                act.wait_ge(root_in2, 1)
                nc.scalar.activation(no[:], no[:], ACT.Sqrt).then_inc(root_ready2, 1)
                for t in range(NT):
                    act.wait_ge(out_turned, t + 1)
                    nc.scalar.copy(g.yT[:, 6:8, t * P:(t + 1) * P], g.ps[:, t % 2, 0:2 * P].rearrange("p (f n) -> p f n", f=2)).then_inc(out_put, 1)

            @block.tensor
            def _(pe):
                for t in range(NT):
                    pe.wait_ge(tile_ready, t + 1)
                    wait(pe, out_put, t - 1)
                    for i in range(2):
                        mm = nc.tensor.transpose(g.ps[:, t % 2, i * P:(i + 1) * P], o_sum[:, t, i * P:(i + 1) * P], g.ident[:])
                    mm.then_inc(out_turned, 1)


def gdn_steps(nc, g, st, qkv, scal, o_sum, M):
    C, FW, W2 = 64, 256, 512
    LEVELS = 5
    RS = [slice(0, C), slice(C, P)]

    def sb(name, shape=(2, 4, C)):
        return st.sb(name, [P] + list(shape))

    x3 = st.sb("x3", [P, 2, 3 * FW])
    sc = st.sb("sc", [P, 2, 7, 4])
    glz = st.sb("glz", [P, 2, 4])
    DG, E, kT, qT, L, At, LT, AtT, T, TT, X, tmp, vb, kbe, kd, qd, U, wT, qdT = (
        sb(n) for n in "DG E kT qT L At LT AtT T TT X tmp vb kbe kd qd U wT qdT".split())
    S = st.sb("S", [P, 4, C])
    Sg = st.sb("Sg", [P, 4, C])
    un = st.sb("un", [P, 4, C])
    names = ("gathered scaled dg_ready gj_ready e_in e_ready kt_turned kt_ready qt_turned qt_ready gram_ready qk_ready l_ready at_ready "
             "lt_turned lt_ready att_turned att_ready t_ready x_prod x_ready txt_prod tx_prod t_next u_prod w_prod qd_prod u_ready "
             "wq_ready ws_prod un_ready s_prod s_ready o_prod o_taken waits_met vec_step").split()
    (gathered, scaled, dg_ready, gj_ready, e_in, e_ready, kt_turned, kt_ready, qt_turned, qt_ready, gram_ready, qk_ready, l_ready, at_ready,
     lt_turned, lt_ready, att_turned, att_ready, t_ready, x_prod, x_ready, txt_prod, tx_prod, t_next, u_prod, w_prod, qd_prod, u_ready,
     wq_ready, ws_prod, un_ready, s_prod, s_ready, o_prod, o_taken, waits_met, vec_step) = (st.sem(n) for n in names)

    def all_steps(eng, body):
        body(0, NTL, NTL + 1)
        body(1, NTL + 1, NTL)
        with eng.Fori(0, NTL) as i:
            body(i + 2, i, NTL - 1 - i)

    def dhc():
        return [(d, h, c) for d in range(2) for h in range(4) for c in range(2)]

    ps = g.ps

    def bank(b):
        return ps[:, b, :].rearrange("p (d h n) -> p d h n", d=2, h=4)

    def per_head(a, v):
        return a[:, :, v, :].unsqueeze(3).to_broadcast([P, 2, 4, C])

    def mask(m):
        return m.unsqueeze(2).to_broadcast([P, 2, 4, C])

    with nc.Block() as block:
        @block.tensor
        def _(pe):
            def wait_step(sem, value):
                pe.wait_ge(sem, value)
                pe.sem_inc(waits_met, 1)

            def body(s, a, b):
                def mms(bk, lhs, rhs, z=False, start=True, stop=True):
                    for d, h, c in dhc():
                        col = (d ^ c if z else d) * FW + h * C
                        mm = nc.tensor.matmul(ps[RS[c], bk, col:col + C], lhs(d, h, c), rhs(d, h, c), start=start, stop=stop)
                    return mm

                pe.wait_ge(dg_ready, s + 1)
                nc.tensor.matmul(ps[:, 0, :], M["gd_negblk"][:], DG[:].rearrange("p d h n -> p (d h n)"), start=True, stop=True).then_inc(gj_ready, 1)
                wait_step(gathered, 4 * s + 4)
                eye = lambda d, h, c: M["gd_eye"][RS[c], :]
                mms(1, lambda d, h, c: x3[RS[c], d, FW + h * C:FW + (h + 1) * C], eye).then_inc(kt_turned, 1)
                mms(2, lambda d, h, c: x3[RS[c], d, h * C:(h + 1) * C], eye).then_inc(qt_turned, 1)
                wait_step(kt_ready, s + 1)
                mms(3, lambda d, h, c: kT[RS[c], d, h, :], lambda d, h, c: kT[RS[c], d, h, :]).then_inc(gram_ready, 1)
                wait_step(qt_ready, s + 1)
                mms(4, lambda d, h, c: qT[RS[c], d, h, :], lambda d, h, c: kT[RS[c], d, h, :]).then_inc(qk_ready, 1)
                wait_step(l_ready, s + 1)
                mms(5, lambda d, h, c: L[RS[c], d, h, :], eye).then_inc(lt_turned, 1)
                wait_step(at_ready, s + 1)
                mms(6, lambda d, h, c: At[RS[c], d, h, :], eye, z=True).then_inc(att_turned, 1)
                wait_step(scaled, s + 1)
                mms(7, lambda d, h, c: qd[RS[c], d, h, :], eye, z=True).then_inc(qd_prod, 1)
                for lv in range(LEVELS):
                    wait_step(t_next, s * LEVELS + lv + 1)
                    mms(0, lambda d, h, c: LT[RS[c], d, h, :], lambda d, h, c: T[RS[c], d, h, :]).then_inc(x_prod, 1)
                    wait_step(x_ready, s * LEVELS + lv + 1)
                    mms(1, lambda d, h, c: X[RS[c], d, h, :], lambda d, h, c: TT[RS[c], d, h, :]).then_inc(txt_prod, 1)
                    if lv < LEVELS - 1:
                        mms(2, lambda d, h, c: TT[RS[c], d, h, :], lambda d, h, c: X[RS[c], d, h, :]).then_inc(tx_prod, 1)
                wait_step(t_ready, s + 1)
                mms(3, lambda d, h, c: TT[RS[c], d, h, :], lambda d, h, c: vb[RS[c], d, h, :], z=True).then_inc(u_prod, 1)
                mms(4, lambda d, h, c: kbe[RS[c], d, h, :], lambda d, h, c: TT[RS[c], d, h, :], z=True).then_inc(w_prod, 1)
                wait_step(wq_ready, 2 * s + 2)
                for z in range(2):
                    wait_step(s_ready, 2 * s + z + 1)
                    for h in range(4):
                        for c in range(2):
                            mm = nc.tensor.matmul(ps[RS[c], 0, h * C:(h + 1) * C], wT[RS[c], z, h, :], S[RS[c], h, :], start=True, stop=True)
                    mm.then_inc(ws_prod, 1)
                    wait_step(un_ready, 2 * s + z + 1)
                    for h in range(4):
                        for c in range(2):
                            d = z ^ c
                            mm = nc.tensor.matmul(ps[RS[1 - c], 1, h * C:(h + 1) * C], kd[RS[c], d, h, :], un[RS[c], h, :], start=True, stop=True)
                    mm.then_inc(s_prod, 1)
                    for h in range(4):
                        for c in range(2):
                            col = z * FW + h * C
                            nc.tensor.matmul(ps[RS[c], 2, col:col + C], qdT[RS[c], z, h, :], S[RS[c], h, :], start=True, stop=False)
                            mm = nc.tensor.matmul(ps[RS[c], 2, col:col + C], AtT[RS[c], z, h, :], un[RS[c], h, :], start=False, stop=True)
                    mm.then_inc(o_prod, 1)

            all_steps(pe, body)

        @block.gpsimd
        def _(pool):
            pool.memset(S[:], 0.0).then_inc(s_ready, 1)

            def body(s, a, b):
                pool.wait_ge(gathered, 4 * s + 4)
                wait(pool, o_taken, s)
                q, k, v = (x3[:, :, i * FW:(i + 1) * FW].rearrange("p d (h n) -> p d h n", h=4) for i in range(3))
                nc.gpsimd.tensor_tensor(qd[:], q, per_head(sc, 3), ALU.mult)
                nc.gpsimd.tensor_tensor(vb[:], v, per_head(sc, 1), ALU.mult)
                nc.gpsimd.tensor_tensor(kbe[:], k, per_head(sc, 5), ALU.mult)
                nc.gpsimd.tensor_tensor(kd[:], k, per_head(sc, 4), ALU.mult).then_inc(scaled, 1)

            all_steps(pool, body)

        @block.scalar
        def _(act):
            def body(s, a, b):
                wait(act, o_taken, s)
                wait(act, scaled, s)
                for d, t in ((0, a), (1, b)):
                    nc.scalar.copy(x3[:, d, :], qkv[:, t, :] if isinstance(t, int) else qkv[:, bass.ds(t, 1), :].rearrange("p o n -> p (o n)")).then_inc(gathered, 1)
                    nc.scalar.copy(sc[:, d], scal[:, t, d] if isinstance(t, int) else scal[:, bass.ds(t, 1), d].rearrange("p o v h -> p (o v) h")).then_inc(gathered, 1)
                act.wait_ge(kt_turned, s + 1)
                nc.scalar.copy(kT[:], bank(1)).then_inc(kt_ready, 1)
                act.wait_ge(e_in, s + 1)
                nc.scalar.activation(E[:], E[:], ACT.Exp).then_inc(e_ready, 1)
                act.wait_ge(att_turned, s + 1)
                nc.scalar.copy(AtT[:], bank(6)).then_inc(att_ready, 1)
                act.wait_ge(qd_prod, s + 1)
                nc.scalar.copy(qdT[:], bank(7)).then_inc(wq_ready, 1)
                act.wait_ge(w_prod, s + 1)
                nc.scalar.copy(wT[:], bank(4)).then_inc(wq_ready, 1)

            all_steps(act, body)

        @block.vector
        def _(dve):
            def body(s, a, b):
                V = nc.vector
                n = [0]
                PER = 13

                def link(ins):
                    n[0] += 1
                    ins.then_inc(vec_step, 1)
                    dve.wait_ge(vec_step, s * PER + n[0])

                dve.wait_ge(gathered, 4 * s + 4)
                V.tensor_tensor(DG[:], mask(M["gd_tri"][:]), per_head(sc, 0), ALU.mult).then_inc(dg_ready, 1)
                for c in range(2):
                    for d in range(2):
                        z = c ^ d
                        V.tensor_copy(glz[RS[c], z, :], sc[RS[c], d, 6, :])
                dve.wait_ge(gj_ready, s + 1)
                link(V.tensor_tensor(E[:], bank(0), per_head(sc, 2), ALU.add))
                V.tensor_tensor(E[:], E[:], mask(M["gd_allow"][:]), ALU.min).then_inc(e_in, 1)
                dve.wait_ge(qt_turned, s + 1)
                V.tensor_copy(qT[:], bank(2)).then_inc(qt_ready, 1)
                dve.wait_ge(e_ready, s + 1)
                link(V.tensor_tensor(tmp[:], E[:], per_head(sc, 1), ALU.mult))
                link(V.tensor_tensor(tmp[:], tmp[:], mask(M["gd_strict"][:]), ALU.mult))
                dve.wait_ge(gram_ready, s + 1)
                V.tensor_tensor(L[:], tmp[:], bank(3), ALU.mult).then_inc(l_ready, 1)
                dve.wait_ge(qk_ready, s + 1)
                V.tensor_tensor(At[:], E[:], bank(4), ALU.mult).then_inc(at_ready, 1)
                eye = M["gd_eye"][:].unsqueeze(1).unsqueeze(1).to_broadcast([P, 2, 4, C])
                dve.wait_ge(l_ready, s + 1)
                link(V.tensor_tensor(T[:], L[:], mask(M["gd_lvl"][:, 0]), ALU.mult))
                link(V.tensor_tensor(T[:], eye, T[:], ALU.subtract))
                dve.wait_ge(lt_turned, s + 1)
                link(V.tensor_copy(LT[:], bank(5)))
                link(V.tensor_tensor(TT[:], LT[:], mask(M["gd_lvl"][:, 1]), ALU.mult))
                V.tensor_tensor(TT[:], eye, TT[:], ALU.subtract).then_inc(t_next, 1)
                for lv in range(LEVELS):
                    dve.wait_ge(x_prod, s * LEVELS + lv + 1)
                    V.tensor_tensor(X[:], bank(0), mask(M["gd_lvl"][:, lv + 2]), ALU.mult).then_inc(x_ready, 1)
                    dve.wait_ge(txt_prod, s * LEVELS + lv + 1)
                    dve.wait_ge(t_next, s * LEVELS + lv + 1)
                    if lv == LEVELS - 1:
                        V.tensor_tensor(TT[:], TT[:], bank(1), ALU.subtract).then_inc(t_ready, 1)
                        continue
                    dve.wait_ge(tx_prod, s * (LEVELS - 1) + lv + 1)
                    link(V.tensor_tensor(TT[:], TT[:], bank(1), ALU.subtract))
                    V.tensor_tensor(T[:], T[:], bank(2), ALU.subtract).then_inc(t_next, 1)
                dve.wait_ge(u_prod, s + 1)
                V.tensor_copy(U[:], bank(3)).then_inc(u_ready, 1)
                dve.wait_ge(u_ready, s + 1)
                for z in range(2):
                    dve.wait_ge(s_ready, 2 * s + z + 1)
                    for c in range(2):
                        last = V.tensor_tensor(Sg[RS[1 - c], :, :], S[RS[c], :, :], glz[RS[c], z, :].unsqueeze(2).to_broadcast([C, 4, C]), ALU.mult)
                    link(last)
                    dve.wait_ge(ws_prod, 2 * s + z + 1)
                    V.tensor_tensor(un[:], U[:, z], ps[:, 0, 0:FW].rearrange("p (h n) -> p h n", h=4), ALU.subtract).then_inc(un_ready, 1)
                    dve.wait_ge(o_prod, 2 * s + z + 1)
                    V.tensor_tensor(S[:], Sg[:], ps[:, 1, 0:FW].rearrange("p (h n) -> p h n", h=4), ALU.add).then_inc(s_ready, 1)
                for c in range(2):
                    for d, t in ((0, a), (1, b)):
                        z = c ^ d
                        o = o_sum[RS[c], t, :] if isinstance(t, int) else o_sum[RS[c], bass.ds(t, 1), :].rearrange("p o n -> p (o n)")
                        last = V.tensor_tensor(o, o, ps[RS[c], 2, z * FW:(z + 1) * FW], ALU.add)
                last.then_inc(o_taken, 1)
                assert n[0] == PER



            all_steps(dve, body)




def stage_mix_out(nc, g, l, tiles, latent, context):
    with Stage(nc, f"mix{l}") as st:
        w = st.sb("w", [P, KD, D])
        gb = st.sb("gb", [P, 2, D])
        x = st.sb("x", [P, 3, D])
        tmp = st.sb("tmp", [P, 2, D])
        w_loaded, gb_loaded, prod_ready, gated, summed = (st.sem(n) for n in "w_loaded gb_loaded prod_ready gated summed".split())
        x_loaded = [st.sem(f"x_loaded{i}") for i in range(3)]
        x_stored = [st.sem(f"x_stored{i}") for i in range(3)]
        with nc.Block() as block:
            @block.sync
            def _(sp):
                sp.dma_start(w[:], g.w_out[l].rearrange("(k p) n -> p k n", p=P)).then_inc(w_loaded, 16)
                for s in range(2):
                    sp.dma_start(gb[:, s], g.mod_rows[s:s + 1, 2 * D:3 * D].to_broadcast([P, D])).then_inc(gb_loaded, 16)
                for t in range(tiles):
                    wait(sp, x_stored[t % 3], 16 * (t // 3))
                    sp.dma_start(x[:, t % 3], token_tile(latent, context, t)).then_inc(x_loaded[t % 3], 16)

            @block.tensor
            def _(pe):
                pe.wait_ge(w_loaded, 16)
                for t in range(tiles):
                    wait(pe, gated, t - 1)
                    for half in range(2):
                        for k in range(KD):
                            mm = nc.tensor.matmul(g.ps[:, 2 * (t % 2) + half, :], g.yT[:, k, t * P:(t + 1) * P],
                                                  w[:, k, half * BANK:(half + 1) * BANK], start=k == 0, stop=k == KD - 1)
                    mm.then_inc(prod_ready, 1)

            @block.vector
            def _(dve):
                dve.wait_ge(gb_loaded, 32)
                for t in range(tiles):
                    dve.wait_ge(prod_ready, t + 1)
                    flat = g.ps[:, 2 * (t % 2):2 * (t % 2) + 2, :].rearrange("p b n -> p (b n)")
                    nc.vector.tensor_tensor(tmp[:, t % 2], flat, gb[:, t // NTL], ALU.mult).then_inc(gated, 1)
                    dve.wait_ge(gated, t + 1)
                    dve.wait_ge(x_loaded[t % 3], 16 * (t // 3 + 1))
                    nc.vector.tensor_tensor(x[:, t % 3], x[:, t % 3], tmp[:, t % 2], ALU.add).then_inc(summed, 1)

            @block.scalar
            def _(act):
                for t in range(tiles):
                    act.wait_ge(summed, t + 1)
                    act.dma_start(g.x_dram[t * P:(t + 1) * P, :], x[:, t % 3]).then_inc(x_stored[t % 3], 16)
                for i in range(3):
                    act.wait_ge(x_stored[i], 16 * len(range(i, tiles, 3)))


def stage_route(nc, g, l, tiles):
    NBK = blocks_of(tiles)
    with Stage(nc, f"route{l}") as st:
        w = st.sb("w", [P, KD, NE])
        bias = st.sb("bias", [P, NE])
        iota = st.sb("iota", [P, MAX_BLOCKS])
        before = st.sb("before", [P, 2, P])
        tok = st.sb("tok", [P, NT], U32)
        zero = st.sb("zero", [P, NBK], U32)
        sc = st.sb("sc", [P, tiles, NE])
        sel = st.sb("sel", [P, tiles, NE])
        eq = st.sb("eq", [P, TOP_K, tiles, NE])
        tmp = st.sb("tmp", [P, tiles, NE])
        top = st.sb("top", [P, tiles, 8])
        idx = st.sb("idx", [P, tiles, 8], U32)
        idf = st.sb("idf", [P, tiles, 8])
        tot = st.sb("tot", [P, tiles])
        slotf = st.sb("slotf", [P, tiles, TOP_K])
        nb = st.sb("nb", [P, 3, NE])
        cmp = st.sb("cmp", [1, NBK, NE])
        be = st.sb("be", [1, 3, NBK])
        ring = st.sb("ring", [1, NE])
        idrow = st.sb("idrow", [NBK, P], U32)
        idrf = st.sb("idrf", [NBK, P])
        names = "small_loaded logits_ready exp_ready step mask_ready sums_ready slots_ready ids_cleared zeroed scattered ids_loaded idf_ready ids_turned".split()
        (small_loaded, logits_ready, exp_ready, step, mask_ready, sums_ready, slots_ready, ids_cleared, zeroed, scattered, ids_loaded,
         idf_ready, ids_turned) = (st.sem(n) for n in names)
        ids_dram = g.ids_dram[0:NBK * P, :]
        with nc.Block() as block:
            @block.sync
            def _(sp):
                with nc.allow_non_contiguous_dma("router, once a layer"):
                    sp.dma_start(w[:], g.moe_router[l].rearrange("(k p) n -> p k n", p=P)).then_inc(small_loaded, 16)
                sp.dma_start(bias[:], g.moe_bias[l].rearrange("(o n) -> o n", o=1).to_broadcast([P, NE])).then_inc(small_loaded, 16)
                sp.dma_start(iota[:], g.t_iota.to_broadcast([P, MAX_BLOCKS])).then_inc(small_loaded, 16)
                sp.dma_start(before[:], g.t_before).then_inc(small_loaded, 16)
                sp.dma_start(tok[:], g.t_tok).then_inc(small_loaded, 16)
                sp.wait_ge(zeroed, 1)
                sp.dma_start(ids_dram.rearrange("(p b) o -> p (b o)", p=P), zero[:]).then_inc(ids_cleared, 16)
                sp.wait_ge(scattered, 16 * tiles * TOP_K)
                sp.dma_start(idrow[:], ids_dram.rearrange("(b p) o -> b (p o)", p=P)).then_inc(ids_loaded, 16)

            @block.gpsimd
            def _(pool):
                pool.memset(zero[:], 0).then_inc(zeroed, 1)
                pool.wait_ge(small_loaded, 80)
                pool.wait_ge(ids_cleared, 16)
                pool.wait_ge(slots_ready, 1)
                for t in range(tiles):
                    for j in range(TOP_K):
                        n = t * TOP_K + j
                        pool.indirect_dma_start(ids_dram, bass.IndirectOffsetOnAxis(g.slots[:, n:n + 1], 0),
                                                tok[:, t:t + 1], None).then_inc(scattered, 16)

            @block.tensor
            def _(pe):
                pe.wait_ge(small_loaded, 80)
                for t in range(tiles):
                    for k in range(KD):
                        mm = nc.tensor.matmul(g.ps[:, 0, t * NE:(t + 1) * NE], g.hT[:, k, t * P:(t + 1) * P], w[:, k, :],
                                              start=k == 0, stop=k == KD - 1)
                mm.then_inc(logits_ready, 1)
                pe.wait_ge(mask_ready, 1)
                for t in range(tiles):
                    for u in range(t):
                        nc.tensor.matmul(g.ps[:, 1, t * NE:(t + 1) * NE], before[:, 1, :], sel[:, u, :], start=u == 0, stop=False)
                    nc.tensor.matmul(g.ps[:, 1, t * NE:(t + 1) * NE], before[:, 0, :], sel[:, t, :], start=t == 0, stop=True)
                for u in range(tiles):
                    mm = nc.tensor.matmul(g.ps[:, 2, 0:NE], before[:, 1, :], sel[:, u, :], start=u == 0, stop=u == tiles - 1)
                mm.then_inc(sums_ready, 1)
                pe.wait_ge(idf_ready, 1)
                nc.tensor.transpose(g.ps[:, 3, 0:NBK], idrf[:], g.ident[0:NBK, 0:NBK]).then_inc(ids_turned, 1)

            @block.scalar
            def _(act):
                act.wait_ge(logits_ready, 1)
                nc.scalar.activation(sc[:], g.ps[:, 0, 0:tiles * NE].rearrange("p (t n) -> p t n", n=NE), ACT.Exp, scale=-1.0).then_inc(exp_ready, 1)

            @block.vector
            def _(dve):
                V = nc.vector
                link = Chain(dve, step)
                wide = [P, tiles, NE]
                dve.wait_ge(exp_ready, 1)
                dve.wait_ge(small_loaded, 80)
                link(V.tensor_scalar(sc[:], sc[:], 1.0, None, ALU.add))
                link(V.reciprocal(sc[:], sc[:]))
                link(V.tensor_tensor(sel[:], sc[:], bias[:].unsqueeze(1).to_broadcast(wide), ALU.add))
                for t in range(tiles):
                    last = V.max(top[:, t, :], sel[:, t, :])
                link(last)
                for t in range(tiles):
                    last = V.max_index(idx[:, t, :], top[:, t, :], sel[:, t, :])
                link(last)
                link(V.tensor_copy(idf[:], idx[:]))
                for j in range(TOP_K):
                    last = V.tensor_tensor(eq[:, j], iota[:, 0:NE].unsqueeze(1).to_broadcast(wide), idf[:, :, j:j + 1].to_broadcast(wide), ALU.is_equal)
                link(last)
                link(V.tensor_tensor(sel[:], eq[:, 0], eq[:, 1], ALU.add))
                link(V.tensor_tensor(sel[:], sel[:], eq[:, 2], ALU.add))
                V.tensor_tensor(sel[:], sel[:], eq[:, 3], ALU.add).then_inc(mask_ready, 1)
                dve.wait_ge(mask_ready, 1)
                link(V.tensor_tensor(tmp[:], sel[:], sc[:], ALU.mult))
                link(V.tensor_reduce(tot[:], tmp[:], AX.X, ALU.add))
                link(V.reciprocal(tot[:], tot[:]))
                link(V.tensor_scalar(tot[:], tot[:], ROUTED_SCALE, None, ALU.mult))
                link(V.tensor_tensor(sc[:], tmp[:], tot[:].unsqueeze(2).to_broadcast(wide), ALU.mult))
                for j in range(TOP_K):
                    link(V.tensor_tensor(tmp[:], eq[:, j], sc[:], ALU.mult))
                    link(V.tensor_reduce(g.slot_w[:, 0:tiles, j], tmp[:], AX.X, ALU.add))
                dve.wait_ge(sums_ready, 1)
                link(V.tensor_scalar(nb[:, 0], g.ps[:, 2, 0:NE], 1.0 / P, (P / 2 - 0.5) / P, ALU.mult, ALU.add))
                link(V.tensor_scalar(nb[:, 0], nb[:, 0], MAGIC, None, ALU.add))
                link(V.tensor_scalar(nb[:, 0], nb[:, 0], -MAGIC, None, ALU.add))
                link(V.tensor_tensor_scan(nb[:, 1], nb[:, 0], nb[:, 0], 0.0, ALU.add, ALU.bypass))
                link(V.tensor_tensor(nb[:, 2], nb[:, 1], nb[:, 0], ALU.subtract))
                link(V.tensor_scalar(nb[:, 2], nb[:, 2], float(P), None, ALU.mult))
                link(V.tensor_tensor(sc[:], g.ps[:, 1, 0:tiles * NE].rearrange("p (t n) -> p t n", n=NE),
                                     nb[:, 2:3, :].to_broadcast(wide), ALU.add))
                for j in range(TOP_K):
                    link(V.tensor_tensor(tmp[:], eq[:, j], sc[:], ALU.mult))
                    link(V.tensor_reduce(slotf[:, :, j], tmp[:], AX.X, ALU.add))
                V.tensor_copy(g.slots[:, 0:tiles * TOP_K], slotf[:].rearrange("p t j -> p (t j)")).then_inc(slots_ready, 1)
                link(V.tensor_tensor(cmp[:], nb[0:1, 1:2, :].to_broadcast([1, NBK, NE]),
                                     iota[0:1, 0:NBK].unsqueeze(2).to_broadcast([1, NBK, NE]), ALU.is_le))
                link(V.tensor_reduce(be[:, 0], cmp[:], AX.X, ALU.add))
                link(V.tensor_scalar(be[:, 0], be[:, 0], float(NE - 1), None, ALU.min))
                link(V.tensor_scalar(be[:, 1], be[:, 0], -1.0, 1.0 / RING, ALU.add, ALU.mult))
                link(V.tensor_scalar(be[:, 1], be[:, 1], MAGIC, None, ALU.add))
                link(V.tensor_scalar(be[:, 1], be[:, 1], -MAGIC, None, ALU.add))
                link(V.scalar_tensor_tensor(out=be[:, 2], in0=be[:, 1], scalar=-float(RING), in1=be[:, 0], op0=ALU.mult, op1=ALU.add))
                link(V.tensor_scalar(be[:, 0], be[:, 0], 1.0, None, ALU.add))
                V.tensor_copy(g.block_tab[:, 0, 0:NBK], be[:, 0])
                V.tensor_copy(g.block_tab[:, 1, 0:NBK], be[:, 2])
                link(V.memset(ring[:], 1.0))
                link(V.tensor_scalar(ring[:, RING:], nb[0:1, 1, 0:NE - RING], 1.0, None, ALU.add))
                link(V.tensor_copy(g.ring_tab[:], ring[:]))
                dve.wait_ge(ids_loaded, 16)
                V.tensor_copy(idrf[:], idrow[:]).then_inc(idf_ready, 1)
                dve.wait_ge(ids_turned, 1)
                V.tensor_copy(g.ids[:, 0:NBK], g.ps[:, 3, 0:NBK])


def stage_shared(nc, g, l, tiles):
    chunks = CHUNKS if tiles == NT else CHUNKS[:2]
    with Stage(nc, f"shared{l}") as st:
        wg = st.sb("wg", [P, KD, DE])
        wu = st.sb("wu", [P, KD, DE])
        wd = st.sb("wd", [P, 2, D])
        sg = st.sb("sg", [P, 2, BANK])
        hid = st.sb("hid", [P, 2, TOK])
        w_loaded, up_ready, silu_ready, hid_ready, down_ready, took_lo, took_hi = (
            st.sem(n) for n in "w_loaded up_ready silu_ready hid_ready down_ready took_lo took_hi".split())
        with nc.Block() as block:
            @block.sync
            def _(sp):
                for dst, src in ((wg, g.sh_gate), (wu, g.sh_up), (wd, g.sh_down)):
                    sp.dma_start(dst[:], src[l].rearrange("(k p) n -> p k n", p=P)).then_inc(w_loaded, 16)

            @block.tensor
            def _(pe):
                pe.wait_ge(w_loaded, 48)
                for c, (c0, n) in enumerate(chunks):
                    for f in range(2):
                        m = 2 * c + f
                        wait(pe, hid_ready, m - 1)
                        for i, w in enumerate((wg, wu)):
                            for k in range(KD):
                                mm = nc.tensor.matmul(g.ps[:, 2 * (m % 2) + i, 0:n], w[:, k, f * P:(f + 1) * P],
                                                      g.hT[:, k, c0:c0 + n], start=k == 0, stop=k == KD - 1)
                        mm.then_inc(up_ready, 1)
                for t in range(tiles):
                    pe.wait_ge(hid_ready, 2 * min(t // 4, len(chunks) - 1) + 2)
                    wait(pe, took_lo, t - 1)
                    wait(pe, took_hi, t - 1)
                    for half in range(2):
                        for f in range(2):
                            mm = nc.tensor.matmul(g.ps[:, 4 + 2 * (t % 2) + half, :], hid[:, f, t * P:(t + 1) * P],
                                                  wd[:, f, half * BANK:(half + 1) * BANK], start=f == 0, stop=f == 1)
                    mm.then_inc(down_ready, 1)

            @block.scalar
            def _(act):
                for c, (c0, n) in enumerate(chunks):
                    for f in range(2):
                        m = 2 * c + f
                        act.wait_ge(up_ready, m + 1)
                        wait(act, hid_ready, m - 1)
                        nc.scalar.activation(sg[:, m % 2, 0:n], g.ps[:, 2 * (m % 2), 0:n], ACT.Silu).then_inc(silu_ready, 1)
                for t in range(tiles):
                    act.wait_ge(down_ready, t + 1)
                    nc.scalar.copy(g.acc[:, t, BANK:], g.ps[:, 5 + 2 * (t % 2), :]).then_inc(took_hi, 1)

            @block.vector
            def _(dve):
                for c, (c0, n) in enumerate(chunks):
                    for f in range(2):
                        m = 2 * c + f
                        dve.wait_ge(silu_ready, m + 1)
                        nc.vector.tensor_tensor(hid[:, f, c0:c0 + n], sg[:, m % 2, 0:n], g.ps[:, 2 * (m % 2) + 1, 0:n],
                                                ALU.mult).then_inc(hid_ready, 1)
                for t in range(tiles):
                    dve.wait_ge(down_ready, t + 1)
                    nc.vector.tensor_copy(g.acc[:, t, 0:BANK], g.ps[:, 4 + 2 * (t % 2), :]).then_inc(took_lo, 1)


def stage_experts(nc, g, l, tiles):
    NBK = blocks_of(tiles)
    with Stage(nc, f"moe{l}") as st:
        wgu = st.sb("wgu", [P, RING, KD, 2 * DE])
        wd = st.sb("wd", [P, RING, 2, D])
        xg = st.sb("xg", [P, 2, D])
        xT = st.sb("xT", [P, 2, KD, P])
        ix = st.sb("ix", [P, 2], U32)
        sg = st.sb("sg", [P, 2, DE])
        hid = st.sb("hid", [P, 2, DE])
        hT = st.sb("hidT", [P, 2, 2, P])
        y = st.sb("y", [P, 2, D])
        names = "landed picked waits_met turned xt_lo xt_hi gu_ready silu_ready hid_ready hid_turned hidt_ready down_ready y_lo y_hi".split()
        (landed, picked, waits_met, turned, xt_lo, xt_hi, gu_ready, silu_ready, hid_ready, hid_turned, hidt_ready, down_ready, y_lo, y_hi) = (
            st.sem(n) for n in names)
        w_loaded = [st.sem(f"w_loaded{i}") for i in range(RING)]
        x_landed = [st.sem(f"x_landed{i}") for i in range(2)]
        y_stored = [st.sem(f"y_stored{i}") for i in range(2)]

        def all_blocks(eng, body):
            body(0, 0)
            body(1, 1)
            with eng.Fori(1, NBK // 2 - 1) as i:
                body(i * 2, 0)
                body(i * 2 + 1, 1)
            body(NBK - 2, 0)
            body(NBK - 1, 1)

        def last(b):
            return isinstance(b, int) and b == NBK - 1

        def first(b):
            return isinstance(b, int) and b == 0

        with nc.Block() as block:
            @block.sync
            def _(sp):
                def load(e, r, turn):
                    free = sp.value_load(g.ring_tab[0:1, bass.ds(e, 1)], min_val=1, max_val=NBK + 1)
                    sp.wait_ge(down_ready, free)
                    one = bass.ds(e, 1)
                    sp.dma_start(wgu[:, r, :, 0:DE], g.moe_gate[l][one].rearrange("o (k p) n -> p (o k) n", p=P)).then_inc(w_loaded[r], 16)
                    sp.dma_start(wgu[:, r, :, DE:], g.moe_up[l][one].rearrange("o (k p) n -> p (o k) n", p=P)).then_inc(w_loaded[r], 16)
                    sp.dma_start(wd[:, r], g.moe_down[l][one].rearrange("o (k p) n -> p (o k) n", p=P)).then_inc(w_loaded[r], 16)

                def tell(r, turn):
                    sp.wait_ge(w_loaded[r], turn * 48 + 48)
                    sp.sem_inc(landed, 1)

                load(0, 0, 0)
                for e in range(1, RING):
                    load(e, e, 0)
                    tell(e - 1, 0)
                with sp.Fori(1, NE // RING) as i:
                    load(i * RING, 0, i)
                    tell(RING - 1, i - 1)
                    for r in range(1, RING):
                        load(i * RING + r, r, i)
                        tell(r - 1, i)
                for e in range(NE // RING * RING, NE):
                    load(e, e % RING, e // RING)
                    tell((e - 1) % RING, (e - 1) // RING)
                tell((NE - 1) % RING, (NE - 1) // RING)

            @block.gpsimd
            def _(pool):
                pool.sem_inc(down_ready, 1)

                def body(b, q):
                    wait(pool, turned, b - 1)
                    nc.gpsimd.tensor_copy(ix[:, q:q + 1], g.ids[:, bass.ds(b, 1)]).then_inc(picked, 1)
                    pool.wait_ge(picked, b + 1)
                    pool.sem_inc(waits_met, 1)
                    pool.indirect_dma_start(xg[:, q], None, g.h_dram, bass.IndirectOffsetOnAxis(ix[:, q:q + 1], 0)).then_inc(x_landed[q], 16)

                all_blocks(pool, body)

            @block.tensor
            def _(pe):
                def turn(b, q, half):
                    pe.wait_ge(x_landed[q], half * 16 + 16)
                    wait(pe, xt_lo, b)
                    wait(pe, xt_hi, b)
                    for k in range(KD):
                        mm = nc.tensor.transpose(g.ps[:, k // 4, (k % 4) * P:(k % 4 + 1) * P], xg[:, q, k * P:(k + 1) * P], g.ident[:])
                    mm.then_inc(turned, 1)

                def down(b, q, place):
                    pe.wait_ge(hidt_ready, b + 1)
                    wait(pe, y_lo, b)
                    wait(pe, y_hi, b)
                    for half in range(2):
                        for f in range(2):
                            mm = nc.tensor.matmul(g.ps[:, 6 + half, :], hT[:, q, f, :],
                                                  wd[:, bass.ds(place, 1), f, half * BANK:(half + 1) * BANK].rearrange("p o n -> p (o n)"),
                                                  start=f == 0, stop=f == 1)
                    mm.then_inc(down_ready, 1)

                def place_of(b):
                    return pe.value_load(g.block_tab[0:1, 1, bass.ds(b, 1)], min_val=0, max_val=RING - 1)

                def body(b, q):
                    expert = pe.value_load(g.block_tab[0:1, 0, bass.ds(b, 1)], min_val=1, max_val=NE)
                    place = place_of(b)
                    pe.wait_ge(landed, expert)
                    pe.wait_ge(xt_lo, b + 1)
                    pe.wait_ge(xt_hi, b + 1)
                    wait(pe, hid_ready, b - 1)
                    for k in range(KD):
                        mm = nc.tensor.matmul(g.ps[:, 2 + q, :], xT[:, q, k, :],
                                              wgu[:, bass.ds(place, 1), k, :].rearrange("p o n -> p (o n)"),
                                              start=k == 0, stop=k == KD - 1)
                    mm.then_inc(gu_ready, 1)
                    if not first(b):
                        down(b - 1, 1 - q, place_of(b - 1))
                    if not last(b):
                        turn(b + 1, 1 - q, (b + 1 - (1 - q)) // 2 if isinstance(b, int) else half_of(b, q))
                    pe.wait_ge(hid_ready, b + 1)
                    for f in range(2):
                        mm = nc.tensor.transpose(g.ps[:, 4, f * P:(f + 1) * P], hid[:, q, f * P:(f + 1) * P], g.ident[:])
                    mm.then_inc(hid_turned, 1)
                    if last(b):
                        down(b, q, place_of(b))

                halves = {}

                def half_of(b, q):
                    return halves[q]

                turn(0, 0, 0)
                body(0, 0)
                body(1, 1)
                with pe.Fori(1, NBK // 2 - 1) as i:
                    halves[0], halves[1] = i, i + 1
                    body(i * 2, 0)
                    body(i * 2 + 1, 1)
                body(NBK - 2, 0)
                body(NBK - 1, 1)

            @block.scalar
            def _(act):
                def put(b, q):
                    act.wait_ge(down_ready, b + 2)
                    nc.scalar.copy(y[:, q, BANK:], g.ps[:, 7, :]).then_inc(y_hi, 1)
                    act.wait_ge(y_hi, b + 1)
                    act.wait_ge(y_lo, b + 1)
                    row = g.y_dram[bass.ds(b, 1)].rearrange("o p n -> p (o n)")
                    act.dma_start(row, y[:, q]).then_inc(y_stored[q], 16)

                def take(b, q):
                    act.wait_ge(turned, b + 1)
                    nc.scalar.copy(xT[:, q, 4:8, :], g.ps[:, 1, :].rearrange("p (k n) -> p k n", n=P)).then_inc(xt_hi, 1)

                def body(b, q):
                    act.wait_ge(gu_ready, b + 1)
                    nc.scalar.activation(sg[:, q], g.ps[:, 2 + q, 0:DE], ACT.Silu).then_inc(silu_ready, 1)
                    if not first(b):
                        if not (isinstance(b, int) and b < 3):
                            act.wait_ge(y_stored[1 - q], (b - 1 - (1 - q)) * 8)
                        put(b - 1, 1 - q)
                    if not last(b):
                        take(b + 1, 1 - q)

                take(0, 0)
                all_blocks(act, body)
                act.wait_ge(y_stored[1], (NBK - 2) * 8)
                put(NBK - 1, 1)
                for q in range(2):
                    act.wait_ge(y_stored[q], NBK * 8)

            @block.vector
            def _(dve):
                def put(b, q):
                    dve.wait_ge(down_ready, b + 2)
                    if not (isinstance(b, int) and b < 2):
                        dve.wait_ge(y_stored[q], (b - q) * 8)
                    nc.vector.tensor_copy(y[:, q, 0:BANK], g.ps[:, 6, :]).then_inc(y_lo, 1)

                def take(b, q):
                    dve.wait_ge(turned, b + 1)
                    nc.vector.tensor_copy(xT[:, q, 0:4, :], g.ps[:, 0, :].rearrange("p (k n) -> p k n", n=P)).then_inc(xt_lo, 1)

                def body(b, q):
                    dve.wait_ge(silu_ready, b + 1)
                    nc.vector.tensor_tensor(hid[:, q], sg[:, q], g.ps[:, 2 + q, DE:], ALU.mult).then_inc(hid_ready, 1)
                    if not first(b):
                        put(b - 1, 1 - q)
                    if not last(b):
                        take(b + 1, 1 - q)
                    dve.wait_ge(hid_turned, b + 1)
                    nc.vector.tensor_copy(hT[:, q], g.ps[:, 4, 0:2 * P].rearrange("p (f n) -> p f n", n=P)).then_inc(hidt_ready, 1)

                take(0, 0)
                all_blocks(dve, body)
                put(NBK - 1, 1)


def stage_moe_out(nc, g, l, tiles, final):
    with Stage(nc, f"res{l}") as st:
        gb = st.sb("gb", [P, 2, D])
        nf = st.sb("nf", [P, D])
        x = st.sb("x", [P, 3, D])
        tmp = st.sb("tmp", [P, 2, D])
        ye = st.sb("ye", [P, 6, D])
        ss = st.sb("ss", [P, tiles])
        y_landed = [st.sem(f"y_landed{i}") for i in range(6)]
        added = st.sem("added")
        names = "gb_loaded gated summed squared mean_ready root_ready rstd_ready normed out_ready".split()
        gb_loaded, gated, summed, squared, mean_ready, root_ready, rstd_ready, normed, out_ready = (st.sem(n) for n in names)
        x_loaded = [st.sem(f"x_loaded{i}") for i in range(3)]
        x_stored = [st.sem(f"x_stored{i}") for i in range(3)]
        with nc.Block() as block:
            @block.sync
            def _(sp):
                for s in range(2):
                    sp.dma_start(gb[:, s], g.mod_rows[s:s + 1, 5 * D:6 * D].to_broadcast([P, D])).then_inc(gb_loaded, 16)
                sp.dma_start(nf[:], g.norm_f.rearrange("(o n) -> o n", o=1).to_broadcast([P, D])).then_inc(gb_loaded, 16)
                for t in range(tiles):
                    wait(sp, x_stored[t % 3], 16 * (t // 3))
                    sp.dma_start(x[:, t % 3], g.x_dram[t * P:(t + 1) * P, :]).then_inc(x_loaded[t % 3], 16)

            @block.gpsimd
            def _(pool):
                rows = g.y_dram[0:blocks_of(tiles)].rearrange("b p n -> (b p) n")
                for n in range(tiles * TOP_K):
                    wait(pool, added, n - 5)
                    pool.indirect_dma_start(ye[:, n % 6], None, rows, bass.IndirectOffsetOnAxis(g.slots[:, n:n + 1], 0)).then_inc(y_landed[n % 6], 16)

            @block.vector
            def _(dve):
                dve.wait_ge(gb_loaded, 48)
                for t in range(tiles):
                    for j in range(TOP_K):
                        n = t * TOP_K + j
                        dve.wait_ge(y_landed[n % 6], 16 * (n // 6 + 1))
                        nc.vector.scalar_tensor_tensor(out=g.acc[:, t, :], in0=ye[:, n % 6], scalar=g.slot_w[:, t, j:j + 1],
                                                       in1=g.acc[:, t, :], op0=ALU.mult, op1=ALU.add).then_inc(added, 1)
                        dve.wait_ge(added, n + 1)
                    if final:
                        wait(dve, squared, t - 1)
                    nc.vector.tensor_tensor(tmp[:, t % 2], g.acc[:, t, :], gb[:, t // NTL], ALU.mult).then_inc(gated, 1)
                    dve.wait_ge(gated, t + 1)
                    dve.wait_ge(x_loaded[t % 3], 16 * (t // 3 + 1))
                    nc.vector.tensor_tensor(x[:, t % 3], x[:, t % 3], tmp[:, t % 2], ALU.add).then_inc(summed, 1)
                    if final:
                        dve.wait_ge(squared, t + 1)
                        nc.vector.tensor_scalar(ss[:, t:t + 1], ss[:, t:t + 1], 1.0 / D, EPS, ALU.mult, ALU.add).then_inc(mean_ready, 1)
                        dve.wait_ge(root_ready, t + 1)
                        nc.vector.reciprocal(ss[:, t:t + 1], ss[:, t:t + 1]).then_inc(rstd_ready, 1)
                        dve.wait_ge(rstd_ready, t + 1)
                        nc.vector.scalar_tensor_tensor(out=x[:, t % 3], in0=x[:, t % 3], scalar=ss[:, t:t + 1], in1=nf[:],
                                                       op0=ALU.mult, op1=ALU.mult).then_inc(out_ready, 1)

            @block.scalar
            def _(act):
                for t in range(tiles):
                    act.wait_ge(summed, t + 1)
                    if final:
                        nc.scalar.activation(tmp[:, t % 2], x[:, t % 3], ACT.Square, accum_out=ss[:, t:t + 1]).then_inc(squared, 1)
                        act.wait_ge(mean_ready, t + 1)
                        nc.scalar.activation(ss[:, t:t + 1], ss[:, t:t + 1], ACT.Sqrt).then_inc(root_ready, 1)
                        act.wait_ge(out_ready, t + 1)
                        dst = g.out[0, t * P:(t + 1) * P, :]
                    else:
                        dst = g.x_dram[t * P:(t + 1) * P, :]
                    act.dma_start(dst, x[:, t % 3]).then_inc(x_stored[t % 3], 16)
                for i in range(3):
                    act.wait_ge(x_stored[i], 16 * len(range(i, tiles, 3)))


def shape_tables():
    t = {}
    f32 = np.float32
    t["t_ident"] = np.eye(P, dtype=f32)

    t["t_iota"] = np.arange(MAX_BLOCKS, dtype=f32)[None, :]
    a = np.arange(P)
    t["t_before"] = np.stack([a[:, None] < a[None, :], np.ones((P, P))], axis=1).astype(f32)
    t["t_tok"] = np.ascontiguousarray(np.arange(TOK, dtype=np.uint32).reshape(NT, P).T)
    for name, L in (("", SEQ), ("_c", CTX)):
        n = np.arange(L, dtype=f32)
        t_norm = n / f32(L - 1)
        bands = np.linspace(1e-4, HY_BANDS - 1, HY_BANDS, dtype=f32)
        ang = (f32(2.0 * math.pi / L) * n[:, None] * bands[None, :]).astype(f32)
        z = np.concatenate([t_norm[:, None], np.cos(ang), -np.sin(ang)], axis=-1).astype(f32)
        t["t_hy_z" + name] = np.ascontiguousarray(z.T)
        lo, hi = -math.log(1e-2) / 1.5, -math.log(1e-2) / 0.3
        decay = np.linspace(lo, hi, HY_CH, dtype=f32)
        d = np.exp(-t_norm[:, None] * decay[None, :]).astype(f32)
        db = d.copy()
        db[0] = 0
        t["t_hy_dec" + name] = np.concatenate([d, db], axis=1)
        j = np.arange(L)[:, None].astype(np.float64)
        k = np.arange(L)[None, :].astype(np.float64)

        def blocks(a):
            return a.reshape(L // P, P, L // P, P).transpose(2, 1, 0, 3)

        a = math.pi / (2 * L) * (2 * k + 1)
        t["t_dft" + name] = np.ascontiguousarray(np.stack([blocks(np.cos(a * j)), blocks(np.sin(a * j))]).astype(f32))
        C2 = np.stack([np.cos(a * (j + 0.5)), np.sin(a * (j + 0.5))]).astype(f32)
        t["t_dft2" + name] = np.ascontiguousarray(np.stack([blocks(C2[0]), blocks(C2[1])]))
        t["t_dft2r" + name] = C2
    quarter = HD // 4
    inv = (f32(10000.0) ** (-np.arange(quarter, dtype=f32) / f32(quarter))).astype(f32)
    pos = np.arange(SEQ)
    row, col = (pos // GRID_W).astype(f32), (pos % GRID_W).astype(f32)
    ang = np.concatenate([np.tile(row[:, None] * inv, 2), np.tile(col[:, None] * inv, 2)], axis=1).astype(f32)
    t["t_rope"] = np.ascontiguousarray(np.stack([np.tile(np.cos(ang), 2).T, np.tile(np.sin(ang), 2).T]).astype(f32))
    rot = np.zeros((P, P), f32)
    for base in range(0, P, 2 * quarter):
        for d in range(quarter):
            rot[base + quarter + d, base + d] = -1.0
            rot[base + d, base + quarter + d] = 1.0
    t["t_rot"] = rot
    q = np.arange(P)[:, None]
    k = np.arange(P)[None, :]
    m = np.zeros((P, CTX + 3 * P), f32)
    m[:, CTX:CTX + P] = np.where(k >= q, 0, NEG)
    m[:, CTX + 2 * P:] = np.where(k <= q, 0, NEG)
    t["t_wa_mask"] = m
    sel = np.zeros((32, GRID_W, 2, GRID_W), f32)
    cq = np.arange(GRID_W)
    start = np.clip(cq - NA_KC // 2, 0, GRID_W - NA_KC)
    for ck in range(GRID_W):
        for c in range(GRID_W):
            if start[c] <= ck < start[c] + NA_KC:
                sel[ck - c + NA_KC - 1, ck, :, c] = 1
            else:
                sel[31, ck, :, c] = 1
    t["t_na_sel"] = sel.reshape(32, GRID_W * P)
    return t


def gdn_tables():
    C = 64
    t = {}
    i = np.arange(C)[:, None]
    j = np.arange(C)[None, :]
    two = lambda a: np.tile(a, (2,) + (1,) * (a.ndim - 1)).astype(np.float32)
    dirs = lambda f, b: np.stack([f, b], axis=1)
    t["t_gd_tri"] = two(dirs(i <= j, i >= j))
    t["t_gd_allow"] = two(np.where(dirs(i >= j, i <= j), 1e30, NEG))
    t["t_gd_strict"] = two(dirs(i > j, i < j))
    t["t_gd_eye"] = two(np.eye(C))
    lv = []
    for s in (1, 2, 4, 8, 16, 32):
        m = (i // (2 * s) == j // (2 * s)) & (i // s % 2 == 1) & (j // s % 2 == 0)
        lv.append(dirs(m, m.T))
    lv.insert(1, lv[0][:, ::-1])
    t["t_gd_lvl"] = two(np.stack(lv, axis=1))
    blk = np.kron(np.eye(2), np.ones((C, C)))
    t["t_gd_negblk"] = -blk.astype(np.float32)
    a = np.arange(P)
    same = blk.astype(bool)
    t["t_gd_cum"] = np.stack([same & (a[:, None] <= a[None, :]), same & (a[:, None] >= a[None, :]), same], axis=1).astype(np.float32)
    return {k: np.ascontiguousarray(v) for k, v in t.items()}


NAMES = ["x", "c", "ctx", "c_ctx", "w_ada", "b_ada", "norm1", "norm2", "norm_f", "w_in", "w_out",
         "hy_conv", "hy_w1", "hy_b1", "hy_w2", "hy_b2", "hy_w3", "hy_freq", "hy_bias",
         "wa_sink", "na_rpb", "gdn_conv", "gdn_a_log", "gdn_dt_bias", "gdn_norm",
         "moe_router", "moe_bias", "moe_gate", "moe_up", "moe_down", "sh_gate", "sh_up", "sh_down"]


class Globals:

    def __init__(self, arrays):
        self.tables = arrays
        (self.x, self.c, self.ctx, self.c_ctx, self.w_ada, self.b_ada, self.norm1, self.norm2, self.norm_f, self.w_in,
         self.w_out, self.hy_conv, self.hy_w1, self.hy_b1, self.hy_w2, self.hy_b2, self.hy_w3, self.hy_freq, self.hy_bias,
         self.wa_sink, self.na_rpb, self.gdn_conv, self.gdn_a_log, self.gdn_dt_bias, self.gdn_norm,
         self.moe_router, self.moe_bias, self.moe_gate, self.moe_up, self.moe_down,
         self.sh_gate, self.sh_up, self.sh_down) = (arrays[n] for n in NAMES)
        self.t_ident, self.t_iota, self.t_before, self.t_tok, self.t_rope, self.t_rot, self.t_wa_mask, self.t_na_sel = (
            arrays[n] for n in ("t_ident", "t_iota", "t_before", "t_tok", "t_rope", "t_rot", "t_wa_mask", "t_na_sel"))


def hybrid_backbone(nc, arrays, out):
    g = Globals(arrays)
    g.out = out
    g.hy_tables = [(arrays["t_hy_z" + s], arrays["t_hy_dec" + s], arrays["t_dft" + s], arrays["t_dft2" + s]) for s in ("", "_c")]
    g.hy_rows = [arrays["t_dft2r"], arrays["t_dft2r_c"]]
    g.gdn_masks = {n: list(arrays["t_" + n].shape[1:]) for n in ("gd_tri", "gd_allow", "gd_strict", "gd_eye", "gd_lvl", "gd_negblk")}
    g.x_dram = nc.dram_tensor("x_dram", [TOK, D], F32, kind="Internal").ap()
    g.h_dram = nc.dram_tensor("h_dram", [TOK, D], F32, kind="Internal").ap()
    g.y_dram = nc.dram_tensor("y_dram", [MAX_BLOCKS, P, D], F32, kind="Internal").ap()
    g.ids_dram = nc.dram_tensor("ids_dram", [MAX_BLOCKS * P, 1], U32, kind="Internal").ap()
    g.mod_rows = nc.dram_tensor("mod_rows", [2, 6 * D], F32, kind="Internal").ap()
    with ExitStack() as ctx:
        def sb(name, shape):
            return ctx.enter_context(nc.sbuf_tensor(name, shape, F32))
        g.ps = ctx.enter_context(nc.psum_tensor("ps", [P, 8, BANK], F32))
        g.ident = sb("ident", [P, P])
        g.siluT = sb("siluT", [P, KD, 2])
        g.modT = sb("modT", [P, 6 * KD, 2])
        g.gain = sb("gain", [P, 2, KD, 2])
        g.slot_w = sb("slot_w", [P, NT, TOP_K])
        g.slots = ctx.enter_context(nc.sbuf_tensor("slots", [P, NT * TOP_K], U32))
        g.ids = ctx.enter_context(nc.sbuf_tensor("ids", [P, MAX_BLOCKS], U32))
        g.block_tab = ctx.enter_context(nc.sbuf_tensor("block_tab", [1, 2, MAX_BLOCKS], U32))
        g.ring_tab = ctx.enter_context(nc.sbuf_tensor("ring_tab", [1, NE], U32))
        g.hT = sb("hT", [P, KD, TOK])
        mixed = sb("mixed", [P, NT * D])
        g.yT = mixed[:].rearrange("p (k n) -> p k n", k=KD)
        g.acc = mixed[:].rearrange("p (t n) -> p t n", t=NT)
        stage_setup(nc, g)
        for l in range(DEPTH):
            last = l == DEPTH - 1
            tiles = NTL if last else NT
            latent, context = (g.x[0], g.ctx[0]) if l == 0 else (g.x_dram[0:SEQ, :], g.x_dram[SEQ:TOK, :])
            stage_modulation(nc, g, l)
            stage_norm(nc, g, l, 0, NT, latent, context)
            stage_hyena(nc, g, l, False)
            if not last:
                stage_hyena(nc, g, l, True)
            stage_window(nc, g, l, not last)
            stage_neighbour(nc, g, l, not last)
            stage_gdn(nc, g, l)
            stage_mix_out(nc, g, l, tiles, latent, context)
            stage_norm(nc, g, l, 1, tiles, g.x_dram[0:SEQ, :], g.x_dram[SEQ:TOK, :])
            stage_route(nc, g, l, tiles)
            stage_shared(nc, g, l, tiles)
            stage_experts(nc, g, l, tiles)
            stage_moe_out(nc, g, l, tiles, last)


def kernel(**inputs):
    import concourse.bacc as bacc
    from concourse.bass_utils import run_bass_kernel_spmd

    nc = bacc.Bacc("TRN2", target_bir_lowering=False, num_devices=1)
    tables = shape_tables()
    tables.update(gdn_tables())
    feeds, args = {}, {}
    for name in NAMES:
        feeds["in_" + name] = np.ascontiguousarray(inputs[name])
    for name, a in tables.items():
        feeds["in_" + name] = a
    for name, a in feeds.items():
        args[name[3:]] = nc.dram_tensor(name, a.shape, mybir.dt.from_np(a.dtype), kind="ExternalInput").ap()
    out = nc.dram_tensor("out", (1, SEQ, D), F32, kind="ExternalOutput").ap()
    hybrid_backbone(nc, args, out)
    nc.compile()
    r = run_bass_kernel_spmd(nc, [feeds], core_ids=[0])
    return r.results[0]["out"]
```

```python
import math
from contextlib import ExitStack

import numpy as np

import concourse.bass as bass
from concourse import mybir

F32 = mybir.dt.float32
U32 = mybir.dt.uint32
ALU = mybir.AluOpType
ACT = mybir.ActivationFunctionType
AX = mybir.AxisListType

P = 128
D = 1024
KD = D // P
SEQ = 1024
CTX = 256
NTL = SEQ // P
NTC = CTX // P
NT = NTL + NTC
TOK = SEQ + CTX
DEPTH = 2
BANK = 512
HD = 64

HY_CH = 256
HY_BANDS = 16
HY_EMB = 1 + 2 * HY_BANDS
HY_FFN = 64
HY_IN = 3 * HY_CH
WA_IN = 512
NA_IN = 768
GW = 256
GDN_IN = 4 * GW + 16
WA0, NA0, GD0 = HY_IN, HY_IN + WA_IN, HY_IN + WA_IN + NA_IN
D_IN = GD0 + GDN_IN
NE = 32
DE = 256
NEG = -1e30
EPS = 1e-6
SCALE = HD ** -0.5
GRID_W = 64
NA_KR, NA_KC = 8, 16
ROUTED_SCALE = 2.5
TOP_K = 4
RING = 3
MAGIC = 1.5 * 2.0 ** 23
CHUNKS = [(0, BANK), (BANK, BANK), (SEQ, CTX)]


def blocks_of(tiles):
    return (tiles * TOP_K + NE - 1 + 1) // 2 * 2


MAX_BLOCKS = blocks_of(NT)


def wait(eng, sem, value):
    if not isinstance(value, int) or value > 0:
        eng.wait_ge(sem, value)


class Chain:

    def __init__(self, eng, sem):
        self.eng, self.sem, self.n = eng, sem, 0

    def __call__(self, instruction):
        self.n += 1
        instruction.then_inc(self.sem, 1)
        self.eng.wait_ge(self.sem, self.n)


class Stage:

    def __init__(self, nc, tag):
        self.nc, self.tag, self.sems, self.stack = nc, tag, [], ExitStack()

    def __enter__(self):
        self.stack.__enter__()
        return self

    def __exit__(self, *a):
        self.nc.clear_and_free_semaphores(self.sems)
        self.nc.all_engine_barrier()
        return self.stack.__exit__(*a)

    def sb(self, name, shape, dt=F32):
        return self.stack.enter_context(self.nc.sbuf_tensor(f"{name}_{self.tag}", shape, dt))

    def sem(self, name):
        s = self.nc.alloc_semaphore(f"{name}_{self.tag}")
        self.sems.append(s)
        return s


def stage_setup(nc, g):
    with Stage(nc, "setup") as st:
        cT = st.sb("cT", [P, KD, 2])
        e = st.sb("e", [P, KD, 2])
        loaded, c_loaded, exp_ready, silu_step = (st.sem(n) for n in ("loaded", "c_loaded", "exp_ready", "silu_step"))
        with nc.Block() as block:
            @block.sync
            def _(sp):
                sp.dma_start(g.ident[:], g.t_ident).then_inc(loaded, 16)

                with nc.allow_non_contiguous_dma("conditioning vectors, once"):
                    sp.dma_start(cT[:, :, 0], g.c.rearrange("o (k p) -> p (o k)", p=P)).then_inc(c_loaded, 16)
                    sp.dma_start(cT[:, :, 1], g.c_ctx.rearrange("(k p) -> p k", p=P)).then_inc(c_loaded, 16)
                sp.wait_ge(loaded, 16)

            @block.scalar
            def _(act):
                act.wait_ge(c_loaded, 32)
                nc.scalar.activation(e[:], cT[:], ACT.Exp, scale=-1.0).then_inc(exp_ready, 1)

            @block.vector
            def _(dve):
                link = Chain(dve, silu_step)
                dve.wait_ge(exp_ready, 1)
                link(nc.vector.tensor_scalar_add(e[:], e[:], 1.0))
                link(nc.vector.reciprocal(e[:], e[:]))
                link(nc.vector.tensor_tensor(g.siluT[:], e[:], cT[:], ALU.mult))


class Modulation:

    CHUNKS = 6 * D // BANK
    BANKS = 7

    def __init__(self, nc, g, l, st, w):
        self.nc, self.g, self.l, self.w, self.places = nc, g, l, w, w.shape[1]
        self.rows = st.sb("mod_rows", [2, 6 * D])
        self.bias = st.sb("mod_bias", [2, 6 * D])
        self.normT = st.sb("normT", [P, 2, KD])
        self.w_loaded = [st.sem(f"ada_loaded{i}") for i in range(self.places)]
        (self.bias_loaded, self.norm_loaded, self.chunk_ready, self.row_ready, self.rows_turned, self.rows_stored, self.mod_step) = (
            st.sem(n) for n in ("bias_loaded", "norm_loaded", "chunk_ready", "row_ready", "rows_turned", "rows_stored", "mod_step"))

    def load_small(self, sp):
        g, l = self.g, self.l
        sp.dma_start(self.bias[:], g.b_ada[l].rearrange("(o n) -> o n", o=1).to_broadcast([2, 6 * D])).then_inc(self.bias_loaded, 16)
        with self.nc.allow_non_contiguous_dma("norm gains, once a layer"):
            sp.dma_start(self.normT[:, 0, :], g.norm1[l].rearrange("(k p) -> p k", p=P)).then_inc(self.norm_loaded, 16)
            sp.dma_start(self.normT[:, 1, :], g.norm2[l].rearrange("(k p) -> p k", p=P)).then_inc(self.norm_loaded, 16)

    def load(self, sp, n):
        wait(sp, self.chunk_ready, n - self.places + 1)
        wv = self.g.w_ada[self.l].rearrange("(k p) n -> p k n", p=P)
        sp.dma_start(self.w[:, n % self.places], wv[:, :, n * BANK:(n + 1) * BANK]).then_inc(self.w_loaded[n % self.places], 16)

    def store(self, sp):
        sp.wait_ge(self.row_ready, self.CHUNKS)
        sp.dma_start(self.g.mod_rows, self.rows[:]).then_inc(self.rows_stored, 16)
        sp.wait_ge(self.rows_stored, 16)

    def products(self, pe):
        nc, g = self.nc, self.g
        for n in range(self.CHUNKS):
            pe.wait_ge(self.w_loaded[n % self.places], 16 * (n // self.places + 1))
            wait(pe, self.row_ready, n - self.BANKS + 1)
            for k in range(KD):
                mm = nc.tensor.matmul(g.ps[0:2, n % self.BANKS, :], g.siluT[:, k, :], self.w[:, n % self.places, k, :],
                                      start=k == 0, stop=k == KD - 1)
            mm.then_inc(self.chunk_ready, 1)
        pe.wait_ge(self.row_ready, self.CHUNKS)
        for k in range(6 * KD):
            mm = nc.tensor.transpose(g.ps[:, self.BANKS, 2 * k:2 * k + 2], self.rows[:, k * P:(k + 1) * P], g.ident[0:2, 0:2])
        mm.then_inc(self.rows_turned, 1)

    def add_bias(self, dve, n):
        if n == 0:
            dve.wait_ge(self.bias_loaded, 16)
        dve.wait_ge(self.chunk_ready, n + 1)
        cols = slice(n * BANK, (n + 1) * BANK)
        self.nc.vector.tensor_tensor(self.rows[:, cols], self.g.ps[0:2, n % self.BANKS, :], self.bias[:, cols], ALU.add).then_inc(self.row_ready, 1)

    def scales(self, dve):
        nc, g = self.nc, self.g
        link = Chain(dve, self.mod_step)
        dve.wait_ge(self.rows_turned, 1)
        link(nc.vector.tensor_copy(g.modT[:], g.ps[:, self.BANKS, 0:12 * KD].rearrange("p (k s) -> p k s", s=2)))
        dve.wait_ge(self.norm_loaded, 32)
        for i, sc0 in ((0, KD), (1, 4 * KD)):
            link(nc.vector.scalar_tensor_tensor(
                out=g.gain[:, i], in0=g.modT[:, sc0:sc0 + KD, :], scalar=1.0,
                in1=self.normT[:, i, :].unsqueeze(2).to_broadcast([P, KD, 2]), op0=ALU.add, op1=ALU.mult))


def stage_modulation(nc, g, l):
    with Stage(nc, f"mod{l}") as st:
        m = Modulation(nc, g, l, st, st.sb("w", [P, 3, KD, BANK]))
        with nc.Block() as block:
            @block.sync
            def _(sp):
                m.load_small(sp)
                for n in range(m.CHUNKS):
                    m.load(sp, n)
                m.store(sp)

            @block.tensor
            def _(pe):
                m.products(pe)

            @block.vector
            def _(dve):
                for n in range(m.CHUNKS):
                    m.add_bias(dve, n)
                m.scales(dve)


def token_tile(latent, context, t):
    return latent[t * P:(t + 1) * P, :] if t < NTL else context[(t - NTL) * P:(t - NTL + 1) * P, :]


def stage_norm(nc, g, l, latent, context):
    tiles = NT
    with Stage(nc, f"norm{l}") as st:
        x = st.sb("x", [P, 3, D])
        xn = st.sb("xn", [P, 2, D])
        sq = st.sb("sq", [P, D])
        ss = st.sb("ss", [P, tiles])
        rs = st.sb("rs", [P, tiles])
        rt = st.sb("rt", [P, tiles])
        x_loaded = [st.sem(f"x_loaded{i}") for i in range(3)]
        names = "squares_summed mean_ready root_ready rstd_ready scaled turned taken_lo taken_hi step".split()
        squares_summed, mean_ready, root_ready, rstd_ready, scaled, turned, taken_lo, taken_hi, step = (st.sem(n) for n in names)
        with nc.Block() as block:
            @block.sync
            def _(sp):
                for t in range(tiles):
                    wait(sp, scaled, t - 2)
                    sp.dma_start(x[:, t % 3], token_tile(latent, context, t)).then_inc(x_loaded[t % 3], 16)

            @block.scalar
            def _(act):
                for t in range(tiles + 1):
                    if t < tiles:
                        act.wait_ge(x_loaded[t % 3], 16 * (t // 3 + 1))
                        wait(act, squares_summed, t)
                        nc.scalar.activation(sq[:], x[:, t % 3], ACT.Square, accum_out=ss[:, t:t + 1]).then_inc(squares_summed, 1)
                        act.wait_ge(mean_ready, t + 1)
                        nc.scalar.activation(rs[:, t:t + 1], ss[:, t:t + 1], ACT.Sqrt).then_inc(root_ready, 1)
                    if t >= 1:
                        u = t - 1
                        s = u // NTL
                        act.wait_ge(turned, u + 1)
                        for k in range(KD // 2, KD):
                            o = nc.scalar.activation(g.hT[:, k, u * P:(u + 1) * P],
                                                     g.ps[:, 2 * (u % 2) + 1, (k % 4) * P:(k % 4 + 1) * P], ACT.Identity,
                                                     scale=g.gain[:, 0, k, s:s + 1], bias=g.modT[:, k, s:s + 1])
                        o.then_inc(taken_hi, 1)

            @block.vector
            def _(dve):
                for t in range(tiles + 1):
                    if t < tiles:
                        dve.wait_ge(squares_summed, t + 1)
                        nc.vector.tensor_scalar(ss[:, t:t + 1], ss[:, t:t + 1], 1.0 / D, EPS, ALU.mult, ALU.add).then_inc(mean_ready, 1)
                        dve.wait_ge(root_ready, t + 1)
                        nc.vector.reciprocal(rt[:, t:t + 1], rs[:, t:t + 1]).then_inc(rstd_ready, 1)
                        dve.wait_ge(rstd_ready, t + 1)
                        wait(dve, turned, t - 1)
                        nc.vector.tensor_scalar(xn[:, t % 2], x[:, t % 3], rt[:, t:t + 1], None, ALU.mult).then_inc(scaled, 1)
                    if t >= 1:
                        u = t - 1
                        s = u // NTL
                        dst = g.hT[:, 0:4, u * P:(u + 1) * P]
                        dve.wait_ge(turned, u + 1)
                        nc.vector.tensor_tensor(dst, g.ps[:, 2 * (u % 2), :].rearrange("p (k n) -> p k n", k=4),
                                                g.gain[:, 0, 0:4, s:s + 1].to_broadcast([P, 4, P]), ALU.mult).then_inc(step, 1)
                        dve.wait_ge(step, t)
                        nc.vector.tensor_tensor(dst, dst, g.modT[:, 0:4, s:s + 1].to_broadcast([P, 4, P]),
                                                ALU.add).then_inc(taken_lo, 1)

            @block.tensor
            def _(pe):
                for t in range(tiles):
                    pe.wait_ge(scaled, t + 1)
                    wait(pe, taken_lo, t - 1)
                    wait(pe, taken_hi, t - 1)
                    for k in range(KD):
                        mm = nc.tensor.transpose(g.ps[:, 2 * (t % 2) + k // 4, (k % 4) * P:(k % 4 + 1) * P],
                                                 xn[:, t % 2, k * P:(k + 1) * P], g.ident[:])
                    mm.then_inc(turned, 1)


def stage_hyena(nc, g, l, ctx):
    L = CTX if ctx else SEQ
    tok0 = SEQ if ctx else 0
    NL = L // P
    CH = min(L, BANK)
    NC = L // CH
    fil_z, fil_dec, t_dft, t_dft2 = g.hy_tables[ctx]
    with Stage(nc, f"hy{l}{'c' if ctx else ''}") as st:
        Kf = st.sb("Kf", [P, NL, 3 * HY_CH])
        x0 = st.sb("x0", [P, 2, L])
        gv = st.sb("gv", [P, 2, L])
        gT = st.sb("gT", [P, NL, HY_CH])
        with ExitStack() as filt:
            def sb(name, shape):
                return filt.enter_context(nc.sbuf_tensor(f"{name}_{st.tag}", shape, F32))
            zT = sb("zT", [HY_EMB, L])
            w1 = sb("w1", [HY_EMB, HY_FFN])
            w2 = sb("w2", [HY_FFN, HY_FFN])
            w3 = sb("w3", [HY_FFN, 2 * HY_CH])
            cols = sb("cols", [HY_FFN, 3])
            arg = sb("arg", [HY_FFN, L])
            rnd = sb("rnd", [HY_FFN, L])
            hid = sb("hid", [HY_FFN, L])
            dec = sb("dec", [P, 2, 2 * HY_CH])
            fb = sb("fb", [P, 2, 2 * HY_CH])
            kpm = sb("kpm", [P, 2, NL, HY_CH])
            dft = sb("dft", [P, 2, 2, NL, P])
            names = ("small_loaded sin_in sin_ready layer_ready filt_ready filt_taken fb_ready kpm_ready spec_ready spec_taken arg_step").split()
            small_loaded, sin_in, sin_ready, layer_ready, filt_ready, filt_taken, fb_ready, kpm_ready, spec_ready, spec_taken, arg_step = (
                st.sem(n) for n in names)
            dec_loaded = [st.sem(f"dec_loaded{i}") for i in range(2)]
            dft_loaded = [st.sem(f"dft_loaded{i}") for i in range(2)]
            with nc.Block() as block:
                @block.sync
                def _(sp):
                    for dst, src in ((zT[:], fil_z), (w1[:], g.hy_w1[l]), (w2[:], g.hy_w2[l]), (w3[:], g.hy_w3[l]),
                                     (cols[:, 0:1], g.hy_b1[l].rearrange("(p o) -> p o", o=1)),
                                     (cols[:, 1:2], g.hy_b2[l].rearrange("(p o) -> p o", o=1)),
                                     (cols[:, 2:3], g.hy_freq[l].rearrange("(p o) -> p o", o=1))):
                        sp.dma_start(dst, src).then_inc(small_loaded, 16)
                    for t in range(NL):
                        wait(sp, fb_ready, t - 1)
                        sp.dma_start(dec[:, t % 2], fil_dec[t * P:(t + 1) * P, :]).then_inc(dec_loaded[t % 2], 16)
                    for t in range(NL):
                        wait(sp, spec_ready, t - 1)
                        for i in range(2):
                            sp.dma_start(dft[:, t % 2, i], t_dft[i, t]).then_inc(dft_loaded[t % 2], 16)

                @block.tensor
                def _(pe):
                    pe.wait_ge(small_loaded, 16 * 7)
                    for layer in range(2):
                        if layer:
                            pe.wait_ge(sin_ready, 1)
                        for c in range(NC):
                            mm = nc.tensor.matmul(g.ps[0:HY_FFN, c, 0:CH], w2[:] if layer else w1[:],
                                                  (hid if layer else zT)[:, c * CH:(c + 1) * CH], start=True, stop=True)
                        mm.then_inc(layer_ready, 1)
                    pe.wait_ge(sin_ready, 2)
                    for t in range(NL):
                        wait(pe, fb_ready, t - 1)
                        nc.tensor.matmul(g.ps[:, 2 + t % 2, :], hid[:, t * P:(t + 1) * P], w3[:], start=True, stop=True).then_inc(filt_ready, 1)
                    pe.wait_ge(kpm_ready, NL)
                    for t in range(NL):
                        pe.wait_ge(dft_loaded[t % 2], 32 * (t // 2 + 1))
                        wait(pe, spec_taken, t - 1)
                        for i in range(2):
                            for j in range(NL):
                                mm = nc.tensor.matmul(g.ps[:, 4 + 2 * (t % 2) + i, 0:HY_CH], dft[:, t % 2, i, j, :], kpm[:, i, j, :],
                                                      start=j == 0, stop=j == NL - 1)
                        mm.then_inc(spec_ready, 1)

                @block.scalar
                def _(act):
                    for layer in range(2):
                        act.wait_ge(sin_in, layer + 1)
                        nc.scalar.activation(hid[:], arg[:], ACT.Sin).then_inc(sin_ready, 1)

                @block.vector
                def _(dve):
                    link = Chain(dve, arg_step)
                    dve.wait_ge(small_loaded, 16 * 7)
                    for layer in range(2):
                        dve.wait_ge(layer_ready, layer + 1)
                        link(nc.vector.tensor_scalar(arg[:].rearrange("p (c n) -> p c n", c=NC), g.ps[0:HY_FFN, 0:NC, 0:CH],
                                                     cols[:, layer:layer + 1], cols[:, 2:3], ALU.add, ALU.mult))
                        link(nc.vector.tensor_scalar(rnd[:], arg[:], 1.0 / (2 * math.pi), MAGIC, ALU.mult, ALU.add))
                        link(nc.vector.tensor_scalar(rnd[:], rnd[:], -MAGIC, None, ALU.add))
                        for part in TWO_PI_PARTS:
                            link(nc.vector.scalar_tensor_tensor(out=arg[:], in0=rnd[:], scalar=-part, in1=arg[:],
                                                                op0=ALU.mult, op1=ALU.add))
                        nc.vector.tensor_scalar(arg[:], arg[:], PI_DOWN, -PI_DOWN, ALU.min, ALU.max).then_inc(sin_in, 1)
                    for t in range(NL):
                        dve.wait_ge(filt_ready, t + 1)
                        dve.wait_ge(dec_loaded[t % 2], 16 * (t // 2 + 1))
                        wait(dve, kpm_ready, t - 1)
                        nc.vector.tensor_tensor(fb[:, t % 2], g.ps[:, 2 + t % 2, :], dec[:, t % 2], ALU.mult).then_inc(fb_ready, 1)
                        dve.wait_ge(fb_ready, t + 1)
                        nc.vector.tensor_tensor(kpm[:, 0, t], fb[:, t % 2, 0:HY_CH], fb[:, t % 2, HY_CH:], ALU.add)
                        nc.vector.tensor_tensor(kpm[:, 1, t], fb[:, t % 2, 0:HY_CH], fb[:, t % 2, HY_CH:], ALU.subtract).then_inc(kpm_ready, 1)
                    for t in range(NL):
                        dve.wait_ge(spec_ready, t + 1)
                        b = 4 + 2 * (t % 2)
                        nc.vector.tensor_copy(Kf[:, t, 0:2 * HY_CH].rearrange("p (i n) -> p i n", i=2), g.ps[:, b:b + 2, 0:HY_CH])
                        nc.vector.tensor_copy(Kf[:, t, 2 * HY_CH:], g.ps[:, b, 0:HY_CH]).then_inc(spec_taken, 1)
        hb = st.sb("hb", [P, 2])
        with ExitStack() as early:
            def sb(name, shape):
                return early.enter_context(nc.sbuf_tensor(f"{name}_{st.tag}", shape, F32))
            w = sb("w", [P, KD, HY_IN])
            raw = sb("raw", [P, 2, L + 2])
            u1 = sb("u1", [P, L])
            cw = sb("cw", [P, 6, 3])
            w_in_loaded = [st.sem(f"w_in_loaded{i}") for i in range(2)]
            names = ("cw_loaded padded proj_ready proj_taken conv_step tile_ready gv_turned gt_ready").split()
            cw_loaded, padded, proj_ready, proj_taken, conv_step, tile_ready, gv_turned, gt_ready = (st.sem(n) for n in names)
            order = [0, 1, 2, 4, 3, 5]
            with nc.Block() as block:
                @block.sync
                def _(sp):
                    wv = g.w_in[l].rearrange("(k p) n -> p k n", p=P)
                    for i, cols in enumerate((slice(0, 2 * P), slice(2 * P, HY_IN))):
                        sp.dma_start(w[:, :, cols], wv[:, :, cols]).then_inc(w_in_loaded[i], 16)
                    with nc.allow_non_contiguous_dma("filter taps, once a layer"):
                        for i in range(3):
                            sp.dma_start(cw[:, :, i], g.hy_conv[l, i].rearrange("(f p) -> p f", p=P)).then_inc(cw_loaded, 16)
                        sp.dma_start(hb[:], g.hy_bias[l].rearrange("(f p) -> p f", p=P)).then_inc(cw_loaded, 16)

                @block.gpsimd
                def _(pool):
                    pool.memset(raw[:, :, 0:1], 0.0)
                    pool.memset(raw[:, :, L + 1:L + 2], 0.0).then_inc(padded, 1)

                @block.tensor
                def _(pe):
                    n = 0
                    for f in order:
                        pe.wait_ge(w_in_loaded[f > 1], 16)
                        for c in range(NC):
                            wait(pe, proj_taken, n - 3)
                            for k in range(KD):
                                mm = nc.tensor.matmul(g.ps[:, n % 4, 0:CH], w[:, k, f * P:(f + 1) * P],
                                                      g.hT[:, k, tok0 + c * CH:tok0 + (c + 1) * CH], start=k == 0, stop=k == KD - 1)
                            mm.then_inc(proj_ready, 1)
                            n += 1
                    for ct in range(2):
                        pe.wait_ge(tile_ready, 4 + 2 * ct)
                        for t0 in range(0, NL, 4):
                            m = ct * ((NL + 3) // 4) + t0 // 4
                            wait(pe, gt_ready, m - 1)
                            for t in range(t0, min(t0 + 4, NL)):
                                mm = nc.tensor.transpose(g.ps[:, 4 + m % 2, (t - t0) * P:(t - t0 + 1) * P],
                                                         gv[:, ct, t * P:(t + 1) * P], g.ident[:])
                            mm.then_inc(gv_turned, 1)

                @block.scalar
                def _(act):
                    n = 0
                    for j, f in enumerate(order):
                        wait(act, tile_ready, j - 1)
                        for c in range(NC):
                            act.wait_ge(proj_ready, n + 1)
                            nc.scalar.copy(raw[:, j % 2, 1 + c * CH:1 + (c + 1) * CH], g.ps[:, n % 4, 0:CH]).then_inc(proj_taken, 1)
                            n += 1
                    m = 0
                    for ct in range(2):
                        for t0 in range(0, NL, 4):
                            nt = min(4, NL - t0)
                            act.wait_ge(gv_turned, m + 1)
                            nc.scalar.copy(gT[:, t0:t0 + nt, ct * P:(ct + 1) * P],
                                           g.ps[:, 4 + m % 2, 0:nt * P].rearrange("p (t n) -> p t n", n=P)).then_inc(gt_ready, 1)
                            m += 1

                @block.vector
                def _(dve):
                    link = Chain(dve, conv_step)
                    dve.wait_ge(padded, 1)
                    dve.wait_ge(cw_loaded, 64)
                    for j, f in enumerate(order):
                        dve.wait_ge(proj_taken, NC * (j + 1))
                        dst = x0[:, f] if f < 2 else (gv[:, f % 2] if f < 4 else u1[:])
                        r = raw[:, j % 2]
                        link(nc.vector.tensor_scalar(dst, r[:, 0:L], cw[:, f, 0:1], None, ALU.mult))
                        link(nc.vector.scalar_tensor_tensor(out=dst, in0=r[:, 1:L + 1], scalar=cw[:, f, 1:2], in1=dst, op0=ALU.mult, op1=ALU.add))
                        last = nc.vector.scalar_tensor_tensor(out=dst, in0=r[:, 2:L + 2], scalar=cw[:, f, 2:3], in1=dst, op0=ALU.mult, op1=ALU.add)
                        if f < 4:
                            last.then_inc(tile_ready, 1)
                        else:
                            link(last)
                            nc.vector.tensor_tensor(gv[:, f % 2], gv[:, f % 2], u1[:], ALU.mult).then_inc(tile_ready, 1)
                        if f >= 2:
                            dve.wait_ge(tile_ready, j + 1)
        dft2 = st.sb("dft2", [P, 2, 2, NL, P])
        Y = st.sb("Y", [P, 2, NL, HY_CH])
        prod = st.sb("prod", [P, 2, 2, 2 * HY_CH])
        zb = st.sb("zb", [P, 2, L])
        names = "u_ready prod_ready y_ready inv_ready z_step".split()
        u_ready, prod_ready, y_ready, inv_ready, z_step = (st.sem(n) for n in names)
        dft2_loaded = [st.sem(f"dft2_loaded{i}") for i in range(2)]
        with nc.Block() as block:
            @block.sync
            def _(sp):
                for t in range(NL):
                    wait(sp, u_ready, t - 1)
                    for i in range(2):
                        sp.dma_start(dft2[:, t % 2, i], t_dft2[i, t]).then_inc(dft2_loaded[t % 2], 16)
                for t in range(NL):
                    wait(sp, u_ready, NL)
                    wait(sp, inv_ready, t - 1)
                    for i in range(2):
                        sp.dma_start(dft2[:, t % 2, i], g.hy_rows[ctx][i, t * P:(t + 1) * P, :].rearrange("p (j n) -> p j n", n=P)).then_inc(dft2_loaded[t % 2], 16)

            @block.tensor
            def _(pe):
                for t in range(NL):
                    pe.wait_ge(dft2_loaded[t % 2], 32 * (t // 2 + 1))
                    wait(pe, prod_ready, t - 1)
                    for i in range(2):
                        for j in range(NL):
                            mm = nc.tensor.matmul(g.ps[:, t % 2, i * HY_CH:(i + 1) * HY_CH], dft2[:, t % 2, i, j, :], gT[:, j, :],
                                                  start=j == 0, stop=j == NL - 1)
                    mm.then_inc(u_ready, 1)
                for t in range(NL):
                    pe.wait_ge(dft2_loaded[t % 2], 32 * ((NL + t) // 2 + 1))
                    pe.wait_ge(y_ready, NL)
                    for ct in range(2):
                        for c in range(NC):
                            for i in range(2):
                                mm = nc.tensor.matmul(g.ps[:, 4 + 2 * ct + c, 0:CH], Y[:, i, t, ct * P:(ct + 1) * P],
                                                      dft2[:, t % 2, i].rearrange("p j n -> p (j n)")[:, c * CH:(c + 1) * CH],
                                                      start=t == 0 and i == 0, stop=t == NL - 1 and i == 1)
                    mm.then_inc(inv_ready, 1)

            @block.vector
            def _(dve):
                for t in range(NL):
                    dve.wait_ge(u_ready, t + 1)
                    wait(dve, y_ready, t - 1)
                    nc.vector.tensor_tensor(prod[:, t % 2, 0], g.ps[:, t % 2, :], Kf[:, t, 0:2 * HY_CH], ALU.mult)
                    nc.vector.tensor_tensor(prod[:, t % 2, 1], g.ps[:, t % 2, :], Kf[:, t, HY_CH:], ALU.mult).then_inc(prod_ready, 1)
                    dve.wait_ge(prod_ready, t + 1)
                    nc.vector.tensor_tensor(Y[:, 0, t], prod[:, t % 2, 0, 0:HY_CH], prod[:, t % 2, 0, HY_CH:], ALU.subtract)
                    nc.vector.tensor_tensor(Y[:, 1, t], prod[:, t % 2, 1, 0:HY_CH], prod[:, t % 2, 1, HY_CH:], ALU.add).then_inc(y_ready, 1)
                link = Chain(dve, z_step)
                for ct in range(2):
                    link(nc.vector.tensor_scalar(zb[:, ct], gv[:, ct], hb[:, ct:ct + 1], None, ALU.mult))
                dve.wait_ge(inv_ready, NL)
                for ct in range(2):
                    z = zb[:, ct].rearrange("p (c n) -> p c n", c=NC)
                    link(nc.vector.scalar_tensor_tensor(out=z, in0=g.ps[:, 4 + 2 * ct:4 + 2 * ct + NC, 0:CH], scalar=1.0 / L, in1=z,
                                                        op0=ALU.mult, op1=ALU.add))
                    link(nc.vector.tensor_tensor(g.yT[:, ct, tok0:tok0 + L], zb[:, ct], x0[:, ct], ALU.mult))


TWO_PI_PARTS = [6.28125, 2 * math.pi - 6.28125]
PI_DOWN = float(np.nextafter(np.float32(math.pi), np.float32(0)))


def project(nc, g, st, tag, load, loads, groups):
    names = "first_loaded rest_loaded group_ready dve_took act_took".split()
    first_loaded, rest_loaded, group_ready, dve_took, act_took = (st.sem(f"{n}_{tag}") for n in names)
    took = (dve_took, act_took)
    with nc.Block() as block:
        @block.sync
        def _(sp):
            load(sp, first_loaded, rest_loaded)

        @block.tensor
        def _(pe):
            pe.wait_ge(first_loaded, 16 * loads)
            for n, (products, dst, view) in enumerate(groups):
                if n == 2 * len(CHUNKS):
                    pe.wait_ge(rest_loaded, 16)
                wait(pe, took[n % 2], n // 2 - 1)
                for c0, width, lhs, rhs in products:
                    for k in range(KD):
                        mm = nc.tensor.matmul(g.ps[:, n % 4, c0:c0 + width], lhs(k), rhs(k), start=k == 0, stop=k == KD - 1)
                mm.then_inc(group_ready, 1)

        @block.vector
        def _(dve):
            for n in range(0, len(groups), 2):
                dve.wait_ge(group_ready, n + 1)
                nc.vector.tensor_copy(groups[n][1], groups[n][2](g.ps[:, n % 4, :])).then_inc(dve_took, 1)

        @block.scalar
        def _(act):
            for n in range(1, len(groups), 2):
                act.wait_ge(group_ready, n + 1)
                nc.scalar.copy(groups[n][1], groups[n][2](g.ps[:, n % 4, :])).then_inc(act_took, 1)


def feature_groups(g, dsts, lhs):
    return [([(0, n, lambda k, f=f: lhs(f, k), lambda k, c0=c0, n=n: g.hT[:, k, c0:c0 + n])],
             dst[:, c0:c0 + n], lambda bank, n=n: bank[:, 0:n])
            for f, dst in enumerate(dsts) for c0, n in CHUNKS]


def token_groups(g, dst, width, rhs):
    per = BANK // width
    out = []
    for t0 in range(0, NT, per):
        ts = range(t0, min(t0 + per, NT))
        out.append(([((t - t0) * width, width, lambda k, t=t: g.hT[:, k, t * P:(t + 1) * P], rhs) for t in ts],
                    dst[:, t0:t0 + len(ts), :],
                    lambda bank, m=len(ts): bank[:, 0:m * width].rearrange("p (t n) -> p t n", n=width)))
    return out


class Job:

    def __init__(self, q, scores, soft, values, sink=None):
        self.q, self.scores, self.soft, self.values, self.sink = q, scores, soft, values, sink
        self.cols = soft[-1][1]
        self.lo = min(4, len(values) - 1)


def attend(nc, g, st, jobs, out_tiles, scale):
    NJ = len(jobs)
    width = max(j.cols for j in jobs) + 1
    NPT = max(len(j.values) for j in jobs)
    S = st.sb("S", [P, 2, width])
    PR = st.sb("PR", [P, 2, width])
    PT = st.sb("PT", [P, 2, NPT, P])
    mx = st.sb("mx", [P, 2, 4])
    sums = st.sb("sums", [P, 2, 4])
    inv = st.sb("inv", [P, 4])
    on = st.sb("on", [P, 2, 2 * P])
    names = ("scores_ready soft_ready sink_put max_step exp_ready turned_lo turned_hi copied_lo copied_hi "
             "pv_ready inv_ready normed out_turned out_put").split()
    (scores_ready, soft_ready, sink_put, max_step, exp_ready, turned_lo, turned_hi, copied_lo, copied_hi,
     pv_ready, inv_ready, normed, out_turned, out_put) = (st.sem(n) for n in names)
    with nc.Block() as block:
        @block.tensor
        def _(pe):
            def scores(j):
                wait(pe, soft_ready, j - 1)
                for c0, k, n in jobs[j].scores:
                    bank = 2 * (j % 2) + c0 // BANK
                    mm = nc.tensor.matmul(g.ps[:, bank, c0 % BANK:c0 % BANK + n], jobs[j].q, k, start=True, stop=True)
                mm.then_inc(scores_ready, 1)

            def turn(j):
                pe.wait_ge(exp_ready, j + 1)
                wait(pe, copied_lo, j)
                wait(pe, copied_hi, j)
                lo = jobs[j].lo
                for i, (c0, n, _) in enumerate(jobs[j].values):
                    at = (i if i < lo else i - lo) * P
                    mm = nc.tensor.transpose(g.ps[0:n, 4 if i < lo else 5, at:at + P], PR[:, j % 2, c0:c0 + n], g.ident[:])
                    if i == lo - 1:
                        mm.then_inc(turned_lo, 1)
                mm.then_inc(turned_hi, 1)

            def weigh(j):
                pe.wait_ge(copied_lo, j + 1)
                pe.wait_ge(copied_hi, j + 1)
                if j % 4 == 0:
                    wait(pe, normed, j // 4)
                vals = jobs[j].values
                for i, (c0, n, v) in enumerate(vals):
                    mm = nc.tensor.matmul(g.ps[:, 6, (j % 4) * HD:(j % 4 + 1) * HD], PT[0:n, j % 2, i, :], v,
                                          start=i == 0, stop=i == len(vals) - 1)
                mm.then_inc(pv_ready, 1)
                if j % 4 == 3:
                    b = j // 4
                    pe.wait_ge(normed, b + 1)
                    wait(pe, out_put, b)
                    for i in range(2):
                        mm = nc.tensor.transpose(g.ps[:, 7, i * P:(i + 1) * P], on[:, b % 2, i * P:(i + 1) * P], g.ident[:])
                    mm.then_inc(out_turned, 1)

            def raise_clock():
                for _ in range(5):
                    nc.tensor.matmul(g.ps[:, 7, :], g.ident[:], g.hT[:, 0, 0:BANK], start=True, stop=True)

            scores(0)
            for j in range(NJ):
                if j == 2:
                    raise_clock()
                if j + 1 < NJ:
                    scores(j + 1)
                turn(j)
                if j >= 1:
                    weigh(j - 1)
            weigh(NJ - 1)

        @block.vector
        def _(dve):
            link = Chain(dve, max_step)

            def soft(j):
                job = jobs[j]
                dve.wait_ge(scores_ready, j + 1)
                wait(dve, exp_ready, j - 1)
                if job.sink is not None:
                    nc.vector.tensor_copy(S[:, j % 2, job.cols:job.cols + 1], job.sink).then_inc(sink_put, 1)
                flat = g.ps[:, 2 * (j % 2):2 * (j % 2) + 2, :].rearrange("p b n -> p (b n)")
                for i, (a, b, addend) in enumerate(job.soft):
                    first = -3e38 if job.sink is None else job.sink
                    link(nc.vector.tensor_tensor_reduce(S[:, j % 2, a:b], flat[:, a:b], addend, scale,
                                                        mx[:, j % 2, i - 1:i] if i else first, ALU.add, ALU.max,
                                                        mx[:, j % 2, i:i + 1]))
                i = len(job.soft) - 1
                nc.vector.tensor_scalar(mx[:, j % 2, 3:4], mx[:, j % 2, i:i + 1], -1.0, None, ALU.mult).then_inc(soft_ready, 1)

            def copy(j):
                dve.wait_ge(turned_lo, j + 1)
                wait(dve, pv_ready, j - 1)
                m = jobs[j].lo
                nc.vector.tensor_copy(PT[:, j % 2, 0:m, :], g.ps[:, 4, 0:m * P].rearrange("p (i n) -> p i n", n=P)).then_inc(copied_lo, 1)

            def norm(b):
                dve.wait_ge(exp_ready, 4 * b + 4)
                wait(dve, inv_ready, b)
                nc.vector.reciprocal(inv[:], sums[:, b % 2, :]).then_inc(inv_ready, 1)
                dve.wait_ge(inv_ready, b + 1)
                dve.wait_ge(pv_ready, 4 * b + 4)
                wait(dve, out_turned, b - 1)
                nc.vector.tensor_tensor(on[:, b % 2, :].rearrange("p (h n) -> p h n", h=4),
                                        g.ps[:, 6, 0:4 * HD].rearrange("p (h n) -> p h n", h=4),
                                        inv[:].unsqueeze(2).to_broadcast([P, 4, HD]), ALU.mult).then_inc(normed, 1)

            for j in range(NJ + 1):
                if j < NJ:
                    soft(j)
                if j >= 1:
                    copy(j - 1)
                if j >= 2 and (j - 2) % 4 == 3:
                    norm((j - 2) // 4)
            norm(NJ // 4 - 1)

        @block.scalar
        def _(act):
            def exp(j):
                job = jobs[j]
                act.wait_ge(soft_ready, j + 1)
                if job.sink is not None:
                    act.wait_ge(sink_put, j + 1)
                wait(act, turned_lo, j - 1)
                wait(act, turned_hi, j - 1)
                if j % 4 == 0:
                    wait(act, inv_ready, j // 4 - 1)
                n = job.cols + (job.sink is not None)
                nc.scalar.activation(PR[:, j % 2, 0:n], S[:, j % 2, 0:n], ACT.Exp, bias=mx[:, j % 2, 3:4],
                                     accum_out=sums[:, (j // 4) % 2, j % 4:j % 4 + 1]).then_inc(exp_ready, 1)

            def copy(j):
                act.wait_ge(turned_hi, j + 1)
                wait(act, pv_ready, j - 1)
                vals = jobs[j].values
                lo, full = jobs[j].lo, sum(n == P for _, n, _ in vals)
                m = full - lo
                last = nc.scalar.copy(PT[:, j % 2, lo:full, :], g.ps[:, 5, 0:m * P].rearrange("p (i n) -> p i n", n=P)) if m else None
                if full < len(vals):
                    n = vals[-1][1]
                    last = nc.scalar.copy(PT[0:n, j % 2, full, :], g.ps[0:n, 5, m * P:(m + 1) * P])
                last.then_inc(copied_hi, 1)

            def put(b):
                f, tok = out_tiles[b]
                act.wait_ge(out_turned, b + 1)
                nc.scalar.copy(g.yT[:, f:f + 2, tok:tok + P], g.ps[:, 7, 0:2 * P].rearrange("p (f n) -> p f n", f=2)).then_inc(out_put, 1)

            for j in range(NJ):
                exp(j)
                if j >= 1:
                    copy(j - 1)
                if j >= 8 and j % 4 == 0:
                    put(j // 4 - 2)
            copy(NJ - 1)
            for b in range(max(0, (NJ - 1) // 4 - 1), NJ // 4):
                put(b)


def stage_window(nc, g, l, ctx):
    with Stage(nc, f"wa{l}") as st:
        qk = st.sb("qk", [P, 3, TOK])
        v = st.sb("v", [P, NT, P])
        mask = st.sb("mask", [P, CTX + 3 * P])
        sinks = st.sb("sinks", [P, 4])
        zero = st.sb("zero", [P, CTX])
        small_loaded = st.sem("small_loaded")
        with ExitStack() as early:
            w = early.enter_context(nc.sbuf_tensor(f"w_{st.tag}", [P, KD, WA_IN], F32))

            def load(sp, first_loaded, rest_loaded):
                wv = g.w_in[l].rearrange("(k p) n -> p k n", p=P)[:, :, WA0:WA0 + WA_IN]
                for h in range(4):
                    to = (h % 2 * 2 + h // 2) * HD
                    sp.dma_start(w[:, :, to:to + HD], wv[:, :, h * HD:(h + 1) * HD]).then_inc(first_loaded, 16)
                sp.dma_start(w[:, :, 256:], wv[:, :, 256:]).then_inc(rest_loaded, 16)
                sp.dma_start(mask[:], g.t_wa_mask).then_inc(small_loaded, 16)
                sp.dma_start(sinks[:], g.wa_sink[l].rearrange("(o n) -> o n", o=1).to_broadcast([P, 4])).then_inc(small_loaded, 16)
                sp.wait_ge(small_loaded, 32)

            project(nc, g, st, "p", load, 4,
                    feature_groups(g, [qk[:, f] for f in range(3)], lambda f, k: w[:, k, f * P:(f + 1) * P]) + token_groups(g, v, P, lambda k: w[:, k, 384:512]))
        with ExitStack() as early:
            rope = early.enter_context(nc.sbuf_tensor(f"rope_{st.tag}", [P, 2, SEQ], F32))
            rot = early.enter_context(nc.sbuf_tensor(f"rot_{st.tag}", [P, P], F32))
            tmp = early.enter_context(nc.sbuf_tensor(f"tmp_{st.tag}", [P, 2, BANK], F32))
            rope_loaded, rotated, tmp_ready, scaled, roped = (st.sem(n) for n in "rope_loaded rotated tmp_ready scaled roped".split())
            spans = [(f, c) for f in range(3) for c in range(2)]
            with nc.Block() as block:
                @block.sync
                def _(sp):
                    sp.dma_start(rope[:], g.t_rope.rearrange("i p n -> p i n")).then_inc(rope_loaded, 16)
                    sp.dma_start(rot[:], g.t_rot).then_inc(rope_loaded, 16)

                @block.gpsimd
                def _(pool):
                    pool.memset(zero[:], 0.0)

                @block.tensor
                def _(pe):
                    pe.wait_ge(rope_loaded, 32)
                    for n, (f, c) in enumerate(spans):
                        wait(pe, tmp_ready, n - 1)
                        nc.tensor.matmul(g.ps[:, n % 2, :], rot[:], qk[:, f, c * BANK:(c + 1) * BANK], start=True, stop=True).then_inc(rotated, 1)

                @block.vector
                def _(dve):
                    dve.wait_ge(rope_loaded, 32)
                    for n, (f, c) in enumerate(spans):
                        cols = slice(c * BANK, (c + 1) * BANK)
                        dve.wait_ge(rotated, n + 1)
                        wait(dve, roped, n - 1)
                        nc.vector.tensor_tensor(tmp[:, n % 2], g.ps[:, n % 2, :], rope[:, 1, cols], ALU.mult).then_inc(tmp_ready, 1)
                        nc.vector.tensor_tensor(qk[:, f, cols], qk[:, f, cols], rope[:, 0, cols], ALU.mult).then_inc(scaled, 1)
                        dve.wait_ge(tmp_ready, n + 1)
                        dve.wait_ge(scaled, n + 1)
                        nc.vector.tensor_tensor(qk[:, f, cols], qk[:, f, cols], tmp[:, n % 2], ALU.add).then_inc(roped, 1)
        jobs, outs = [], []
        for t in range(NTL + (NTC if ctx else 0)):
            for grp in range(2):
                for r in range(2):
                    half = slice(grp * HD, (grp + 1) * HD)
                    q = qk[half, r, t * P:(t + 1) * P]
                    key, dv = qk[half, 2], slice(grp * HD, (grp + 1) * HD)
                    scores = [(0, key[:, SEQ:TOK], CTX)]
                    values = [(i * P, P, v[:, NTL + i, dv]) for i in range(NTC)]
                    m0, cols = CTX, CTX
                    if t < NTL:
                        lo, hi = max(t - 1, 0), min(t + 2, NTL)
                        m0 = CTX + (lo - (t - 1)) * P
                        for i, u in enumerate(range(lo, hi)):
                            scores.append((CTX + i * P, key[:, u * P:(u + 1) * P], P))
                            values.append((CTX + i * P, P, v[:, u, dv]))
                        cols = CTX + (hi - lo) * P
                    h = 2 * grp + r
                    if m0 == CTX:
                        soft = [(0, cols, mask[:, 0:cols])] if t < NTL else [(0, CTX, zero[:])]
                    else:
                        soft = [(0, CTX, zero[:]), (CTX, cols, mask[:, m0:m0 + cols - CTX])]
                    jobs.append(Job(q, scores, soft, values, sinks[:, h:h + 1]))
            outs.append((2, t * P))
        attend(nc, g, st, jobs, outs, SCALE)


def stage_neighbour(nc, g, l, ctx):
    NR = 2 * NA_KR - 1
    NB = 2 * NA_KR
    with Stage(nc, f"na{l}") as st:
        qk = st.sb("qk", [P, 4, TOK])
        v = st.sb("v", [P, NT, 2 * P])
        bias = st.sb("bias", [P, 4, NB, GRID_W])
        inner = st.sb("inner", [P, 4, NA_KR + 1, GRID_W])
        zero = st.sb("zero", [P, CTX])
        with ExitStack() as early:
            sel = early.enter_context(nc.sbuf_tensor(f"sel_{st.tag}", [32, GRID_W * P], F32))
            rpb = early.enter_context(nc.sbuf_tensor(f"rpb_{st.tag}", [4 * NR, 2 * NA_KC - 1], F32))
            rpbT = early.enter_context(nc.sbuf_tensor(f"rpbT_{st.tag}", [32, 4 * NR], F32))
            names = "sel_loaded rpb_turned rpb_filled rpb_ready bias_ready bias_taken cleared copied".split()
            sel_loaded, rpb_turned, rpb_filled, rpb_ready, bias_ready, bias_taken, cleared, copied = (st.sem(n) for n in names)
            with nc.Block() as block:
                @block.sync
                def _(sp):
                    sp.dma_start(rpb[:], g.na_rpb[l].rearrange("h r c -> (h r) c")).then_inc(sel_loaded, 16)
                    sp.dma_start(sel[:], g.t_na_sel).then_inc(sel_loaded, 16)

                @block.gpsimd
                def _(pool):
                    pool.memset(zero[:], 0.0).then_inc(cleared, 1)
                    pool.memset(rpbT[:], NEG).then_inc(rpb_filled, 1)

                @block.tensor
                def _(pe):
                    pe.wait_ge(sel_loaded, 32)
                    nc.tensor.transpose(g.ps[0:31, 4, 0:4 * NR], rpb[:], g.ident[0:4 * NR, 0:4 * NR]).then_inc(rpb_turned, 1)
                    pe.wait_ge(rpb_ready, 1)
                    for n in range(8):
                        wait(pe, bias_taken, n - 1)
                        for i in range(8):
                            ck = 8 * n + i
                            mm = nc.tensor.matmul(g.ps[:, n % 2, i * 4 * NR:(i + 1) * 4 * NR], sel[:, ck * P:(ck + 1) * P], rpbT[:],
                                                  start=True, stop=True)
                        mm.then_inc(bias_ready, 1)

                @block.vector
                def _(dve):
                    dve.wait_ge(rpb_filled, 1)
                    dve.wait_ge(rpb_turned, 1)
                    nc.vector.tensor_scalar(rpbT[0:31, :], g.ps[0:31, 4, 0:4 * NR], 1.0 / SCALE, None, ALU.mult).then_inc(rpb_ready, 1)
                    for n in range(8):
                        dve.wait_ge(bias_ready, n + 1)
                        for rr in range(2):
                            half = slice(rr * HD, (rr + 1) * HD)
                            for h in range(4):
                                src = g.ps[half, n % 2, 0:32 * NR].rearrange("p (c h r) -> p h r c", h=4, r=NR)[:, h]
                                last = nc.vector.tensor_copy(bias[half, h, rr:rr + NR, 8 * n:8 * n + 8], src)
                        last.then_inc(bias_taken, 1)
                    dve.wait_ge(bias_taken, 8)
                    for rr in range(2):
                        half = slice(rr * HD, (rr + 1) * HD)
                        nc.vector.tensor_copy(inner[half, :, rr:rr + NA_KR, :], bias[half, :, 3 + rr:3 + rr + NA_KR, :])
                        edge = NA_KR if rr == 0 else 0
                        last = nc.vector.memset(inner[half, :, edge:edge + 1, :], NEG)
        with ExitStack() as early:
            w = early.enter_context(nc.sbuf_tensor(f"w_{st.tag}", [P, KD, NA_IN], F32))

            def load(sp, first_loaded, rest_loaded):
                wv = g.w_in[l].rearrange("(k p) n -> p k n", p=P)[:, :, NA0:NA0 + NA_IN]
                sp.dma_start(w[:, :, 0:2 * P], wv[:, :, 0:2 * P]).then_inc(first_loaded, 16)
                sp.dma_start(w[:, :, 2 * P:], wv[:, :, 2 * P:]).then_inc(rest_loaded, 16)

            project(nc, g, st, "p", load, 1,
                    feature_groups(g, [qk[:, f] for f in range(4)], lambda f, k: w[:, k, f * P:(f + 1) * P])
                    + token_groups(g, v, 2 * P, lambda k: w[:, k, 512:768]))
        jobs, outs = [], []
        for t in range(NTL + (NTC if ctx else 0)):
            for h in range(4):
                half = slice(h % 2 * HD, (h % 2 + 1) * HD)
                dv = slice(h * HD, (h + 1) * HD)
                q = qk[half, h // 2, t * P:(t + 1) * P]
                key = qk[half, 2 + h // 2]
                scores = [(0, key[:, SEQ:TOK], CTX)]
                values = [(i * P, P, v[:, NTL + i, dv]) for i in range(NTC)]
                soft = [(0, CTX, zero[:])]
                if t < NTL:
                    first = min(max(2 * t - NA_KR // 2, 0), SEQ // GRID_W - NA_KR)
                    last = min(max(2 * t + 1 - NA_KR // 2, 0), SEQ // GRID_W - NA_KR)
                    rows = last - first + NA_KR
                    k0, n = first * GRID_W, rows * GRID_W
                    scores += [(CTX, key[:, k0:k0 + CTX], CTX), (BANK, key[:, k0 + CTX:k0 + n], n - CTX)]
                    for i in range(0, n, P):
                        m = min(P, n - i)
                        values.append((CTX + i, m, v[0:m, (k0 + i) // P, dv]))
                    b = first - 2 * t + NA_KR - 1
                    table = inner[:, h] if rows > NA_KR else bias[:, h, b:b + NA_KR, :]
                    soft.append((CTX, CTX + n, table.rearrange("p r c -> p (r c)")))
                jobs.append(Job(q, scores, soft, values))
            outs.append((4, t * P))
        attend(nc, g, st, jobs, outs, SCALE)


def stage_gdn(nc, g, l):
    C = 64
    FW = 4 * C
    GV = 7
    SEG = SEQ + 3
    with Stage(nc, f"gd{l}") as st:
        qkv = st.sb("qkv", [P, NT, 3 * GW])
        gate = st.sb("gate", [P, NT, GW])
        ab = st.sb("ab", [P, NT, 16])
        with ExitStack() as early:
            def sb(name, shape):
                return early.enter_context(nc.sbuf_tensor(f"{name}_{st.tag}", shape, F32))
            w = sb("w", [P, 2, KD, P])
            wg = sb("wg", [P, KD, GW + 16])
            raw = sb("raw", [P, 2, SEG + CTX + 3])
            u = sb("u", [P, TOK])
            s = sb("s", [P, 2, TOK])
            cw = sb("cw", [P, 6, 4])
            names = "cw_loaded wg_loaded padded proj_ready proj_taken conv_ready silu_ready turned tm_dve tm_act gate_ready gate_taken ab_ready ab_taken conv_step".split()
            (cw_loaded, wg_loaded, padded, proj_ready, proj_taken, conv_ready, silu_ready, turned, tm_dve, tm_act, gate_ready,
             gate_taken, ab_ready, ab_taken, conv_step) = (st.sem(n) for n in names)
            w_loaded = [st.sem(f"w_loaded{i}") for i in range(2)]
            wv = g.w_in[l].rearrange("(k p) n -> p k n", p=P)
            starts = [(2, 0, SEQ), (SEG + 2, SEQ, CTX)]
            TS = [(0, 4), (4, 8), (8, 10)]
            with nc.Block() as block:
                @block.sync
                def _(sp):
                    for f in range(6):
                        wait(sp, proj_ready, 3 * (f - 1))
                        sp.dma_start(w[:, f % 2], wv[:, :, GD0 + f * P:GD0 + (f + 1) * P]).then_inc(w_loaded[f % 2], 16)
                        if f == 1:
                            with nc.allow_non_contiguous_dma("filter taps, once a layer"):
                                for i in range(4):
                                    sp.dma_start(cw[:, :, i], g.gdn_conv[l, i].rearrange("(f p) -> p f", p=P)).then_inc(cw_loaded, 16)
                    sp.dma_start(wg[:], wv[:, :, GD0 + 3 * GW:]).then_inc(wg_loaded, 16)

                @block.gpsimd
                def _(pool):
                    pool.memset(raw[:, :, 0:2], 0.0)
                    pool.memset(raw[:, :, SEQ + 2:SEQ + 5], 0.0)
                    pool.memset(raw[:, :, SEG + CTX + 2:SEG + CTX + 3], 0.0).then_inc(padded, 1)

                @block.tensor
                def _(pe):
                    def project_tile(f):
                        pe.wait_ge(w_loaded[f % 2], 16 * (f // 2 + 1))
                        for i, (c0, n) in enumerate(CHUNKS):
                            m = 3 * f + i
                            wait(pe, proj_taken, m - 1)
                            for k in range(KD):
                                mm = nc.tensor.matmul(g.ps[:, m % 2, 0:n], w[:, f % 2, k, :], g.hT[:, k, c0:c0 + n],
                                                      start=k == 0, stop=k == KD - 1)
                            mm.then_inc(proj_ready, 1)

                    def turn_tile(f):
                        pe.wait_ge(silu_ready, f + 1)
                        wait(pe, tm_dve, 2 * f)
                        wait(pe, tm_act, f)
                        for i, (t0, t1) in enumerate(TS):
                            for t in range(t0, t1):
                                mm = nc.tensor.transpose(g.ps[:, 2 + i, (t - t0) * P:(t - t0 + 1) * P],
                                                         s[:, f % 2, t * P:(t + 1) * P], g.ident[:])
                        mm.then_inc(turned, 1)

                    for f in range(6):
                        project_tile(f)
                        if f >= 1:
                            turn_tile(f - 1)
                    turn_tile(5)
                    pe.wait_ge(wg_loaded, 16)
                    for t in range(NT):
                        for k in range(KD):
                            mm = nc.tensor.matmul(g.ps[:, 7, t * 16:(t + 1) * 16], g.hT[:, k, t * P:(t + 1) * P],
                                                  wg[:, k, GW:GW + 16], start=k == 0, stop=k == KD - 1)
                    mm.then_inc(ab_ready, 1)
                    for t in range(NT):
                        wait(pe, gate_taken, t - 1)
                        for k in range(KD):
                            mm = nc.tensor.matmul(g.ps[:, 5 + t % 2, 0:GW], g.hT[:, k, t * P:(t + 1) * P],
                                                  wg[:, k, 0:GW], start=k == 0, stop=k == KD - 1)
                        mm.then_inc(gate_ready, 1)

                @block.scalar
                def _(act):
                    def take(f):
                        wait(act, conv_ready, f - 1)
                        for i, (c0, n) in enumerate(CHUNKS):
                            at = c0 + 2 if c0 < SEQ else SEG + 2
                            act.wait_ge(proj_ready, 3 * f + i + 1)
                            nc.scalar.copy(raw[:, f % 2, at:at + n], g.ps[:, (3 * f + i) % 2, 0:n]).then_inc(proj_taken, 1)

                    def silu(f):
                        act.wait_ge(conv_ready, f + 1)
                        wait(act, turned, f - 1)
                        nc.scalar.activation(s[:, f % 2], u[:], ACT.Silu).then_inc(silu_ready, 1)

                    def place(f):
                        act.wait_ge(turned, f + 1)
                        nc.scalar.copy(qkv[:, 8:10, f * P:(f + 1) * P], g.ps[:, 4, 0:2 * P].rearrange("p (t n) -> p t n", n=P)).then_inc(tm_act, 1)

                    for f in range(6):
                        if f >= 2:
                            place(f - 2)
                        take(f)
                        if f >= 1:
                            silu(f - 1)
                    silu(5)
                    place(4)
                    place(5)
                    for t in range(NT):
                        act.wait_ge(gate_ready, t + 1)
                        nc.scalar.activation(gate[:, t, :], g.ps[:, 5 + t % 2, 0:GW], ACT.Silu).then_inc(gate_taken, 1)

                @block.vector
                def _(dve):
                    link = Chain(dve, conv_step)

                    def conv(f):
                        dve.wait_ge(proj_taken, 3 * f + 3)
                        wait(dve, silu_ready, f)
                        for tap in range(4):
                            for a, c0, n in starts:
                                r = raw[:, f % 2, a - 2 + tap:a - 2 + tap + n]
                                dst = u[:, c0:c0 + n]
                                if tap == 0:
                                    o = nc.vector.tensor_scalar(dst, r, cw[:, f, 0:1], None, ALU.mult)
                                else:
                                    o = nc.vector.scalar_tensor_tensor(out=dst, in0=r, scalar=cw[:, f, tap:tap + 1], in1=dst, op0=ALU.mult, op1=ALU.add)
                                if tap < 3:
                                    link(o)
                        o.then_inc(conv_ready, 1)

                    def place(f):
                        dve.wait_ge(turned, f + 1)
                        for i in range(2):
                            nc.vector.tensor_copy(qkv[:, 4 * i:4 * i + 4, f * P:(f + 1) * P],
                                                  g.ps[:, 2 + i, :].rearrange("p (t n) -> p t n", n=P)).then_inc(tm_dve, 1)

                    dve.wait_ge(padded, 1)
                    dve.wait_ge(cw_loaded, 64)
                    for f in range(6):
                        if f >= 2:
                            place(f - 2)
                        conv(f)
                    place(4)
                    place(5)
                    dve.wait_ge(ab_ready, 1)
                    nc.vector.tensor_copy(ab[:], g.ps[:, 7, 0:NT * 16].rearrange("p (t n) -> p t n", n=16)).then_inc(ab_taken, 1)
        scal = st.sb("scal", [P, NT, 2, GV, 4])
        o_sum = st.sb("o_sum", [P, NT, GW])
        M = {n: st.sb(n, [P] + s) for n, s in g.gdn_masks.items()}
        with ExitStack() as early:
            def sb(name, shape):
                return early.enter_context(nc.sbuf_tensor(f"{name}_{st.tag}", shape, F32))
            cum = sb("cum", [P, 3, P])
            sq = sb("sq", [P, 2, 2 * GW])
            nrm = sb("nrm", [P, NT, 8])
            al = sb("al", [P, 2, 8])
            xs = sb("xs", [P, NT, 8])
            ax = sb("ax", [P, NT, 8])
            names = "masks_loaded al_loaded a_ready al_exp soft_in soft_exp soft_ln ln_in g_ready sums_ready sums_copied decay_ready root_in root_ready l2_step gate_step cleared".split()
            (masks_loaded, al_loaded, a_ready, al_exp, soft_in, soft_exp, soft_ln, ln_in, g_ready, sums_ready, sums_copied, decay_ready,
             root_in, root_ready, l2_step, gate_step, cleared) = (st.sem(n) for n in names)
            with nc.Block() as block:
                @block.sync
                def _(sp):
                    for n in M:
                        sp.dma_start(M[n][:], g.tables[f"t_{n}"]).then_inc(masks_loaded, 16)
                    sp.dma_start(cum[:], g.tables["t_gd_cum"]).then_inc(masks_loaded, 16)
                    for i, src in enumerate((g.gdn_a_log, g.gdn_dt_bias)):
                        sp.dma_start(al[:, i], src[l].rearrange("(o d) h -> o (d h)", o=1).to_broadcast([P, 8])).then_inc(al_loaded, 16)
                    sp.wait_ge(masks_loaded, 16 * (len(M) + 1))

                @block.gpsimd
                def _(pool):
                    pool.memset(o_sum[:], 0.0)

                @block.tensor
                def _(pe):
                    pe.wait_ge(masks_loaded, 16 * (len(M) + 1))
                    pe.wait_ge(g_ready, 1)
                    for d in range(2):
                        gd = scal[:, :, d, 0, :]
                        nc.tensor.matmul(g.ps[:, 0, d * 40:d * 40 + 40], cum[:, d, :], gd, start=True, stop=True)
                        mm = nc.tensor.matmul(g.ps[:, 0, 80 + d * 40:120 + d * 40], cum[:, 2, :], gd, start=True, stop=True)
                    mm.then_inc(sums_ready, 1)

                @block.scalar
                def _(act):
                    act.wait_ge(al_loaded, 32)
                    nc.scalar.activation(al[:, 0], al[:, 0], ACT.Exp).then_inc(al_exp, 1)
                    act.wait_ge(soft_in, 1)
                    nc.scalar.activation(ax[:], ax[:], ACT.Exp).then_inc(soft_exp, 1)
                    nc.scalar.activation(ab[:, :, 8:16], ab[:, :, 8:16], ACT.Exp, scale=-1.0).then_inc(soft_exp, 1)
                    act.wait_ge(ln_in, 1)
                    nc.scalar.activation(ax[:], ax[:], ACT.Ln).then_inc(soft_ln, 1)
                    act.wait_ge(decay_ready, 1)
                    for v in (3, 4, 6):
                        nc.scalar.activation(scal[:, :, :, v, :], scal[:, :, :, v, :], ACT.Exp).then_inc(decay_ready, 1)
                    act.wait_ge(root_in, 1)
                    nc.scalar.activation(nrm[:], nrm[:], ACT.Sqrt).then_inc(root_ready, 1)

                @block.vector
                def _(dve):
                    link = Chain(dve, gate_step)
                    dve.wait_ge(al_loaded, 32)
                    link(nc.vector.tensor_tensor(xs[:], ab[:, :, 0:8], al[:, 1:2, :].to_broadcast([P, NT, 8]), ALU.add))
                    link(nc.vector.tensor_scalar(ax[:], xs[:], -1.0, None, ALU.mult))
                    nc.vector.tensor_tensor(ax[:], ax[:], xs[:], ALU.min).then_inc(soft_in, 1)
                    for t in range(NT):
                        nc.vector.tensor_tensor(sq[:, t % 2], qkv[:, t, 0:2 * GW], qkv[:, t, 0:2 * GW], ALU.mult).then_inc(l2_step, 1)
                        dve.wait_ge(l2_step, t + 1)
                        last = nc.vector.tensor_reduce(nrm[:, t, :], sq[:, t % 2].rearrange("p (h n) -> p h n", h=8), AX.X, ALU.add)
                    link(last)
                    nc.vector.tensor_scalar(nrm[:], nrm[:], EPS, None, ALU.add).then_inc(root_in, 1)
                    dve.wait_ge(soft_exp, 2)
                    nc.vector.tensor_scalar(ax[:], ax[:], 1.0, None, ALU.add).then_inc(ln_in, 1)
                    link(nc.vector.tensor_scalar(ab[:, :, 8:16], ab[:, :, 8:16], 1.0, None, ALU.add))
                    for d in range(2):
                        link(nc.vector.reciprocal(scal[:, :, d, 1, :], ab[:, :, 8 + 4 * d:12 + 4 * d]))
                    link(nc.vector.tensor_scalar(xs[:], xs[:], 0.0, None, ALU.max))
                    dve.wait_ge(soft_ln, 1)
                    dve.wait_ge(al_exp, 1)
                    link(nc.vector.tensor_tensor(xs[:], xs[:], ax[:], ALU.add))
                    for d in range(2):
                        o = nc.vector.scalar_tensor_tensor(out=scal[:, :, d, 0, :], in0=xs[:, :, 4 * d:4 * d + 4], scalar=-1.0,
                                                           in1=al[:, 0:1, 4 * d:4 * d + 4].to_broadcast([P, NT, 4]), op0=ALU.mult, op1=ALU.mult)
                    o.then_inc(g_ready, 1)
                    dve.wait_ge(sums_ready, 1)
                    for d in range(2):
                        gc = g.ps[:, 0, d * 40:d * 40 + 40].rearrange("p (t h) -> p t h", h=4)
                        tot = g.ps[:, 0, 80 + d * 40:120 + d * 40].rearrange("p (t h) -> p t h", h=4)
                        link(nc.vector.tensor_copy(scal[:, :, d, 2, :], gc))
                        nc.vector.tensor_copy(scal[:, :, d, 3, :], gc)
                        link(nc.vector.tensor_copy(scal[:, :, d, 6, :], tot))
                        link(nc.vector.tensor_tensor(scal[:, :, d, 4, :], scal[:, :, d, 6, :], scal[:, :, d, 2, :], ALU.subtract))
                    nc.vector.tensor_copy(al[:, 1, 0:1], al[:, 1, 1:2]).then_inc(decay_ready, 1)
                    dve.wait_ge(decay_ready, 4)
                    link(nc.vector.tensor_tensor(scal[:, :, :, 5, :], scal[:, :, :, 3, :], scal[:, :, :, 1, :], ALU.mult))
                    dve.wait_ge(root_ready, 1)
                    link(nc.vector.reciprocal(nrm[:], nrm[:]))
                    link(nc.vector.tensor_scalar(nrm[:, :, 0:4], nrm[:, :, 0:4], SCALE, None, ALU.mult))
                    for t in range(NT):
                        x = qkv[:, t, 0:2 * GW].rearrange("p (h n) -> p h n", h=8)
                        nc.vector.tensor_tensor(x, x, nrm[:, t, :].unsqueeze(2).to_broadcast([P, 8, C]), ALU.mult)
        gdn_steps(nc, g, st, qkv, scal, o_sum, M, l == 0)
        sqo = st.sb("sqo", [P, 2, GW])
        no = st.sb("no", [P, NT, 4])
        ng = st.sb("ng", [P, C])
        names = "ng_loaded root_in2 root_ready2 fin_step tile_ready out_turned out_put sq_step".split()
        ng_loaded, root_in2, root_ready2, fin_step, tile_ready, out_turned, out_put, sq_step = (st.sem(n) for n in names)
        with nc.Block() as block:
            @block.sync
            def _(sp):
                sp.dma_start(ng[:], g.gdn_norm[l].rearrange("(o n) -> o n", o=1).to_broadcast([P, C])).then_inc(ng_loaded, 16)

            @block.vector
            def _(dve):
                link = Chain(dve, fin_step)
                for t in range(NT):
                    nc.vector.tensor_tensor(sqo[:, t % 2], o_sum[:, t, :], o_sum[:, t, :], ALU.mult).then_inc(sq_step, 1)
                    dve.wait_ge(sq_step, t + 1)
                    last = nc.vector.tensor_reduce(no[:, t, :], sqo[:, t % 2].rearrange("p (h n) -> p h n", h=4), AX.X, ALU.add)
                link(last)
                nc.vector.tensor_scalar(no[:], no[:], 1.0 / C, EPS, ALU.mult, ALU.add).then_inc(root_in2, 1)
                dve.wait_ge(ng_loaded, 16)
                for t in range(NT):
                    x = gate[:, t, :].rearrange("p (h n) -> p h n", h=4)
                    last = nc.vector.tensor_tensor(x, x, ng[:].unsqueeze(1).to_broadcast([P, 4, C]), ALU.mult)
                link(last)
                dve.wait_ge(root_ready2, 1)
                link(nc.vector.reciprocal(no[:], no[:]))
                for t in range(NT):
                    x = o_sum[:, t, :].rearrange("p (h n) -> p h n", h=4)
                    link(nc.vector.tensor_tensor(x, x, no[:, t, :].unsqueeze(2).to_broadcast([P, 4, C]), ALU.mult))
                    nc.vector.tensor_tensor(o_sum[:, t, :], o_sum[:, t, :], gate[:, t, :], ALU.mult).then_inc(tile_ready, 1)

            @block.scalar
            def _(act):
                act.wait_ge(root_in2, 1)
                nc.scalar.activation(no[:], no[:], ACT.Sqrt).then_inc(root_ready2, 1)
                for t in range(NT):
                    act.wait_ge(out_turned, t + 1)
                    nc.scalar.copy(g.yT[:, 6:8, t * P:(t + 1) * P], g.ps[:, t % 2, 0:2 * P].rearrange("p (f n) -> p f n", f=2)).then_inc(out_put, 1)

            @block.tensor
            def _(pe):
                for t in range(NT):
                    pe.wait_ge(tile_ready, t + 1)
                    wait(pe, out_put, t - 1)
                    for i in range(2):
                        mm = nc.tensor.transpose(g.ps[:, t % 2, i * P:(i + 1) * P], o_sum[:, t, i * P:(i + 1) * P], g.ident[:])
                    mm.then_inc(out_turned, 1)


def gdn_steps(nc, g, st, qkv, scal, o_sum, M, fill):
    C, FW = 64, 256
    LEVELS = 5
    RS = [slice(0, C), slice(C, P)]
    D2 = range(2)

    def sb(name, shape=(2, 4, C)):
        return st.sb(name, [P] + list(shape))

    x3 = st.sb("x3", [P, 2, 3 * FW])
    sc = st.sb("sc", [P, 2, 7, 4])
    glz = st.sb("glz", [P, 2, 4])
    DG, E, kT, qT, L, At, LT, AtT, T, TT, X, tmp, vb, kbe, kd, qd, U, wT, qdT = (
        sb(n) for n in "DG E kT qT L At LT AtT T TT X tmp vb kbe kd qd U wT qdT".split())
    S = st.sb("S", [P, 4, C])
    Sg = st.sb("Sg", [P, 4, C])
    un = st.sb("un", [P, 4, C])
    names = ("gathered scaled dg_ready gj_ready e_in e_ready kq_turned kq_ready gram_ready "
             "l_ready at_ready lt_turned t_next x_prod x_ready tt_prod t_ready").split()
    (gathered, scaled, dg_ready, gj_ready, e_in, e_ready, kq_turned, kq_ready, gram_ready,
     l_ready, at_ready, lt_turned, t_next, x_prod, x_ready, tt_prod, t_ready) = ([st.sem(f"{n}{d}") for d in D2] for n in names)
    names = ("att_turned att_ready qd_turned qdt_ready u_prod u_ready w_prod w_ready kd_ready glz_ready s_reset "
             "ws_prod un_ready s_ready o_prod o_taken waits_met vec_step").split()
    (att_turned, att_ready, qd_turned, qdt_ready, u_prod, u_ready, w_prod, w_ready, kd_ready, glz_ready, s_reset,
     ws_prod, un_ready, s_ready, o_prod, o_taken, waits_met, vec_step) = (st.sem(n) for n in names)
    ps = g.ps
    STEPS = NT

    def tiles_of(s):
        return (NTL + s, NTL + 1 - s) if s < NTC else (s - NTC, NT - 1 - s)

    def all_steps(eng, prepare, body):
        prepare(0, tiles_of(0))
        body(0, 1, tiles_of(1))
        body(1, 2, tiles_of(2))
        with eng.Fori(0, NTL - 1) as i:
            body(i + 2, i + 3, (i + 1, NTL - 2 - i))
        body(STEPS - 1, None, None)

    def slot(b, half):
        return ps[:, b, half * FW:(half + 1) * FW].rearrange("p (h n) -> p h n", h=4)

    def bank(b):
        return ps[:, b, :].rearrange("p (d h n) -> p d h n", d=2, h=4)

    GJ, KT, QT, GRAM, QK, LTP = (0, 0), (1, 0), (1, 1), (0, 0), (0, 1), (1, 0)
    XP, TXT, TX = (0, 0), (1, 0), (1, 1)
    ATT, QD, UP, WP = 4, 5, 6, 7
    WS, SP, OP = 4, 5, 6

    def at(d, place):
        return slot(2 * d + place[0], place[1])

    def per_head(a, d, v):
        return a[:, d, v, :].unsqueeze(2).to_broadcast([P, 4, C])

    def mask(m):
        return m.unsqueeze(1).to_broadcast([P, 4, C])

    def eye(d, h, c):
        return M["gd_eye"][RS[c], :]

    zero = st.sb("zero", [P, D])
    zero_ready, filled = st.sem("zero_ready"), st.sem("filled")
    with nc.Block() as block:
        @block.sync
        def _(sp):
            if fill:
                sp.wait_ge(zero_ready, 1)
                for b in range(NT * TOP_K, MAX_BLOCKS):
                    sp.dma_start(g.y_dram[b], zero[:]).then_inc(filled, 16)
                sp.wait_ge(filled, 16 * (MAX_BLOCKS - NT * TOP_K))

        @block.tensor
        def _(pe):
            def wait_step(sem, value):
                pe.wait_ge(sem, value)
                pe.sem_inc(waits_met, 1)

            def unit(d, place, lhs, rhs):
                for h in range(4):
                    for c in range(2):
                        col = place[1] * FW + h * C
                        mm = nc.tensor.matmul(ps[RS[c], 2 * d + place[0], col:col + C], lhs(d, h, c), rhs(d, h, c), start=True, stop=True)
                return mm

            def by_z(d, b, lhs, rhs):
                for h in range(4):
                    for c in range(2):
                        col = (d ^ c) * FW + h * C
                        mm = nc.tensor.matmul(ps[RS[c], b, col:col + C], lhs(d, h, c), rhs(d, h, c), start=True, stop=True)
                return mm

            def of(a):
                return lambda d, h, c: a[RS[c], d, h, :]

            def gj_kt_qt(s):
                for d in D2:
                    pe.wait_ge(dg_ready[d], s + 1)
                    nc.tensor.matmul(ps[:, 2 * d, 0:FW], M["gd_negblk"][:], DG[:, d].rearrange("p h n -> p (h n)"),
                                     start=True, stop=True).then_inc(gj_ready[d], 1)
                for d in D2:
                    wait_step(gathered[d], 2 * s + 2)
                    unit(d, KT, lambda d, h, c: x3[RS[c], d, FW + h * C:FW + (h + 1) * C], eye)
                    unit(d, QT, lambda d, h, c: x3[RS[c], d, h * C:(h + 1) * C], eye).then_inc(kq_turned[d], 1)

            def gram_qk(s, d):
                wait_step(e_in[d], s + 1)
                wait_step(kq_ready[d], s + 1)
                unit(d, GRAM, of(kT), of(kT))
                unit(d, QK, of(qT), of(kT)).then_inc(gram_ready[d], 1)

            def turn_l(s):
                for d in D2:
                    wait_step(l_ready[d], s + 1)
                    unit(d, LTP, of(L), eye).then_inc(lt_turned[d], 1)

            def levels(s):
                if not (isinstance(s, int) and s == 0):
                    wait_step(o_taken, s)
                for d in D2:
                    wait_step(at_ready[d], s + 1)
                    mm = by_z(d, ATT, of(At), eye)
                mm.then_inc(att_turned, 1)
                for lv in range(LEVELS):
                    for d in D2:
                        wait_step(t_next[d], s * LEVELS + lv + 1)
                        unit(d, XP, of(LT), of(T)).then_inc(x_prod[d], 1)
                    if lv == 0:
                        for d in D2:
                            wait_step(scaled[d], s + 1)
                            mm = by_z(d, QD, of(qd), eye)
                        mm.then_inc(qd_turned, 1)
                    for d in D2:
                        wait_step(x_ready[d], s * LEVELS + lv + 1)
                        mm = unit(d, TXT, of(X), of(TT))
                        if lv < LEVELS - 1:
                            mm = unit(d, TX, of(TT), of(X))
                        mm.then_inc(tt_prod[d], 1)
                for d in D2:
                    wait_step(t_ready[d], s + 1)
                    mw = by_z(d, WP, of(kbe), of(TT))
                    if d == 1:
                        mw.then_inc(w_prod, 1)
                    mu = by_z(d, UP, of(TT), of(vb))
                mu.then_inc(u_prod, 1)

            def state_product(s, z):
                if z == 0:
                    wait_step(w_ready, s + 1)
                    wait_step(qdt_ready, s + 1)
                    wait_step(att_ready, s + 1)
                wait_step(s_ready, 2 * s + z + 1)
                for h in range(4):
                    for c in range(2):
                        mm = nc.tensor.matmul(ps[RS[c], WS, h * C:(h + 1) * C], wT[RS[c], z, h, :], S[RS[c], h, :], start=True, stop=True)
                mm.then_inc(ws_prod, 1)

            def state_and_output(s, z):
                if z == 0:
                    wait_step(kd_ready, s + 1)
                wait_step(un_ready, 2 * s + z + 1)
                for h in range(4):
                    for c in range(2):
                        nc.tensor.matmul(ps[RS[1 - c], SP, h * C:(h + 1) * C], kd[RS[c], z ^ c, h, :], un[RS[c], h, :], start=True, stop=True)
                for h in range(4):
                    for c in range(2):
                        col = z * FW + h * C
                        nc.tensor.matmul(ps[RS[c], OP, col:col + C], qdT[RS[c], z, h, :], S[RS[c], h, :], start=True, stop=False)
                        mm = nc.tensor.matmul(ps[RS[c], OP, col:col + C], AtT[RS[c], z, h, :], un[RS[c], h, :], start=False, stop=True)
                mm.then_inc(o_prod, 1)

            def prepare(s, tiles):
                gj_kt_qt(s)
                for d in D2:
                    gram_qk(s, d)
                turn_l(s)

            def body(s, nxt, tiles):
                more = nxt is not None
                levels(s)
                if more:
                    gj_kt_qt(nxt)
                wait_step(u_ready, s + 1)
                state_product(s, 0)
                if more:
                    gram_qk(nxt, 0)
                state_and_output(s, 0)
                state_product(s, 1)
                if more:
                    gram_qk(nxt, 1)
                state_and_output(s, 1)
                if more:
                    turn_l(nxt)

            all_steps(pe, prepare, body)

        @block.gpsimd
        def _(pool):
            def prepare(s, tiles):
                wait(pool, u_prod, s)
                for d in D2:
                    pool.wait_ge(gathered[d], 2 * s + 2)
                    q, k, v = (x3[:, d, i * FW:(i + 1) * FW].rearrange("p (h n) -> p h n", h=4) for i in range(3))
                    nc.gpsimd.tensor_tensor(qd[:, d], q, per_head(sc, d, 3), ALU.mult)
                    nc.gpsimd.tensor_tensor(vb[:, d], v, per_head(sc, d, 1), ALU.mult)
                    nc.gpsimd.tensor_tensor(kbe[:, d], k, per_head(sc, d, 5), ALU.mult).then_inc(scaled[d], 1)

            def body(s, nxt, tiles):
                wait(pool, o_taken, s)
                for d in D2:
                    k = x3[:, d, FW:2 * FW].rearrange("p (h n) -> p h n", h=4)
                    kk = nc.gpsimd.tensor_tensor(kd[:, d], k, per_head(sc, d, 4), ALU.mult)
                kk.then_inc(kd_ready, 1)
                if nxt is not None:
                    prepare(nxt, tiles)

            pool.memset(S[:], 0.0).then_inc(s_ready, 1)
            pool.memset(zero[:], 0.0).then_inc(zero_ready, 1)
            all_steps(pool, prepare, body)

        @block.scalar
        def _(act):
            def gather(s, tiles):
                if not (isinstance(s, int) and s == 0):
                    act.wait_ge(kd_ready, s)
                    act.wait_ge(glz_ready, s)
                for d, t in enumerate(tiles):
                    nc.scalar.copy(x3[:, d, :], qkv[:, t, :] if isinstance(t, int) else qkv[:, bass.ds(t, 1), :].rearrange("p o n -> p (o n)")).then_inc(gathered[d], 1)
                    nc.scalar.copy(sc[:, d], scal[:, t, d] if isinstance(t, int) else scal[:, bass.ds(t, 1), d].rearrange("p o v h -> p (o v) h")).then_inc(gathered[d], 1)

            def take(s):
                for d in D2:
                    act.wait_ge(kq_turned[d], s + 1)
                    nc.scalar.copy(kT[:, d], at(d, KT))
                    nc.scalar.copy(qT[:, d], at(d, QT)).then_inc(kq_ready[d], 1)
                for d in D2:
                    act.wait_ge(e_in[d], s + 1)
                    nc.scalar.activation(E[:, d], E[:, d], ACT.Exp).then_inc(e_ready[d], 1)

            def prepare(s, tiles):
                gather(s, tiles)
                take(s)

            def body(s, nxt, tiles):
                act.wait_ge(att_turned, s + 1)
                nc.scalar.copy(AtT[:], bank(ATT)).then_inc(att_ready, 1)
                if nxt is not None:
                    gather(nxt, tiles)
                act.wait_ge(qd_turned, s + 1)
                nc.scalar.copy(qdT[:], bank(QD)).then_inc(qdt_ready, 1)
                act.wait_ge(w_prod, s + 1)
                nc.scalar.copy(wT[:], bank(WP)).then_inc(w_ready, 1)
                act.wait_ge(u_prod, s + 1)
                nc.scalar.copy(U[:], bank(UP)).then_inc(u_ready, 1)
                if nxt is not None:
                    take(nxt)

            all_steps(act, prepare, body)

        @block.vector
        def _(dve):
            V = nc.vector

            def prepare_steps(s, link):
                def decays():
                    for d in D2:
                        dve.wait_ge(gathered[d], 2 * s + 2)
                        V.tensor_tensor(DG[:, d], mask(M["gd_tri"][:, d]), per_head(sc, d, 0), ALU.mult).then_inc(dg_ready[d], 1)

                def exponents():
                    for d in D2:
                        dve.wait_ge(gj_ready[d], s + 1)
                        o = V.tensor_tensor(E[:, d], at(d, GJ), per_head(sc, d, 2), ALU.add)
                    link(o)
                    for d in D2:
                        V.tensor_tensor(E[:, d], E[:, d], mask(M["gd_allow"][:, d]), ALU.min).then_inc(e_in[d], 1)

                def weights():
                    for d in D2:
                        dve.wait_ge(e_ready[d], s + 1)
                        o = V.tensor_tensor(tmp[:, d], E[:, d], per_head(sc, d, 1), ALU.mult)
                    link(o)
                    for d in D2:
                        o = V.tensor_tensor(tmp[:, d], tmp[:, d], mask(M["gd_strict"][:, d]), ALU.mult)
                    link(o)

                def lower(d):
                    dve.wait_ge(gram_ready[d], s + 1)
                    V.tensor_tensor(L[:, d], tmp[:, d], at(d, GRAM), ALU.mult).then_inc(l_ready[d], 1)
                    V.tensor_tensor(At[:, d], E[:, d], at(d, QK), ALU.mult).then_inc(at_ready[d], 1)

                def inverses():
                    wait(dve, u_prod, s)
                    for d in D2:
                        dve.wait_ge(l_ready[d], s + 1)
                        o = V.tensor_tensor(T[:, d], L[:, d], mask(M["gd_lvl"][:, 0, d]), ALU.mult)
                    link(o)
                    for d in D2:
                        dve.wait_ge(lt_turned[d], s + 1)
                        o = V.tensor_copy(LT[:, d], at(d, LTP))
                    link(o)
                    for d in D2:
                        V.tensor_tensor(T[:, d], mask(M["gd_eye"][:]), T[:, d], ALU.subtract)
                        o = V.tensor_tensor(TT[:, d], LT[:, d], mask(M["gd_lvl"][:, 1, d]), ALU.mult)
                    link(o)
                    for d in D2:
                        V.tensor_tensor(TT[:, d], mask(M["gd_eye"][:]), TT[:, d], ALU.subtract).then_inc(t_next[d], 1)

                return decays, exponents, weights, lower, inverses

            def levels(s):
                for lv in range(LEVELS):
                    for d in D2:
                        dve.wait_ge(x_prod[d], s * LEVELS + lv + 1)
                        V.tensor_tensor(X[:, d], at(d, XP), mask(M["gd_lvl"][:, lv + 2, d]), ALU.mult).then_inc(x_ready[d], 1)
                    if lv == 0:
                        wait(dve, o_taken, s)
                        for c in range(2):
                            for d in range(2):
                                o = V.tensor_copy(glz[RS[c], c ^ d, :], sc[RS[c], d, 6, :])
                        o.then_inc(glz_ready, 1)
                    for d in D2:
                        dve.wait_ge(tt_prod[d], s * LEVELS + lv + 1)
                        dve.wait_ge(t_next[d], s * LEVELS + lv + 1)
                        if lv == LEVELS - 1:
                            V.tensor_tensor(TT[:, d], TT[:, d], at(d, TXT), ALU.subtract).then_inc(t_ready[d], 1)
                            continue
                        V.tensor_tensor(TT[:, d], TT[:, d], at(d, TXT), ALU.subtract)
                        V.tensor_tensor(T[:, d], T[:, d], at(d, TX), ALU.subtract).then_inc(t_next[d], 1)

            def decay_state(s, z):
                dve.wait_ge(s_ready, 2 * s + z + 1)
                if z == 0:
                    dve.wait_ge(glz_ready, s + 1)
                for c in range(2):
                    V.tensor_tensor(Sg[RS[1 - c], :, :], S[RS[c], :, :], glz[RS[c], z, :].unsqueeze(2).to_broadcast([C, 4, C]), ALU.mult)

            def correct(s, z):
                dve.wait_ge(ws_prod, 2 * s + z + 1)
                if z == 0:
                    dve.wait_ge(u_ready, s + 1)
                V.tensor_tensor(un[:], U[:, z], ps[:, WS, 0:FW].rearrange("p (h n) -> p h n", h=4), ALU.subtract).then_inc(un_ready, 1)

            def next_state(s, z):
                dve.wait_ge(o_prod, 2 * s + z + 1)
                dve.wait_ge(un_ready, 2 * s + z + 1)
                V.tensor_tensor(S[:], Sg[:], ps[:, SP, 0:FW].rearrange("p (h n) -> p h n", h=4), ALU.add).then_inc(s_ready, 1)

            def add_output(s, tiles):
                for c in range(2):
                    for d, t in enumerate(tiles):
                        z = c ^ d
                        o = o_sum[RS[c], t, :] if isinstance(t, int) else o_sum[RS[c], bass.ds(t, 1), :].rearrange("p o n -> p (o n)")
                        last = V.tensor_tensor(o, o, ps[RS[c], OP, z * FW:(z + 1) * FW], ALU.add)
                last.then_inc(o_taken, 1)

            PER = 6

            def linker(s):
                n = [0]

                def link(ins):
                    n[0] += 1
                    ins.then_inc(vec_step, 1)
                    dve.wait_ge(vec_step, s * PER + n[0])
                return link

            def prepare(s, tiles):
                decays, exponents, weights, lower, inverses = prepare_steps(s, linker(s))
                decays()
                exponents()
                weights()
                for d in D2:
                    lower(d)
                inverses()

            def body(s, nxt, tiles):
                levels(s)
                own = tiles_of(s) if isinstance(s, int) else (tiles[0] - 1, tiles[1] + 1)
                if nxt is None:
                    for z in range(2):
                        decay_state(s, z)
                        correct(s, z)
                        next_state(s, z)
                    add_output(s, own)
                    return
                decays, exponents, weights, lower, inverses = prepare_steps(nxt, linker(nxt))
                decays()
                decay_state(s, 0)
                exponents()
                correct(s, 0)
                weights()
                lower(0)
                next_state(s, 0)
                decay_state(s, 1)
                correct(s, 1)
                lower(1)
                next_state(s, 1)
                add_output(s, own)
                inverses()

            all_steps(dve, prepare, body)


def stage_mix_out(nc, g, l, tiles, latent, context):
    with Stage(nc, f"mix{l}") as st:
        w = st.sb("w", [P, KD, D])
        gb = st.sb("gb", [P, 2, D])
        x = st.sb("x", [P, 3, D])
        tmp = st.sb("tmp", [P, 2, D])
        xn = st.sb("xn", [P, 2, D])
        rows = st.sb("rows", [P, 2, 2, D])
        nrow = st.sb("nrow", [P, D])
        h = st.sb("h", [P, 2, D])
        ss = st.sb("ss", [P, tiles])
        rs = st.sb("rs", [P, tiles])
        rt = st.sb("rt", [P, tiles])
        names = ("w_loaded gb_loaded prod_ready gated summed rows_loaded row_step h_ready squares_summed mean_ready root_ready "
                 "rstd_ready scaled turned taken_lo taken_hi step").split()
        (w_loaded, gb_loaded, prod_ready, gated, summed, rows_loaded, row_step, h_ready, squares_summed, mean_ready, root_ready,
         rstd_ready, scaled, turned, taken_lo, taken_hi, step) = (st.sem(n) for n in names)
        x_loaded = [st.sem(f"x_loaded{i}") for i in range(3)]
        x_stored = [st.sem(f"x_stored{i}") for i in range(3)]
        h_stored = [st.sem(f"h_stored{i}") for i in range(2)]
        sh0 = 3 * KD
        with nc.Block() as block:
            @block.sync
            def _(sp):
                wv = g.w_out[l].rearrange("(k p) n -> p k n", p=P)
                for half in range(2):
                    cols = slice(half * BANK, (half + 1) * BANK)
                    sp.dma_start(w[:, :, cols], wv[:, :, cols]).then_inc(w_loaded, 16)
                for s in range(2):
                    sp.dma_start(gb[:, s], g.mod_rows[s:s + 1, 2 * D:3 * D].to_broadcast([P, D])).then_inc(gb_loaded, 16)
                    for i, m in ((0, 4), (1, 3)):
                        sp.dma_start(rows[:, i, s], g.mod_rows[s:s + 1, m * D:(m + 1) * D].to_broadcast([P, D])).then_inc(rows_loaded, 16)
                sp.dma_start(nrow[:], g.norm2[l].rearrange("(o n) -> o n", o=1).to_broadcast([P, D])).then_inc(rows_loaded, 16)
                for t in range(tiles + 2):
                    if t < tiles:
                        wait(sp, x_stored[t % 3], 16 * (t // 3))
                        wait(sp, scaled, t - 2)
                        sp.dma_start(x[:, t % 3], token_tile(latent, context, t)).then_inc(x_loaded[t % 3], 16)
                    if t >= 2:
                        u = t - 2
                        sp.wait_ge(h_ready, u + 1)
                        sp.dma_start(g.h_dram[u * P:(u + 1) * P, :], h[:, u % 2]).then_inc(h_stored[u % 2], 16)
                for i in range(2):
                    sp.wait_ge(h_stored[i], 16 * len(range(i, tiles, 2)))

            @block.gpsimd
            def _(pool):
                link = Chain(pool, row_step)
                pool.wait_ge(rows_loaded, 80)
                nr = nrow[:].unsqueeze(1).to_broadcast([P, 2, D])
                link(nc.gpsimd.tensor_tensor(rows[:, 0], rows[:, 0], nr, ALU.mult))
                link(nc.gpsimd.tensor_tensor(rows[:, 0], rows[:, 0], nr, ALU.add))
                for t in range(tiles):
                    pool.wait_ge(scaled, t + 1)
                    wait(pool, h_stored[t % 2], 16 * (t // 2))
                    link(nc.gpsimd.tensor_tensor(h[:, t % 2], xn[:, t % 2], rows[:, 0, t // NTL], ALU.mult))
                    nc.gpsimd.tensor_tensor(h[:, t % 2], h[:, t % 2], rows[:, 1, t // NTL], ALU.add).then_inc(h_ready, 1)

            @block.tensor
            def _(pe):
                def turn(t):
                    pe.wait_ge(scaled, t + 1)
                    wait(pe, taken_lo, t - 1)
                    wait(pe, taken_hi, t - 1)
                    for k in range(KD):
                        mm = nc.tensor.transpose(g.ps[:, 4 + 2 * (t % 2) + k // 4, (k % 4) * P:(k % 4 + 1) * P],
                                                 xn[:, t % 2, k * P:(k + 1) * P], g.ident[:])
                    mm.then_inc(turned, 1)

                for t in range(tiles):
                    wait(pe, gated, t - 1)
                    for half in range(2):
                        if t == 0:
                            pe.wait_ge(w_loaded, 32)
                        for k in range(KD):
                            mm = nc.tensor.matmul(g.ps[:, 2 * (t % 2) + half, :], g.yT[:, k, t * P:(t + 1) * P],
                                                  w[:, k, half * BANK:(half + 1) * BANK], start=k == 0, stop=k == KD - 1)
                    mm.then_inc(prod_ready, 1)
                    if t >= 1:
                        turn(t - 1)
                turn(tiles - 1)

            @block.vector
            def _(dve):
                def take(t):
                    s = t // NTL
                    dst = g.hT[:, 0:4, t * P:(t + 1) * P]
                    dve.wait_ge(turned, t + 1)
                    nc.vector.tensor_tensor(dst, g.ps[:, 4 + 2 * (t % 2), :].rearrange("p (k n) -> p k n", k=4),
                                            g.gain[:, 1, 0:4, s:s + 1].to_broadcast([P, 4, P]), ALU.mult).then_inc(step, 1)
                    dve.wait_ge(step, t + 1)
                    nc.vector.tensor_tensor(dst, dst, g.modT[:, sh0:sh0 + 4, s:s + 1].to_broadcast([P, 4, P]),
                                            ALU.add).then_inc(taken_lo, 1)

                dve.wait_ge(gb_loaded, 32)
                for t in range(tiles):
                    dve.wait_ge(prod_ready, t + 1)
                    wait(dve, squares_summed, t - 1)
                    flat = g.ps[:, 2 * (t % 2):2 * (t % 2) + 2, :].rearrange("p b n -> p (b n)")
                    nc.vector.tensor_tensor(tmp[:, t % 2], flat, gb[:, t // NTL], ALU.mult).then_inc(gated, 1)
                    dve.wait_ge(gated, t + 1)
                    dve.wait_ge(x_loaded[t % 3], 16 * (t // 3 + 1))
                    nc.vector.tensor_tensor(x[:, t % 3], x[:, t % 3], tmp[:, t % 2], ALU.add).then_inc(summed, 1)
                    dve.wait_ge(squares_summed, t + 1)
                    nc.vector.tensor_scalar(ss[:, t:t + 1], ss[:, t:t + 1], 1.0 / D, EPS, ALU.mult, ALU.add).then_inc(mean_ready, 1)
                    dve.wait_ge(root_ready, t + 1)
                    nc.vector.reciprocal(rt[:, t:t + 1], rs[:, t:t + 1]).then_inc(rstd_ready, 1)
                    dve.wait_ge(rstd_ready, t + 1)
                    wait(dve, turned, t - 1)
                    wait(dve, h_ready, t - 1)
                    nc.vector.tensor_scalar(xn[:, t % 2], x[:, t % 3], rt[:, t:t + 1], None, ALU.mult).then_inc(scaled, 1)
                    if t >= 1:
                        take(t - 1)
                take(tiles - 1)

            @block.scalar
            def _(act):
                def take(t):
                    s = t // NTL
                    act.wait_ge(turned, t + 1)
                    for k in range(KD // 2, KD):
                        o = nc.scalar.activation(g.hT[:, k, t * P:(t + 1) * P],
                                                 g.ps[:, 4 + 2 * (t % 2) + 1, (k % 4) * P:(k % 4 + 1) * P], ACT.Identity,
                                                 scale=g.gain[:, 1, k, s:s + 1], bias=g.modT[:, sh0 + k, s:s + 1])
                    o.then_inc(taken_hi, 1)

                for t in range(tiles):
                    act.wait_ge(summed, t + 1)
                    act.dma_start(g.x_dram[t * P:(t + 1) * P, :], x[:, t % 3]).then_inc(x_stored[t % 3], 16)
                    nc.scalar.activation(tmp[:, t % 2], x[:, t % 3], ACT.Square, accum_out=ss[:, t:t + 1]).then_inc(squares_summed, 1)
                    act.wait_ge(mean_ready, t + 1)
                    nc.scalar.activation(rs[:, t:t + 1], ss[:, t:t + 1], ACT.Sqrt).then_inc(root_ready, 1)
                    if t >= 1:
                        take(t - 1)
                take(tiles - 1)
                for i in range(3):
                    act.wait_ge(x_stored[i], 16 * len(range(i, tiles, 3)))


def stage_route(nc, g, l, tiles):
    NBK = blocks_of(tiles)
    chunks = CHUNKS if tiles == NT else CHUNKS[:2]
    GROUPS = 2 * len(chunks)
    with Stage(nc, f"route{l}") as st:
        wg = st.sb("wg", [P, KD, DE])
        wu = st.sb("wu", [P, KD, DE])
        wd = st.sb("wd", [P, 2, D])
        sg = st.sb("sg", [P, 2, BANK])
        hid = st.sb("hid", [P, 2, TOK])
        w_loaded, up_ready, silu_ready, hid_ready, down_ready, acc_taken = (
            st.sem(n) for n in "w_loaded up_ready silu_ready hid_ready down_ready acc_taken".split())
        w = st.sb("w", [P, KD, NE])
        bias = st.sb("bias", [P, NE])
        iota = st.sb("iota", [P, MAX_BLOCKS])
        before = st.sb("before", [P, 2, P])
        tok = st.sb("tok", [P, NT], U32)
        zero = st.sb("zero", [P, NBK], U32)
        sc = st.sb("sc", [P, tiles, NE])
        sel = st.sb("sel", [P, tiles, NE])
        eq = st.sb("eq", [P, TOP_K, tiles, NE])
        tmp = st.sb("tmp", [P, tiles, NE])
        top = st.sb("top", [P, tiles, 8])
        idx = st.sb("idx", [P, tiles, 8], U32)
        idf = st.sb("idf", [P, tiles, 8])
        tot = st.sb("tot", [P, tiles])
        slotf = st.sb("slotf", [P, tiles, TOP_K])
        nb = st.sb("nb", [P, 3, NE])
        cmp = st.sb("cmp", [1, NBK, NE])
        be = st.sb("be", [1, 3, NBK])
        ring = st.sb("ring", [1, NE])
        idrow = st.sb("idrow", [NBK, P], U32)
        idrf = st.sb("idrf", [NBK, P])
        names = "small_loaded logits_ready exp_ready step mask_ready sums_ready slots_ready ids_cleared zeroed scattered ids_loaded idf_ready ids_turned".split()
        (small_loaded, logits_ready, exp_ready, step, mask_ready, sums_ready, slots_ready, ids_cleared, zeroed, scattered, ids_loaded,
         idf_ready, ids_turned) = (st.sem(n) for n in names)
        ids_dram = g.ids_dram[0:NBK * P, :]
        with nc.Block() as block:
            @block.sync
            def _(sp):
                with nc.allow_non_contiguous_dma("router, once a layer"):
                    sp.dma_start(w[:], g.moe_router[l].rearrange("(k p) n -> p k n", p=P)).then_inc(small_loaded, 16)
                sp.dma_start(bias[:], g.moe_bias[l].rearrange("(o n) -> o n", o=1).to_broadcast([P, NE])).then_inc(small_loaded, 16)
                sp.dma_start(iota[:], g.t_iota.to_broadcast([P, MAX_BLOCKS])).then_inc(small_loaded, 16)
                sp.dma_start(before[:], g.t_before).then_inc(small_loaded, 16)
                sp.dma_start(tok[:], g.t_tok).then_inc(small_loaded, 16)
                for dst, src in ((wg, g.sh_gate), (wu, g.sh_up), (wd, g.sh_down)):
                    sp.dma_start(dst[:], src[l].rearrange("(k p) n -> p k n", p=P)).then_inc(w_loaded, 16)
                sp.wait_ge(zeroed, 1)
                sp.dma_start(ids_dram.rearrange("(p b) o -> p (b o)", p=P), zero[:]).then_inc(ids_cleared, 16)
                sp.wait_ge(scattered, 16 * tiles * TOP_K)
                sp.dma_start(idrow[:], ids_dram.rearrange("(b p) o -> b (p o)", p=P)).then_inc(ids_loaded, 16)

            @block.gpsimd
            def _(pool):
                pool.memset(zero[:], 0).then_inc(zeroed, 1)
                pool.wait_ge(small_loaded, 80)
                pool.wait_ge(ids_cleared, 16)
                pool.wait_ge(slots_ready, 1)
                for t in range(tiles):
                    for j in range(TOP_K):
                        n = t * TOP_K + j
                        pool.indirect_dma_start(ids_dram, bass.IndirectOffsetOnAxis(g.slots[:, n:n + 1], 0),
                                                tok[:, t:t + 1], None).then_inc(scattered, 16)

            @block.tensor
            def _(pe):
                pe.wait_ge(small_loaded, 80)
                for t in range(tiles):
                    for k in range(KD):
                        mm = nc.tensor.matmul(g.ps[:, 0, t * NE:(t + 1) * NE], g.hT[:, k, t * P:(t + 1) * P], w[:, k, :],
                                              start=k == 0, stop=k == KD - 1)
                mm.then_inc(logits_ready, 1)

                def up(m):
                    c0, n = chunks[m // 2]
                    f = m % 2
                    wait(pe, hid_ready, m - 1)
                    for i, ws in enumerate((wg, wu)):
                        for k in range(KD):
                            mm = nc.tensor.matmul(g.ps[:, 4 + 2 * (m % 2) + i, 0:n], ws[:, k, f * P:(f + 1) * P],
                                                  g.hT[:, k, c0:c0 + n], start=k == 0, stop=k == KD - 1)
                    mm.then_inc(up_ready, 1)

                pe.wait_ge(w_loaded, 48)
                for m in range(2):
                    up(m)
                pe.wait_ge(mask_ready, 1)
                for t in range(tiles):
                    for u in range(t):
                        nc.tensor.matmul(g.ps[:, 1, t * NE:(t + 1) * NE], before[:, 1, :], sel[:, u, :], start=u == 0, stop=False)
                    nc.tensor.matmul(g.ps[:, 1, t * NE:(t + 1) * NE], before[:, 0, :], sel[:, t, :], start=t == 0, stop=True)
                for u in range(tiles):
                    mm = nc.tensor.matmul(g.ps[:, 2, 0:NE], before[:, 1, :], sel[:, u, :], start=u == 0, stop=u == tiles - 1)
                mm.then_inc(sums_ready, 1)
                for m in range(2, GROUPS):
                    up(m)
                pe.wait_ge(hid_ready, GROUPS)
                for t in range(tiles):
                    wait(pe, acc_taken, t - 1)
                    for half in range(2):
                        for f in range(2):
                            mm = nc.tensor.matmul(g.ps[:, 4 + 2 * (t % 2) + half, :], hid[:, f, t * P:(t + 1) * P],
                                                  wd[:, f, half * BANK:(half + 1) * BANK], start=f == 0, stop=f == 1)
                    mm.then_inc(down_ready, 1)
                pe.wait_ge(idf_ready, 1)
                nc.tensor.transpose(g.ps[:, 3, 0:NBK], idrf[:], g.ident[0:NBK, 0:NBK]).then_inc(ids_turned, 1)

            @block.scalar
            def _(act):
                act.wait_ge(logits_ready, 1)
                nc.scalar.activation(sc[:], g.ps[:, 0, 0:tiles * NE].rearrange("p (t n) -> p t n", n=NE), ACT.Exp, scale=-1.0).then_inc(exp_ready, 1)
                for m in range(GROUPS):
                    n = chunks[m // 2][1]
                    act.wait_ge(up_ready, m + 1)
                    wait(act, hid_ready, m - 1)
                    nc.scalar.activation(sg[:, m % 2, 0:n], g.ps[:, 4 + 2 * (m % 2), 0:n], ACT.Silu).then_inc(silu_ready, 1)
                for t in range(tiles):
                    act.wait_ge(down_ready, t + 1)
                    nc.scalar.copy(g.acc[:, t, :], g.ps[:, 4 + 2 * (t % 2):6 + 2 * (t % 2), :].rearrange("p b n -> p (b n)")).then_inc(acc_taken, 1)

            @block.vector
            def _(dve):
                V = nc.vector
                link = Chain(dve, step)
                wide = [P, tiles, NE]

                def hidden(m):
                    c0, n = chunks[m // 2]
                    dve.wait_ge(silu_ready, m + 1)
                    V.tensor_tensor(hid[:, m % 2, c0:c0 + n], sg[:, m % 2, 0:n], g.ps[:, 5 + 2 * (m % 2), 0:n], ALU.mult).then_inc(hid_ready, 1)

                dve.wait_ge(exp_ready, 1)
                dve.wait_ge(small_loaded, 80)
                link(V.tensor_scalar(sc[:], sc[:], 1.0, None, ALU.add))
                link(V.reciprocal(sc[:], sc[:]))
                link(V.tensor_tensor(sel[:], sc[:], bias[:].unsqueeze(1).to_broadcast(wide), ALU.add))
                for t in range(tiles):
                    last = V.max(top[:, t, :], sel[:, t, :])
                link(last)
                for t in range(tiles):
                    last = V.max_index(idx[:, t, :], top[:, t, :], sel[:, t, :])
                link(last)
                link(V.tensor_copy(idf[:], idx[:]))
                for j in range(TOP_K):
                    last = V.tensor_tensor(eq[:, j], iota[:, 0:NE].unsqueeze(1).to_broadcast(wide), idf[:, :, j:j + 1].to_broadcast(wide), ALU.is_equal)
                link(last)
                link(V.tensor_tensor(sel[:], eq[:, 0], eq[:, 1], ALU.add))
                link(V.tensor_tensor(sel[:], sel[:], eq[:, 2], ALU.add))
                V.tensor_tensor(sel[:], sel[:], eq[:, 3], ALU.add).then_inc(mask_ready, 1)
                hidden(0)
                dve.wait_ge(mask_ready, 1)
                link(V.tensor_tensor(tmp[:], sel[:], sc[:], ALU.mult))
                link(V.tensor_reduce(tot[:], tmp[:], AX.X, ALU.add))
                link(V.reciprocal(tot[:], tot[:]))
                link(V.tensor_scalar(tot[:], tot[:], ROUTED_SCALE, None, ALU.mult))
                link(V.tensor_tensor(sc[:], tmp[:], tot[:].unsqueeze(2).to_broadcast(wide), ALU.mult))
                for j in range(TOP_K):
                    link(V.tensor_tensor(tmp[:], eq[:, j], sc[:], ALU.mult))
                    link(V.tensor_reduce(g.slot_w[:, 0:tiles, j], tmp[:], AX.X, ALU.add))
                hidden(1)
                dve.wait_ge(sums_ready, 1)
                link(V.tensor_scalar(nb[:, 0], g.ps[:, 2, 0:NE], 1.0 / P, (P / 2 - 0.5) / P, ALU.mult, ALU.add))
                link(V.tensor_scalar(nb[:, 0], nb[:, 0], MAGIC, None, ALU.add))
                link(V.tensor_scalar(nb[:, 0], nb[:, 0], -MAGIC, None, ALU.add))
                link(V.tensor_tensor_scan(nb[:, 1], nb[:, 0], nb[:, 0], 0.0, ALU.add, ALU.bypass))
                link(V.tensor_tensor(nb[:, 2], nb[:, 1], nb[:, 0], ALU.subtract))
                link(V.tensor_scalar(nb[:, 2], nb[:, 2], float(P), None, ALU.mult))
                link(V.tensor_tensor(sc[:], g.ps[:, 1, 0:tiles * NE].rearrange("p (t n) -> p t n", n=NE),
                                     nb[:, 2:3, :].to_broadcast(wide), ALU.add))
                for j in range(TOP_K):
                    link(V.tensor_tensor(tmp[:], eq[:, j], sc[:], ALU.mult))
                    link(V.tensor_reduce(slotf[:, :, j], tmp[:], AX.X, ALU.add))
                V.tensor_copy(g.slots[:, 0:tiles * TOP_K], slotf[:].rearrange("p t j -> p (t j)")).then_inc(slots_ready, 1)
                hidden(2)
                link(V.tensor_tensor(cmp[:], nb[0:1, 1:2, :].to_broadcast([1, NBK, NE]),
                                     iota[0:1, 0:NBK].unsqueeze(2).to_broadcast([1, NBK, NE]), ALU.is_le))
                link(V.tensor_reduce(be[:, 0], cmp[:], AX.X, ALU.add))
                link(V.tensor_scalar(be[:, 0], be[:, 0], float(NE - 1), None, ALU.min))
                link(V.tensor_scalar(be[:, 1], be[:, 0], -1.0, 1.0 / RING, ALU.add, ALU.mult))
                link(V.tensor_scalar(be[:, 1], be[:, 1], MAGIC, None, ALU.add))
                link(V.tensor_scalar(be[:, 1], be[:, 1], -MAGIC, None, ALU.add))
                link(V.scalar_tensor_tensor(out=be[:, 2], in0=be[:, 1], scalar=-float(RING), in1=be[:, 0], op0=ALU.mult, op1=ALU.add))
                link(V.tensor_scalar(be[:, 0], be[:, 0], 1.0, None, ALU.add))
                V.tensor_copy(g.block_tab[:, 0, 0:NBK], be[:, 0])
                V.tensor_copy(g.block_tab[:, 1, 0:NBK], be[:, 2])
                link(V.memset(ring[:], 1.0))
                link(V.tensor_scalar(ring[:, RING:], nb[0:1, 1, 0:NE - RING], 1.0, None, ALU.add))
                link(V.tensor_copy(g.ring_tab[:], ring[:]))
                link(V.tensor_scalar(ring[:, 0:1], nb[0:1, 1, NE - 1:NE], 0.5, 0.25, ALU.mult, ALU.add))
                link(V.tensor_scalar(ring[:, 0:1], ring[:, 0:1], MAGIC, None, ALU.add))
                link(V.tensor_scalar(ring[:, 0:1], ring[:, 0:1], -MAGIC - 2.0, None, ALU.add))
                link(V.tensor_copy(g.middle_pairs[:], ring[:, 0:1]))
                for m in range(3, GROUPS):
                    hidden(m)
                dve.wait_ge(ids_loaded, 16)
                V.tensor_copy(idrf[:], idrow[:]).then_inc(idf_ready, 1)
                dve.wait_ge(ids_turned, 1)
                V.tensor_copy(g.ids[:, 0:NBK], g.ps[:, 3, 0:NBK])


def stage_experts(nc, g, l, tiles):
    NBK = blocks_of(tiles)
    with Stage(nc, f"moe{l}") as st:
        wgu = st.sb("wgu", [P, RING, KD, 2 * DE])
        wd = st.sb("wd", [P, RING, 2, D])
        xg = st.sb("xg", [P, 2, D])
        xT = st.sb("xT", [P, 2, KD, P])
        ix = st.sb("ix", [P, 2], U32)
        sg = st.sb("sg", [P, 2, DE])
        hid = st.sb("hid", [P, 2, DE])
        hT = st.sb("hidT", [P, 2, 2, P])
        y = st.sb("y", [P, 2, D])
        names = "landed picked waits_met turned xt_lo xt_hi gu_ready silu_ready hid_ready hid_turned hidt_ready down_ready y_lo y_hi".split()
        (landed, picked, waits_met, turned, xt_lo, xt_hi, gu_ready, silu_ready, hid_ready, hid_turned, hidt_ready, down_ready, y_lo, y_hi) = (
            st.sem(n) for n in names)
        w_loaded = [st.sem(f"w_loaded{i}") for i in range(RING)]
        x_landed = [st.sem(f"x_landed{i}") for i in range(2)]
        y_stored = [st.sem(f"y_stored{i}") for i in range(2)]

        def all_blocks(eng, body):
            end = eng.value_load(g.middle_pairs[0:1, 0:1], min_val=0, max_val=NBK // 2 - 2) + 1
            body(0, 0, 0)
            body(1, 1, 0)
            with eng.Fori(1, NBK // 2 - 1) as i:
                with eng.If(i < end):
                    body(i * 2, 0, i)
                    body(i * 2 + 1, 1, i)
                eng.end_ifs()
            body(end * 2, 0, end)
            body(end * 2 + 1, 1, end, last=True)
            return end

        def first(b):
            return isinstance(b, int) and b == 0

        with nc.Block() as block:
            @block.sync
            def _(sp):
                def load(e, r, turn):
                    free = sp.value_load(g.ring_tab[0:1, bass.ds(e, 1)], min_val=1, max_val=NBK + 1)
                    sp.wait_ge(down_ready, free)
                    one = bass.ds(e, 1)
                    sp.dma_start(wgu[:, r, :, 0:DE], g.moe_gate[l][one].rearrange("o (k p) n -> p (o k) n", p=P)).then_inc(w_loaded[r], 16)
                    sp.dma_start(wgu[:, r, :, DE:], g.moe_up[l][one].rearrange("o (k p) n -> p (o k) n", p=P)).then_inc(w_loaded[r], 16)
                    sp.dma_start(wd[:, r], g.moe_down[l][one].rearrange("o (k p) n -> p (o k) n", p=P)).then_inc(w_loaded[r], 16)

                def tell(r, turn):
                    sp.wait_ge(w_loaded[r], turn * 48 + 48)
                    sp.sem_inc(landed, 1)

                load(0, 0, 0)
                for e in range(1, RING):
                    load(e, e, 0)
                    tell(e - 1, 0)
                with sp.Fori(1, NE // RING) as i:
                    load(i * RING, 0, i)
                    tell(RING - 1, i - 1)
                    for r in range(1, RING):
                        load(i * RING + r, r, i)
                        tell(r - 1, i)
                for e in range(NE // RING * RING, NE):
                    load(e, e % RING, e // RING)
                    tell((e - 1) % RING, (e - 1) // RING)
                tell((NE - 1) % RING, (NE - 1) // RING)

            @block.gpsimd
            def _(pool):
                pool.sem_inc(down_ready, 1)

                def body(b, q, pair, last=False):
                    wait(pool, turned, b - 1)
                    nc.gpsimd.tensor_copy(ix[:, q:q + 1], g.ids[:, bass.ds(b, 1)]).then_inc(picked, 1)
                    pool.wait_ge(picked, b + 1)
                    pool.sem_inc(waits_met, 1)
                    pool.indirect_dma_start(xg[:, q], None, g.h_dram, bass.IndirectOffsetOnAxis(ix[:, q:q + 1], 0)).then_inc(x_landed[q], 16)

                all_blocks(pool, body)

            @block.tensor
            def _(pe):
                def turn(b, q, half):
                    pe.wait_ge(x_landed[q], half * 16 + 16)
                    wait(pe, xt_lo, b)
                    wait(pe, xt_hi, b)
                    for k in range(KD):
                        mm = nc.tensor.transpose(g.ps[:, k // 4, (k % 4) * P:(k % 4 + 1) * P], xg[:, q, k * P:(k + 1) * P], g.ident[:])
                    mm.then_inc(turned, 1)

                def down(b, q, place):
                    pe.wait_ge(hidt_ready, b + 1)
                    wait(pe, y_lo, b)
                    wait(pe, y_hi, b)
                    for half in range(2):
                        for f in range(2):
                            mm = nc.tensor.matmul(g.ps[:, 6 + half, :], hT[:, q, f, :],
                                                  wd[:, bass.ds(place, 1), f, half * BANK:(half + 1) * BANK].rearrange("p o n -> p (o n)"),
                                                  start=f == 0, stop=f == 1)
                    mm.then_inc(down_ready, 1)

                def place_of(b):
                    return pe.value_load(g.block_tab[0:1, 1, bass.ds(b, 1)], min_val=0, max_val=RING - 1)

                def expert_of(b):
                    return pe.value_load(g.block_tab[0:1, 0, bass.ds(b, 1)], min_val=1, max_val=NE)

                known = {}

                def body(b, q, pair, last=False):
                    expert, place = known["next"] if q else (expert_of(b), place_of(b))
                    pe.wait_ge(landed, expert)
                    pe.wait_ge(xt_lo, b + 1)
                    pe.wait_ge(xt_hi, b + 1)
                    wait(pe, hid_ready, b - 1)
                    for k in range(KD):
                        mm = nc.tensor.matmul(g.ps[:, 2 + q, :], xT[:, q, k, :],
                                              wgu[:, bass.ds(place, 1), k, :].rearrange("p o n -> p (o n)"),
                                              start=k == 0, stop=k == KD - 1)
                    mm.then_inc(gu_ready, 1)
                    if not first(b):
                        down(b - 1, 1 - q, known["own"] if q else place_of(b - 1))
                    if not last:
                        turn(b + 1, 1 - q, pair + q)
                    known["own"] = place
                    if not q:
                        known["next"] = expert_of(b + 1), place_of(b + 1)
                    pe.wait_ge(hid_ready, b + 1)
                    for f in range(2):
                        mm = nc.tensor.transpose(g.ps[:, 4, f * P:(f + 1) * P], hid[:, q, f * P:(f + 1) * P], g.ident[:])
                    mm.then_inc(hid_turned, 1)
                    if last:
                        down(b, q, place)

                turn(0, 0, 0)
                all_blocks(pe, body)

            @block.scalar
            def _(act):
                def put(b, q):
                    act.wait_ge(down_ready, b + 2)
                    nc.scalar.copy(y[:, q, BANK:], g.ps[:, 7, :]).then_inc(y_hi, 1)
                    act.wait_ge(y_hi, b + 1)
                    act.wait_ge(y_lo, b + 1)
                    row = g.y_dram[bass.ds(b, 1)].rearrange("o p n -> p (o n)")
                    act.dma_start(row, y[:, q]).then_inc(y_stored[q], 16)

                def take(b, q):
                    act.wait_ge(turned, b + 1)
                    nc.scalar.copy(xT[:, q, 4:8, :], g.ps[:, 1, :].rearrange("p (k n) -> p k n", n=P)).then_inc(xt_hi, 1)

                def body(b, q, pair, last=False):
                    act.wait_ge(gu_ready, b + 1)
                    nc.scalar.activation(sg[:, q], g.ps[:, 2 + q, 0:DE], ACT.Silu).then_inc(silu_ready, 1)
                    if not last:
                        take(b + 1, 1 - q)
                    if not first(b):
                        if not (isinstance(b, int) and b < 3):
                            act.wait_ge(y_stored[1 - q], (b - 1 - (1 - q)) * 8)
                        put(b - 1, 1 - q)

                take(0, 0)
                end = all_blocks(act, body)
                act.wait_ge(y_stored[1], end * 16)
                put(end * 2 + 1, 1)
                for q in range(2):
                    act.wait_ge(y_stored[q], end * 16 + 16)
                act.sem_inc(waits_met, 1)

            @block.vector
            def _(dve):
                def put(b, q):
                    dve.wait_ge(down_ready, b + 2)
                    if not (isinstance(b, int) and b < 2):
                        dve.wait_ge(y_stored[q], (b - q) * 8)
                    nc.vector.tensor_copy(y[:, q, 0:BANK], g.ps[:, 6, :]).then_inc(y_lo, 1)

                def take(b, q):
                    dve.wait_ge(turned, b + 1)
                    nc.vector.tensor_copy(xT[:, q, 0:4, :], g.ps[:, 0, :].rearrange("p (k n) -> p k n", n=P)).then_inc(xt_lo, 1)

                def body(b, q, pair, last=False):
                    dve.wait_ge(silu_ready, b + 1)
                    nc.vector.tensor_tensor(hid[:, q], sg[:, q], g.ps[:, 2 + q, DE:], ALU.mult).then_inc(hid_ready, 1)
                    if not first(b):
                        put(b - 1, 1 - q)
                    if not last:
                        take(b + 1, 1 - q)
                    dve.wait_ge(hid_turned, b + 1)
                    nc.vector.tensor_copy(hT[:, q], g.ps[:, 4, 0:2 * P].rearrange("p (f n) -> p f n", n=P)).then_inc(hidt_ready, 1)

                take(0, 0)
                end = all_blocks(dve, body)
                put(end * 2 + 1, 1)


def stage_moe_out(nc, g, l, tiles, final):
    with Stage(nc, f"res{l}") as st:
        gb = st.sb("gb", [P, 2, D])
        nf = st.sb("nf", [P, D])
        x = st.sb("x", [P, 3, D])
        tmp = st.sb("tmp", [P, 2, D])
        ye = st.sb("ye", [P, 6, D])
        ss = st.sb("ss", [P, tiles])
        mod = None if final else Modulation(nc, g, l + 1, st, g.hT[:].rearrange("p k n -> p (k n)")[:, 0:2 * KD * BANK].rearrange(
            "p (i k n) -> p i k n", i=2, k=KD))
        y_landed = [st.sem(f"y_landed{i}") for i in range(6)]
        added = st.sem("added")
        names = "gb_loaded gated summed squared mean_ready root_ready rstd_ready normed out_ready".split()
        gb_loaded, gated, summed, squared, mean_ready, root_ready, rstd_ready, normed, out_ready = (st.sem(n) for n in names)
        x_loaded = [st.sem(f"x_loaded{i}") for i in range(3)]
        x_stored = [st.sem(f"x_stored{i}") for i in range(3)]
        with nc.Block() as block:
            @block.sync
            def _(sp):
                for s in range(2):
                    sp.dma_start(gb[:, s], g.mod_rows[s:s + 1, 5 * D:6 * D].to_broadcast([P, D])).then_inc(gb_loaded, 16)
                sp.dma_start(nf[:], g.norm_f.rearrange("(o n) -> o n", o=1).to_broadcast([P, D])).then_inc(gb_loaded, 16)
                if mod:
                    mod.load_small(sp)
                for t in range(max(tiles, mod.CHUNKS) if mod else tiles):
                    if mod:
                        mod.load(sp, t)
                    if t < tiles:
                        wait(sp, x_stored[t % 3], 16 * (t // 3))
                        sp.dma_start(x[:, t % 3], g.x_dram[t * P:(t + 1) * P, :]).then_inc(x_loaded[t % 3], 16)
                if mod:
                    sp.wait_ge(gb_loaded, 48)
                    mod.store(sp)

            if mod:
                @block.tensor
                def _(pe):
                    mod.products(pe)

            @block.gpsimd
            def _(pool):
                rows = g.y_dram[0:blocks_of(tiles)].rearrange("b p n -> (b p) n")
                for n in range(tiles * TOP_K):
                    wait(pool, added, n - 5)
                    pool.indirect_dma_start(ye[:, n % 6], None, rows, bass.IndirectOffsetOnAxis(g.slots[:, n:n + 1], 0)).then_inc(y_landed[n % 6], 16)

            @block.vector
            def _(dve):
                def norm(t):
                    dve.wait_ge(squared, t + 1)
                    nc.vector.tensor_scalar(ss[:, t:t + 1], ss[:, t:t + 1], 1.0 / D, EPS, ALU.mult, ALU.add).then_inc(mean_ready, 1)
                    dve.wait_ge(root_ready, t + 1)
                    nc.vector.reciprocal(ss[:, t:t + 1], ss[:, t:t + 1]).then_inc(rstd_ready, 1)
                    dve.wait_ge(rstd_ready, t + 1)
                    nc.vector.scalar_tensor_tensor(out=x[:, t % 3], in0=x[:, t % 3], scalar=ss[:, t:t + 1], in1=nf[:],
                                                   op0=ALU.mult, op1=ALU.mult).then_inc(out_ready, 1)

                dve.wait_ge(gb_loaded, 48)
                for t in range(tiles):
                    if mod and t:
                        mod.add_bias(dve, t - 1)
                    for j in range(TOP_K):
                        n = t * TOP_K + j
                        dve.wait_ge(y_landed[n % 6], 16 * (n // 6 + 1))
                        nc.vector.scalar_tensor_tensor(out=g.acc[:, t, :], in0=ye[:, n % 6], scalar=g.slot_w[:, t, j:j + 1],
                                                       in1=g.acc[:, t, :], op0=ALU.mult, op1=ALU.add).then_inc(added, 1)
                        dve.wait_ge(added, n + 1)
                    if final:
                        wait(dve, squared, t - 1)
                    nc.vector.tensor_tensor(tmp[:, t % 2], g.acc[:, t, :], gb[:, t // NTL], ALU.mult).then_inc(gated, 1)
                    dve.wait_ge(gated, t + 1)
                    dve.wait_ge(x_loaded[t % 3], 16 * (t // 3 + 1))
                    nc.vector.tensor_tensor(x[:, t % 3], x[:, t % 3], tmp[:, t % 2], ALU.add).then_inc(summed, 1)
                    if final and t:
                        norm(t - 1)
                if final:
                    norm(tiles - 1)
                if mod:
                    for n in range(tiles - 1, mod.CHUNKS):
                        mod.add_bias(dve, n)
                    mod.scales(dve)

            @block.scalar
            def _(act):
                for t in range(tiles):
                    act.wait_ge(summed, t + 1)
                    if final:
                        nc.scalar.activation(tmp[:, t % 2], x[:, t % 3], ACT.Square, accum_out=ss[:, t:t + 1]).then_inc(squared, 1)
                        act.wait_ge(mean_ready, t + 1)
                        nc.scalar.activation(ss[:, t:t + 1], ss[:, t:t + 1], ACT.Sqrt).then_inc(root_ready, 1)
                        act.wait_ge(out_ready, t + 1)
                        dst = g.out[0, t * P:(t + 1) * P, :]
                    else:
                        dst = g.x_dram[t * P:(t + 1) * P, :]
                    act.dma_start(dst, x[:, t % 3]).then_inc(x_stored[t % 3], 16)
                for i in range(3):
                    act.wait_ge(x_stored[i], 16 * len(range(i, tiles, 3)))


def shape_tables():
    t = {}
    f32 = np.float32
    t["t_ident"] = np.eye(P, dtype=f32)

    t["t_iota"] = np.arange(MAX_BLOCKS, dtype=f32)[None, :]
    a = np.arange(P)
    t["t_before"] = np.stack([a[:, None] < a[None, :], np.ones((P, P))], axis=1).astype(f32)
    t["t_tok"] = np.ascontiguousarray(np.arange(TOK, dtype=np.uint32).reshape(NT, P).T)
    for name, L in (("", SEQ), ("_c", CTX)):
        n = np.arange(L, dtype=f32)
        t_norm = n / f32(L - 1)
        bands = np.linspace(1e-4, HY_BANDS - 1, HY_BANDS, dtype=f32)
        ang = (f32(2.0 * math.pi / L) * n[:, None] * bands[None, :]).astype(f32)
        z = np.concatenate([t_norm[:, None], np.cos(ang), -np.sin(ang)], axis=-1).astype(f32)
        t["t_hy_z" + name] = np.ascontiguousarray(z.T)
        lo, hi = -math.log(1e-2) / 1.5, -math.log(1e-2) / 0.3
        decay = np.linspace(lo, hi, HY_CH, dtype=f32)
        d = np.exp(-t_norm[:, None] * decay[None, :]).astype(f32)
        db = d.copy()
        db[0] = 0
        t["t_hy_dec" + name] = np.concatenate([d, db], axis=1)
        j = np.arange(L)[:, None].astype(np.float64)
        k = np.arange(L)[None, :].astype(np.float64)

        def blocks(a):
            return a.reshape(L // P, P, L // P, P).transpose(2, 1, 0, 3)

        a = math.pi / (2 * L) * (2 * k + 1)
        t["t_dft" + name] = np.ascontiguousarray(np.stack([blocks(np.cos(a * j)), blocks(np.sin(a * j))]).astype(f32))
        C2 = np.stack([np.cos(a * (j + 0.5)), np.sin(a * (j + 0.5))]).astype(f32)
        t["t_dft2" + name] = np.ascontiguousarray(np.stack([blocks(C2[0]), blocks(C2[1])]))
        t["t_dft2r" + name] = C2
    quarter = HD // 4
    inv = (f32(10000.0) ** (-np.arange(quarter, dtype=f32) / f32(quarter))).astype(f32)
    pos = np.arange(SEQ)
    row, col = (pos // GRID_W).astype(f32), (pos % GRID_W).astype(f32)
    ang = np.concatenate([np.tile(row[:, None] * inv, 2), np.tile(col[:, None] * inv, 2)], axis=1).astype(f32)
    t["t_rope"] = np.ascontiguousarray(np.stack([np.tile(np.cos(ang), 2).T, np.tile(np.sin(ang), 2).T]).astype(f32))
    rot = np.zeros((P, P), f32)
    for base in range(0, P, 2 * quarter):
        for d in range(quarter):
            rot[base + quarter + d, base + d] = -1.0
            rot[base + d, base + quarter + d] = 1.0
    t["t_rot"] = rot
    q = np.arange(P)[:, None]
    k = np.arange(P)[None, :]
    m = np.zeros((P, CTX + 3 * P), f32)
    m[:, CTX:CTX + P] = np.where(k >= q, 0, NEG)
    m[:, CTX + 2 * P:] = np.where(k <= q, 0, NEG)
    t["t_wa_mask"] = m
    sel = np.zeros((32, GRID_W, 2, GRID_W), f32)
    cq = np.arange(GRID_W)
    start = np.clip(cq - NA_KC // 2, 0, GRID_W - NA_KC)
    for ck in range(GRID_W):
        for c in range(GRID_W):
            if start[c] <= ck < start[c] + NA_KC:
                sel[ck - c + NA_KC - 1, ck, :, c] = 1
            else:
                sel[31, ck, :, c] = 1
    t["t_na_sel"] = sel.reshape(32, GRID_W * P)
    return t


def gdn_tables():
    C = 64
    t = {}
    i = np.arange(C)[:, None]
    j = np.arange(C)[None, :]
    two = lambda a: np.tile(a, (2,) + (1,) * (a.ndim - 1)).astype(np.float32)
    dirs = lambda f, b: np.stack([f, b], axis=1)
    t["t_gd_tri"] = two(dirs(i <= j, i >= j))
    t["t_gd_allow"] = two(np.where(dirs(i >= j, i <= j), 1e30, NEG))
    t["t_gd_strict"] = two(dirs(i > j, i < j))
    t["t_gd_eye"] = two(np.eye(C))
    lv = []
    for s in (1, 2, 4, 8, 16, 32):
        m = (i // (2 * s) == j // (2 * s)) & (i // s % 2 == 1) & (j // s % 2 == 0)
        lv.append(dirs(m, m.T))
    lv.insert(1, lv[0][:, ::-1])
    t["t_gd_lvl"] = two(np.stack(lv, axis=1))
    blk = np.kron(np.eye(2), np.ones((C, C)))
    t["t_gd_negblk"] = -blk.astype(np.float32)
    a = np.arange(P)
    same = blk.astype(bool)
    t["t_gd_cum"] = np.stack([same & (a[:, None] <= a[None, :]), same & (a[:, None] >= a[None, :]), same], axis=1).astype(np.float32)
    return {k: np.ascontiguousarray(v) for k, v in t.items()}


NAMES = ["x", "c", "ctx", "c_ctx", "w_ada", "b_ada", "norm1", "norm2", "norm_f", "w_in", "w_out",
         "hy_conv", "hy_w1", "hy_b1", "hy_w2", "hy_b2", "hy_w3", "hy_freq", "hy_bias",
         "wa_sink", "na_rpb", "gdn_conv", "gdn_a_log", "gdn_dt_bias", "gdn_norm",
         "moe_router", "moe_bias", "moe_gate", "moe_up", "moe_down", "sh_gate", "sh_up", "sh_down"]


class Globals:

    def __init__(self, arrays):
        self.tables = arrays
        (self.x, self.c, self.ctx, self.c_ctx, self.w_ada, self.b_ada, self.norm1, self.norm2, self.norm_f, self.w_in,
         self.w_out, self.hy_conv, self.hy_w1, self.hy_b1, self.hy_w2, self.hy_b2, self.hy_w3, self.hy_freq, self.hy_bias,
         self.wa_sink, self.na_rpb, self.gdn_conv, self.gdn_a_log, self.gdn_dt_bias, self.gdn_norm,
         self.moe_router, self.moe_bias, self.moe_gate, self.moe_up, self.moe_down,
         self.sh_gate, self.sh_up, self.sh_down) = (arrays[n] for n in NAMES)
        self.t_ident, self.t_iota, self.t_before, self.t_tok, self.t_rope, self.t_rot, self.t_wa_mask, self.t_na_sel = (
            arrays[n] for n in ("t_ident", "t_iota", "t_before", "t_tok", "t_rope", "t_rot", "t_wa_mask", "t_na_sel"))


def hybrid_backbone(nc, arrays, out):
    g = Globals(arrays)
    g.out = out
    g.hy_tables = [(arrays["t_hy_z" + s], arrays["t_hy_dec" + s], arrays["t_dft" + s], arrays["t_dft2" + s]) for s in ("", "_c")]
    g.hy_rows = [arrays["t_dft2r"], arrays["t_dft2r_c"]]
    g.gdn_masks = {n: list(arrays["t_" + n].shape[1:]) for n in ("gd_tri", "gd_allow", "gd_strict", "gd_eye", "gd_lvl", "gd_negblk")}
    g.x_dram = nc.dram_tensor("x_dram", [TOK, D], F32, kind="Internal").ap()
    g.h_dram = nc.dram_tensor("h_dram", [TOK, D], F32, kind="Internal").ap()
    g.y_dram = nc.dram_tensor("y_dram", [MAX_BLOCKS, P, D], F32, kind="Internal").ap()
    g.ids_dram = nc.dram_tensor("ids_dram", [MAX_BLOCKS * P, 1], U32, kind="Internal").ap()
    g.mod_rows = nc.dram_tensor("mod_rows", [2, 6 * D], F32, kind="Internal").ap()
    with ExitStack() as ctx:
        def sb(name, shape):
            return ctx.enter_context(nc.sbuf_tensor(name, shape, F32))
        g.ps = ctx.enter_context(nc.psum_tensor("ps", [P, 8, BANK], F32))
        g.ident = sb("ident", [P, P])
        g.siluT = sb("siluT", [P, KD, 2])
        g.modT = sb("modT", [P, 6 * KD, 2])
        g.gain = sb("gain", [P, 2, KD, 2])
        g.slot_w = sb("slot_w", [P, NT, TOP_K])
        g.slots = ctx.enter_context(nc.sbuf_tensor("slots", [P, NT * TOP_K], U32))
        g.ids = ctx.enter_context(nc.sbuf_tensor("ids", [P, MAX_BLOCKS], U32))
        g.block_tab = ctx.enter_context(nc.sbuf_tensor("block_tab", [1, 2, MAX_BLOCKS], U32))
        g.middle_pairs = ctx.enter_context(nc.sbuf_tensor("middle_pairs", [1, 1], U32))
        g.ring_tab = ctx.enter_context(nc.sbuf_tensor("ring_tab", [1, NE], U32))
        g.hT = sb("hT", [P, KD, TOK])
        mixed = sb("mixed", [P, NT * D])
        g.yT = mixed[:].rearrange("p (k n) -> p k n", k=KD)
        g.acc = mixed[:].rearrange("p (t n) -> p t n", t=NT)
        stage_setup(nc, g)
        for l in range(DEPTH):
            last = l == DEPTH - 1
            tiles = NTL if last else NT
            latent, context = (g.x[0], g.ctx[0]) if l == 0 else (g.x_dram[0:SEQ, :], g.x_dram[SEQ:TOK, :])
            if l == 0:
                stage_modulation(nc, g, l)
            stage_norm(nc, g, l, latent, context)
            stage_hyena(nc, g, l, False)
            if not last:
                stage_hyena(nc, g, l, True)
            stage_window(nc, g, l, not last)
            stage_neighbour(nc, g, l, not last)
            stage_gdn(nc, g, l)
            stage_mix_out(nc, g, l, tiles, latent, context)
            stage_route(nc, g, l, tiles)
            stage_experts(nc, g, l, tiles)
            stage_moe_out(nc, g, l, tiles, last)


def kernel(**inputs):
    import concourse.bacc as bacc
    from concourse.bass_utils import run_bass_kernel_spmd

    nc = bacc.Bacc("TRN2", target_bir_lowering=False, num_devices=1)
    tables = shape_tables()
    tables.update(gdn_tables())
    feeds, args = {}, {}
    for name in NAMES:
        feeds["in_" + name] = np.ascontiguousarray(inputs[name])
    for name, a in tables.items():
        feeds["in_" + name] = a
    for name, a in feeds.items():
        args[name[3:]] = nc.dram_tensor(name, a.shape, mybir.dt.from_np(a.dtype), kind="ExternalInput").ap()
    out = nc.dram_tensor("out", (1, SEQ, D), F32, kind="ExternalOutput").ap()
    hybrid_backbone(nc, args, out)
    nc.compile()
    r = run_bass_kernel_spmd(nc, [feeds], core_ids=[0])
    return r.results[0]["out"]
```
